# Optimizing a Trainium2 kernel written in Bass

```python
import math
import jax
import jax.numpy as jnp
from jax import lax
import numpy as np

D_MODEL = 1024
BATCH = 1
SEQ = 512
DEPTH = 2

N_MIXERS = 3
HEAD_DIM = 64
DIFF_HEADS = D_MODEL // (2 * HEAD_DIM)
ATTN_QBLOCK = 128
DIL_HEADS = D_MODEL // HEAD_DIM
DIL_PATTERNS = ((128, 1), (512, 4), (2048, 16))
DIL_QBLOCK = 64
RWKV_HEADS = D_MODEL // HEAD_DIM
DECAY_LORA = 64
AAA_LORA = 64
GATE_LORA = 128
MEM_LEN = 256
XATT_HEADS = 4
D_FF = 2816
CONV_WIDTH = 3
ALPHA = (2 * DEPTH) ** 0.25
BETA = (8 * DEPTH) ** -0.25
LN_EPS = 1e-5
GN_EPS = 64e-5
NEG_INF = -1e30
N_A = len(range(0, DEPTH, N_MIXERS))
N_B = len(range(1, DEPTH, N_MIXERS))
N_C = len(range(2, DEPTH, N_MIXERS))


def layer_norm(x, g, b):
    xf = x.astype(jnp.float32)
    mu = jnp.mean(xf, -1, keepdims=True)
    var = jnp.mean(jnp.square(xf - mu), -1, keepdims=True)
    return ((xf - mu) * lax.rsqrt(var + LN_EPS) * g + b).astype(x.dtype)

def rms_norm(x, g):
    xf = x.astype(jnp.float32)
    return (xf * lax.rsqrt(jnp.mean(jnp.square(xf), -1, keepdims=True) + LN_EPS) * g).astype(x.dtype)

def alibi_slopes(n):
    return jnp.exp2(-8.0 * jnp.arange(1, n + 1, dtype=jnp.float32) / n)

def diff_attention(x, w_qkv, lam, subln, w_o, lambda_init):
    B, S, D = x.shape
    H, E = DIFF_HEADS, HEAD_DIM
    q, k, v = jnp.split(x @ w_qkv, 3, axis=-1)
    q = q.reshape(B, S, H, 2, E)
    k = k.reshape(B, S, H, 2, E)
    v = v.reshape(B, S, H, 2 * E)
    lamf = lam.astype(jnp.float32)
    lam_full = jnp.exp(jnp.sum(lamf[0] * lamf[1])) - jnp.exp(jnp.sum(lamf[2] * lamf[3])) + lambda_init
    slopes = alibi_slopes(H)
    pos = jnp.arange(S)
    nblk = S // ATTN_QBLOCK
    qb = q.reshape(B, nblk, ATTN_QBLOCK, H, 2, E).transpose(1, 0, 2, 3, 4, 5)
    starts = jnp.arange(nblk) * ATTN_QBLOCK

    def block(args):
        q_blk, start = args
        s = jnp.einsum('bqhce,bkhce->bhcqk', q_blk, k,
                       preferred_element_type=jnp.float32) * (E ** -0.5)
        dist = jnp.abs((start + jnp.arange(ATTN_QBLOCK))[:, None] - pos[None, :]).astype(jnp.float32)
        s = s - slopes[None, :, None, None, None] * dist[None, None, None]
        p = jax.nn.softmax(s, axis=-1)
        attn = p[:, :, 0] - lam_full * p[:, :, 1]
        return jnp.einsum('bhqk,bkhe->bqhe', attn.astype(v.dtype), v)

    o = lax.map(block, (qb, starts))
    o = o.transpose(1, 0, 2, 3, 4).reshape(B, S, H, 2 * E)
    o = rms_norm(o, subln) * (1.0 - lambda_init)
    return o.reshape(B, S, D) @ w_o

def dilated_group(q, k, v, window, dilation, slopes):
    B, S, H, E = q.shape
    half = window // (2 * dilation)
    L = S // dilation
    nblk = -(-L // DIL_QBLOCK)
    Lp = nblk * DIL_QBLOCK
    KB = DIL_QBLOCK + 2 * half

    def to_res(a):
        return a.reshape(B, L, dilation, H, E).transpose(0, 2, 1, 3, 4)

    qr = jnp.pad(to_res(q), ((0, 0), (0, 0), (0, Lp - L), (0, 0), (0, 0)))
    pad_k = ((0, 0), (0, 0), (half, Lp - L + half), (0, 0), (0, 0))
    kr = jnp.pad(to_res(k), pad_k)
    vr = jnp.pad(to_res(v), pad_k)
    starts = jnp.arange(nblk) * DIL_QBLOCK
    idx = starts[:, None] + jnp.arange(KB)[None, :]
    kb = kr[:, :, idx]
    vb = vr[:, :, idx]
    qb = qr.reshape(B, dilation, nblk, DIL_QBLOCK, H, E)
    s = jnp.einsum('brnqhe,brnkhe->brnhqk', qb, kb,
                   preferred_element_type=jnp.float32) * (E ** -0.5)
    u_q = starts[:, None] + jnp.arange(DIL_QBLOCK)[None, :]
    u_k = idx - half
    rel = u_k[:, None, :] - u_q[:, :, None]
    valid = (jnp.abs(rel) <= half) & (u_k[:, None, :] >= 0) & (u_k[:, None, :] < L)
    dist = (dilation * jnp.abs(rel)).astype(jnp.float32)
    bias = -slopes[None, :, None, None] * dist[:, None]
    s = jnp.where(valid[:, None], s + bias, NEG_INF)
    lse = jax.nn.logsumexp(s, axis=-1)
    p = jnp.exp(s - lse[..., None])
    o = jnp.einsum('brnhqk,brnkhe->brnqhe', p.astype(v.dtype), vb)
    o = o.reshape(B, dilation, Lp, H, E)[:, :, :L].transpose(0, 2, 1, 3, 4).reshape(B, S, H, E)
    lse = lse.transpose(0, 1, 2, 4, 3).reshape(B, dilation, Lp, H)[:, :, :L]
    lse = lse.transpose(0, 2, 1, 3).reshape(B, S, H)
    return o, lse

def dilated_attention(x, w_qkv, w_o):
    B, S, D = x.shape
    H, E, G = DIL_HEADS, HEAD_DIM, len(DIL_PATTERNS)
    qkv = (x @ w_qkv).reshape(B, S, G, 3, H, E)
    slopes = alibi_slopes(H)
    outs, lses = [], []
    for g, (window, dilation) in enumerate(DIL_PATTERNS):
        o, l = dilated_group(qkv[:, :, g, 0], qkv[:, :, g, 1], qkv[:, :, g, 2], window, dilation, slopes)
        outs.append(o)
        lses.append(l)
    wts = jax.nn.softmax(jnp.stack(lses), axis=0)
    o = jnp.sum(wts[..., None] * jnp.stack(outs).astype(jnp.float32), axis=0)
    return o.astype(x.dtype).reshape(B, S, D) @ w_o

def token_shift(x, reverse):
    if reverse:
        return jnp.pad(x[:, 1:], ((0, 0), (0, 1), (0, 0)))
    return jnp.pad(x[:, :-1], ((0, 0), (1, 0), (0, 0)))

def wkv7_scan(r, w, k, v, kk, a, reverse):
    B, S, H, N = r.shape
    seq = tuple(t.transpose(1, 0, 2, 3) for t in (r, w, k, v, kk, a))

    def step(state, inp):
        r_t, w_t, k_t, v_t, kk_t, a_t = inp
        sa = jnp.einsum('bhij,bhj->bhi', state, -kk_t)
        state = (state * w_t[:, :, None, :] + sa[..., None] * (kk_t * a_t)[:, :, None, :]
                 + v_t[..., None] * k_t[:, :, None, :])
        return state, jnp.einsum('bhij,bhj->bhi', state, r_t)

    _, y = lax.scan(step, jnp.zeros((B, H, N, N), jnp.float32), seq, reverse=reverse)
    return y.transpose(1, 0, 2, 3)

def head_group_norm(y, g, b):
    H, N = y.shape[-2], y.shape[-1]
    mu = jnp.mean(y, -1, keepdims=True)
    var = jnp.mean(jnp.square(y - mu), -1, keepdims=True)
    return (y - mu) * lax.rsqrt(var + GN_EPS) * g.reshape(H, N) + b.reshape(H, N)

def rwkv7_direction(x, mu, w_r, w_k, w_v, w0, w1, w2, a0, a1, a2, g1, g2, k_k, k_a, r_k,
                    gn_g, gn_b, reverse):
    B, S, D = x.shape
    H, N = RWKV_HEADS, HEAD_DIM
    xx = token_shift(x, reverse) - x
    xr, xw, xk, xv, xa, xg = (x + xx * mu[j] for j in range(6))
    r = xr @ w_r
    k = xk @ w_k
    v = xv @ w_v
    w_log = -jax.nn.softplus(-(w0 + jnp.tanh(xw @ w1) @ w2).astype(jnp.float32)) - 0.5
    w = jnp.exp(-jnp.exp(w_log))
    a = jax.nn.sigmoid((a0 + (xa @ a1) @ a2).astype(jnp.float32))
    g = jax.nn.sigmoid(xg @ g1) @ g2

    def heads(t):
        return t.astype(jnp.float32).reshape(B, S, H, N)

    r, k, v, w, a = heads(r), heads(k), heads(v), heads(w), heads(a)
    kk = k * k_k.astype(jnp.float32).reshape(H, N)
    kk = kk / jnp.maximum(jnp.linalg.norm(kk, axis=-1, keepdims=True), 1e-12)
    k = k * (1.0 + (a - 1.0) * k_a.astype(jnp.float32).reshape(H, N))
    y = wkv7_scan(r, w, k, v, kk, a, reverse)
    y = head_group_norm(y, gn_g, gn_b) + jnp.sum(r * k * r_k.astype(jnp.float32), -1, keepdims=True) * v
    return (y.reshape(B, S, D) * g).astype(x.dtype)

def rwkv7_time_mix(x, mu, w_rkv, w0, w1, w2, a0, a1, a2, g1, g2, k_k, k_a, r_k, gn_g, gn_b, w_o):
    fwd = rwkv7_direction(x, mu[0], w_rkv[0], w_rkv[1], w_rkv[2], w0[0], w1[0], w2[0], a0[0], a1[0], a2[0],
                          g1[0], g2[0], k_k[0], k_a[0], r_k, gn_g, gn_b, False)
    bwd = rwkv7_direction(x, mu[1], w_rkv[0], w_rkv[1], w_rkv[2], w0[1], w1[1], w2[1], a0[1], a1[1], a2[1],
                          g1[1], g2[1], k_k[1], k_a[1], r_k, gn_g, gn_b, True)
    return (fwd + bwd) @ w_o

def memory_cross_attention(x, mem, w_q, w_kv, w_o):
    B, S, D = x.shape
    M = mem.shape[1]
    H = XATT_HEADS
    E = D // H
    q = (x @ w_q).reshape(B, S, H, E)
    kv = (mem @ w_kv).reshape(B, M, 2, H, E)
    s = jnp.einsum('bshe,bmhe->bhsm', q, kv[:, :, 0], preferred_element_type=jnp.float32) * (E ** -0.5)
    p = jax.nn.softmax(s, axis=-1).astype(x.dtype)
    o = jnp.einsum('bhsm,bmhe->bshe', p, kv[:, :, 1])
    return o.reshape(B, S, D) @ w_o

def conv_glu(x, w_in, conv_w, conv_b, w_out):
    gate, val = jnp.split(x @ w_in, 2, axis=-1)
    gate = lax.conv_general_dilated(gate, conv_w[:, None, :], window_strides=(1,),
                                    padding=((CONV_WIDTH // 2, CONV_WIDTH // 2),),
                                    dimension_numbers=('NWC', 'WIO', 'NWC'),
                                    feature_group_count=gate.shape[-1]) + conv_b
    return (jax.nn.gelu(gate, approximate=False) * val) @ w_out

def first_inputs(seed: int = 0) -> dict:
    key = jax.random.key(seed)
    keys = iter(jax.random.split(key, 48))
    D, F, H, N = D_MODEL, D_FF, RWKV_HEADS, HEAD_DIM
    G = len(DIL_PATTERNS)
    inv = D ** -0.5

    def normal(shape, scale):
        return jax.random.normal(next(keys), shape, jnp.float32) * scale

    def uniform(shape, lo, hi):
        return jax.random.uniform(next(keys), shape, jnp.float32, lo, hi)

    return {
        "x": normal((BATCH, SEQ, D), 1.0),
        "mem": normal((BATCH, MEM_LEN, D), 1.0),
        "diff_w_qkv": normal((N_A, D, 3 * D), inv),
        "diff_lambda": normal((N_A, 4, HEAD_DIM), 0.1),
        "diff_subln": 1.0 + normal((N_A, 2 * HEAD_DIM), 0.02),
        "diff_w_o": normal((N_A, D, D), inv * BETA),
        "dil_w_qkv": normal((N_B, D, G * 3 * D), inv),
        "dil_w_o": normal((N_B, D, D), inv * BETA),
        "rwkv_mu": uniform((N_C, 2, 6, D), 0.0, 1.0),
        "rwkv_w_rkv": normal((N_C, 3, D, D), inv),
        "rwkv_w0": uniform((N_C, 2, D), -5.0, 0.0),
        "rwkv_w1": normal((N_C, 2, D, DECAY_LORA), inv),
        "rwkv_w2": normal((N_C, 2, DECAY_LORA, D), 0.1 * DECAY_LORA ** -0.5),
        "rwkv_a0": normal((N_C, 2, D), 0.1),
        "rwkv_a1": normal((N_C, 2, D, AAA_LORA), inv),
        "rwkv_a2": normal((N_C, 2, AAA_LORA, D), 0.1 * AAA_LORA ** -0.5),
        "rwkv_g1": normal((N_C, 2, D, GATE_LORA), inv),
        "rwkv_g2": normal((N_C, 2, GATE_LORA, D), GATE_LORA ** -0.5),
        "rwkv_k_k": 0.85 + normal((N_C, 2, D), 0.02),
        "rwkv_k_a": 1.0 + normal((N_C, 2, D), 0.02),
        "rwkv_r_k": normal((N_C, H, N), 0.1),
        "rwkv_gn_g": 1.0 + normal((N_C, D), 0.02),
        "rwkv_gn_b": normal((N_C, D), 0.02),
        "rwkv_w_o": normal((N_C, D, D), inv * BETA),
        "xatt_w_q": normal((DEPTH, D, D), inv),
        "xatt_w_kv": normal((DEPTH, D, 2 * D), inv),
        "xatt_w_o": normal((DEPTH, D, D), inv * BETA),
        "ffn_w_in": normal((DEPTH, D, 2 * F), inv),
        "ffn_conv_w": normal((DEPTH, CONV_WIDTH, F), CONV_WIDTH ** -0.5),
        "ffn_conv_b": normal((DEPTH, F), 0.02),
        "ffn_w_out": normal((DEPTH, F, D), F ** -0.5 * BETA),
        "ln_g": 1.0 + normal((DEPTH, 3, D), 0.02),
        "ln_b": normal((DEPTH, 3, D), 0.02),
    }

def first_block(x, mem, diff_w_qkv, diff_lambda, diff_subln, diff_w_o, dil_w_qkv, dil_w_o,
              rwkv_mu, rwkv_w_rkv, rwkv_w0, rwkv_w1, rwkv_w2, rwkv_a0, rwkv_a1, rwkv_a2,
              rwkv_g1, rwkv_g2, rwkv_k_k, rwkv_k_a, rwkv_r_k, rwkv_gn_g, rwkv_gn_b, rwkv_w_o,
              xatt_w_q, xatt_w_kv, xatt_w_o, ffn_w_in, ffn_conv_w, ffn_conv_b, ffn_w_out,
              ln_g, ln_b):
    for i in range(DEPTH):
        m, j = i % N_MIXERS, i // N_MIXERS
        if m == 0:
            lambda_init = 0.8 - 0.6 * math.exp(-0.3 * i)
            h = diff_attention(x, diff_w_qkv[j], diff_lambda[j], diff_subln[j], diff_w_o[j], lambda_init)
        elif m == 1:
            h = dilated_attention(x, dil_w_qkv[j], dil_w_o[j])
        else:
            h = rwkv7_time_mix(x, rwkv_mu[j], rwkv_w_rkv[j], rwkv_w0[j], rwkv_w1[j], rwkv_w2[j],
                               rwkv_a0[j], rwkv_a1[j], rwkv_a2[j], rwkv_g1[j], rwkv_g2[j],
                               rwkv_k_k[j], rwkv_k_a[j], rwkv_r_k[j], rwkv_gn_g[j], rwkv_gn_b[j],
                               rwkv_w_o[j])
        x = layer_norm(ALPHA * x + h, ln_g[i, 0], ln_b[i, 0])
        x = layer_norm(ALPHA * x + memory_cross_attention(x, mem, xatt_w_q[i], xatt_w_kv[i], xatt_w_o[i]),
                       ln_g[i, 1], ln_b[i, 1])
        x = layer_norm(ALPHA * x + conv_glu(x, ffn_w_in[i], ffn_conv_w[i], ffn_conv_b[i], ffn_w_out[i]),
                       ln_g[i, 2], ln_b[i, 2])
    return x


DEPTH_2 = 1

CHUNK = 64
GLA_HEADS = 4
GLA_DK = 64
GLA_DV = 128
GLA_GATE_RANK = 16
GLA_TAU = 16.0
ATT_HEADS = 8
ATT_DH = 64
IDX_HEADS = 8
IDX_DH = 32
TOPK_MAX = 256
Q_BLOCK = CHUNK
REL_BUCKETS = 32
REL_MAX_DIST = 128
N_GROUPS = 4
EXPERTS_PER_GROUP = 8
N_EXPERTS = N_GROUPS * EXPERTS_PER_GROUP
EXPERT_TOPK = 2
D_EXPERT = 128
EPS = 1e-6

GLA_QK_W = GLA_HEADS * GLA_DK
GLA_V_W = GLA_HEADS * GLA_DV
ATT_W = ATT_HEADS * ATT_DH
IDX_Q_W = IDX_HEADS * IDX_DH
SPLITS = (GLA_QK_W, GLA_QK_W, GLA_V_W, GLA_V_W, GLA_GATE_RANK, ATT_W, ATT_W, ATT_W, IDX_Q_W, IDX_DH, IDX_HEADS, D_MODEL, D_MODEL)
D_IN = 2 * GLA_QK_W + 2 * GLA_V_W + GLA_GATE_RANK + 3 * ATT_W + IDX_Q_W + IDX_DH + IDX_HEADS + 2 * D_MODEL


def rms_norm_2(x, g):
    xf = x.astype(jnp.float32)
    y = xf * lax.rsqrt(jnp.mean(xf * xf, axis=-1, keepdims=True) + EPS)
    return (y * g.astype(jnp.float32)).astype(x.dtype)

def gla_mixer(q, k, v, r, a_lr, w_alpha2, b_alpha, g_out):
    b, t, _ = q.shape
    nc = t // CHUNK
    f32 = jnp.float32
    q = q.reshape(b, nc, CHUNK, GLA_HEADS, GLA_DK).astype(f32) * (GLA_DK ** -0.5)
    k = k.reshape(b, nc, CHUNK, GLA_HEADS, GLA_DK)
    v = v.reshape(b, nc, CHUNK, GLA_HEADS, GLA_DV)
    log_a = jax.nn.log_sigmoid((a_lr @ w_alpha2 + b_alpha).astype(f32)) / GLA_TAU
    log_a = log_a.reshape(b, nc, CHUNK, GLA_HEADS, GLA_DK)
    cum = jnp.cumsum(log_a, axis=2)
    total = cum[:, :, -1]
    k_dec = (k.astype(f32) * jnp.exp(total[:, :, None] - cum)).astype(k.dtype)
    u = jnp.einsum('bnchd,bnche->nbhde', k_dec, v).astype(f32)

    def step(s, inp):
        dec, u_c = inp
        s = s * dec[..., None] + u_c
        return s, s

    s0 = jnp.zeros((b, GLA_HEADS, GLA_DK, GLA_DV), f32)
    _, states = lax.scan(step, s0, (jnp.exp(total).transpose(1, 0, 2, 3), u))
    o = jnp.einsum('bnchd,nbhde->bnche', q, states)
    o = rms_norm_2(o, g_out)
    o = o.reshape(b, t, GLA_V_W) * jax.nn.silu(r.astype(f32))
    return o.astype(r.dtype)

def t5_bucket(rel):
    half = REL_BUCKETS // 2
    exact = half // 2
    n = jnp.abs(rel)
    nf = jnp.maximum(n, 1).astype(jnp.float32)
    large = exact + (jnp.log(nf / exact) / math.log(REL_MAX_DIST / exact) * (half - exact)).astype(jnp.int32)
    large = jnp.minimum(large, half - 1)
    return jnp.where(rel > 0, half, 0) + jnp.where(n < exact, n, large)

def dsa_mixer(q, k, v, q_idx, k_idx, w_idx, rel_bias):
    b, t = q.shape[:2]
    k_top = min(TOPK_MAX, t // 4)
    nb = t // Q_BLOCK
    key_pos = jnp.arange(t)
    k_idx_f = k_idx.astype(jnp.float32)

    def to_blocks(a):
        return a.reshape(b, nb, Q_BLOCK, *a.shape[2:]).swapaxes(0, 1)

    def block(args):
        qb, qib, wb, i = args
        s = jnp.einsum('bqhd,bsd->bqhs', qib.astype(jnp.float32), k_idx_f)
        score = jnp.einsum('bqhs,bqh->bqs', jax.nn.relu(s), wb.astype(jnp.float32))
        admissible = key_pos < (i + 1) * Q_BLOCK
        score = jnp.where(admissible[None, None, :], score, -jnp.inf)
        top_val, top_idx = lax.top_k(score, k_top)
        valid = jnp.isfinite(top_val)
        k_sel = jax.vmap(lambda kk, ii: kk[ii])(k, top_idx)
        v_sel = jax.vmap(lambda vv, ii: vv[ii])(v, top_idx)
        logits = jnp.einsum('bqhd,bqkhd->bqhk', qb, k_sel).astype(jnp.float32) * (ATT_DH ** -0.5)
        q_pos = i * Q_BLOCK + jnp.arange(Q_BLOCK)
        bias = rel_bias[t5_bucket(top_idx - q_pos[None, :, None])]
        logits = logits + bias.astype(jnp.float32).transpose(0, 1, 3, 2)
        logits = jnp.where(valid[:, :, None, :], logits, -jnp.inf)
        p = jax.nn.softmax(logits, axis=-1)
        return jnp.einsum('bqhk,bqkhd->bqhd', p.astype(v.dtype), v_sel)

    out = lax.map(block, (to_blocks(q), to_blocks(q_idx), to_blocks(w_idx), jnp.arange(nb)))
    return out.swapaxes(0, 1).reshape(b, t, ATT_W)

def hier_moe(h, w_rg, b_rg, w_re, b_re, w_gate, w_up, w_down):
    b, t, d = h.shape
    f32 = jnp.float32
    xf = h.reshape(b * t, d)
    g_logits = (xf @ w_rg + b_rg).astype(f32)
    g_sel = jnp.argmax(g_logits, axis=-1)
    g_w = jnp.take_along_axis(jax.nn.softmax(g_logits, axis=-1), g_sel[:, None], axis=-1)
    e_logits = (xf @ w_re + b_re).astype(f32).reshape(-1, N_GROUPS, EXPERTS_PER_GROUP)
    e_in_group = jnp.take_along_axis(e_logits, g_sel[:, None, None], axis=1)[:, 0]
    top_v, top_i = lax.top_k(e_in_group, EXPERT_TOPK)
    top_w = jax.nn.softmax(top_v, axis=-1) * g_w
    within = jnp.sum(jax.nn.one_hot(top_i, EXPERTS_PER_GROUP, dtype=f32) * top_w[..., None], axis=1)
    combine = (jax.nn.one_hot(g_sel, N_GROUPS, dtype=f32)[:, :, None] * within[:, None, :]).reshape(-1, N_EXPERTS)
    y = jnp.zeros((b * t, d), f32)
    for e in range(N_EXPERTS):
        hid = jax.nn.silu(xf @ w_gate[e]) * (xf @ w_up[e])
        y = y + combine[:, e:e + 1] * (hid @ w_down[e]).astype(f32)
    return y.astype(h.dtype).reshape(b, t, d)

def second_inputs(seed: int = 0) -> dict:
    key = jax.random.key(seed)
    ks = jax.random.split(key, 20)
    f32 = jnp.float32

    def nrm(k, shape, scale):
        return jax.random.normal(k, shape, f32) * scale

    def gain(k, shape):
        return 1.0 + 0.02 * jax.random.normal(k, shape, f32)

    L = DEPTH_2
    return {
        'x': nrm(ks[0], (BATCH, SEQ, D_MODEL), 1.0),
        'g_mix': gain(ks[1], (L, D_MODEL)),
        'w_in': nrm(ks[2], (L, D_MODEL, D_IN), D_MODEL ** -0.5),
        'w_alpha2': nrm(ks[3], (L, GLA_GATE_RANK, GLA_QK_W), GLA_GATE_RANK ** -0.5),
        'b_alpha': nrm(ks[4], (L, GLA_QK_W), 0.1),
        'g_gla': gain(ks[5], (L, GLA_DV)),
        'w_br_gla': nrm(ks[6], (L, GLA_V_W, D_MODEL), GLA_V_W ** -0.5),
        'g_q': gain(ks[7], (L, ATT_DH)),
        'g_k': gain(ks[8], (L, ATT_DH)),
        'rel_bias': nrm(ks[9], (REL_BUCKETS, ATT_HEADS), 0.3),
        'w_br_att': nrm(ks[10], (L, ATT_W, D_MODEL), ATT_W ** -0.5),
        'w_out': nrm(ks[11], (L, D_MODEL, D_MODEL), D_MODEL ** -0.5),
        'g_ffn': gain(ks[12], (L, D_MODEL)),
        'w_rg': nrm(ks[13], (L, D_MODEL, N_GROUPS), D_MODEL ** -0.5),
        'b_rg': nrm(ks[14], (L, N_GROUPS), 0.01),
        'w_re': nrm(ks[15], (L, D_MODEL, N_EXPERTS), D_MODEL ** -0.5),
        'b_re': nrm(ks[16], (L, N_EXPERTS), 0.01),
        'w_gate': nrm(ks[17], (L, N_EXPERTS, D_MODEL, D_EXPERT), D_MODEL ** -0.5),
        'w_up': nrm(ks[18], (L, N_EXPERTS, D_MODEL, D_EXPERT), D_MODEL ** -0.5),
        'w_down': nrm(ks[19], (L, N_EXPERTS, D_EXPERT, D_MODEL), D_EXPERT ** -0.5),
    }

def second_block(x, g_mix, w_in, w_alpha2, b_alpha, g_gla, w_br_gla, g_q, g_k, rel_bias, w_br_att, w_out, g_ffn, w_rg, b_rg, w_re, b_re, w_gate, w_up, w_down):
    b, t, _ = x.shape
    split_points = [int(p) for p in np.cumsum(SPLITS)[:-1]]
    for l in range(DEPTH_2):
        hn = rms_norm_2(x, g_mix[l])
        proj = hn @ w_in[l]
        (qa, ka, va, ra, alr, qb, kb, vb, qi, ki, wi, gate_a, gate_b) = jnp.split(proj, split_points, axis=-1)
        ya = gla_mixer(qa, ka, va, ra, alr, w_alpha2[l], b_alpha[l], g_gla[l]) @ w_br_gla[l]
        qb = rms_norm_2(qb.reshape(b, t, ATT_HEADS, ATT_DH), g_q[l])
        kb = rms_norm_2(kb.reshape(b, t, ATT_HEADS, ATT_DH), g_k[l])
        vb = vb.reshape(b, t, ATT_HEADS, ATT_DH)
        qi = qi.reshape(b, t, IDX_HEADS, IDX_DH)
        wi = wi * (IDX_HEADS ** -0.5 * IDX_DH ** -0.5)
        yb = dsa_mixer(qb, kb, vb, qi, ki, wi, rel_bias) @ w_br_att[l]
        mixed = jax.nn.sigmoid(gate_a) * ya + jax.nn.sigmoid(gate_b) * yb
        x = x + mixed @ w_out[l]
        x = x + hier_moe(rms_norm_2(x, g_ffn[l]), w_rg[l], b_rg[l], w_re[l], b_re[l], w_gate[l], w_up[l], w_down[l])
    return x


def setup_inputs(seed=0):
    out = dict(first_inputs(seed))
    for name, value in second_inputs(seed + 1).items():
        if name != "x":
            out[name + "_2"] = value
    return out


def reference(
    x, mem, diff_w_qkv, diff_lambda, diff_subln, diff_w_o, dil_w_qkv, dil_w_o, rwkv_mu,
    rwkv_w_rkv, rwkv_w0, rwkv_w1, rwkv_w2, rwkv_a0, rwkv_a1, rwkv_a2, rwkv_g1, rwkv_g2,
    rwkv_k_k, rwkv_k_a, rwkv_r_k, rwkv_gn_g, rwkv_gn_b, rwkv_w_o, xatt_w_q, xatt_w_kv, xatt_w_o,
    ffn_w_in, ffn_conv_w, ffn_conv_b, ffn_w_out, ln_g, ln_b, g_mix_2, w_in_2, w_alpha2_2,
    b_alpha_2, g_gla_2, w_br_gla_2, g_q_2, g_k_2, rel_bias_2, w_br_att_2, w_out_2, g_ffn_2,
    w_rg_2, b_rg_2, w_re_2, b_re_2, w_gate_2, w_up_2, w_down_2,
):
    x = first_block(
        x, mem, diff_w_qkv, diff_lambda, diff_subln, diff_w_o, dil_w_qkv, dil_w_o, rwkv_mu,
        rwkv_w_rkv, rwkv_w0, rwkv_w1, rwkv_w2, rwkv_a0, rwkv_a1, rwkv_a2, rwkv_g1, rwkv_g2,
        rwkv_k_k, rwkv_k_a, rwkv_r_k, rwkv_gn_g, rwkv_gn_b, rwkv_w_o, xatt_w_q, xatt_w_kv,
        xatt_w_o, ffn_w_in, ffn_conv_w, ffn_conv_b, ffn_w_out, ln_g, ln_b,
    )
    return second_block(
        x, g_mix_2, w_in_2, w_alpha2_2, b_alpha_2, g_gla_2, w_br_gla_2, g_q_2, g_k_2,
        rel_bias_2, w_br_att_2, w_out_2, g_ffn_2, w_rg_2, b_rg_2, w_re_2, b_re_2, w_gate_2,
        w_up_2, w_down_2,
    )


_drawn_inputs = setup_inputs


def setup_inputs(seed=0):
    import zlib

    import numpy as np

    out = dict(_drawn_inputs(seed))
    spreads = {}
    factors = {'diff_lambda': 5.7,
     'diff_subln': 3.174,
     'ffn_conv_b': 3.189,
     'g_gla_2': 10.674,
     'g_q_2': 8.0,
     'g_k_2': 8.0,
     'b_rg_2': 26.809,
     'b_re_2': 17.576,
     'rel_bias_2': 4.168,
     'g_ffn_2': 2.86}
    for name, (base, spread) in spreads.items():
        noise = np.random.default_rng([zlib.crc32(name.encode()), seed]).standard_normal(out[name].shape)
        drawn = base * np.exp(spread * noise) if base else spread * noise
        out[name] = jnp.asarray(drawn.astype(out[name].dtype))
    for name, factor in factors.items():
        out[name] = (out[name] * factor).astype(out[name].dtype)
    return out
```

```python
import math
from contextlib import ExitStack

import numpy as np

import concourse.bass as bass
from concourse import mybir

F32 = mybir.dt.float32
F32R = mybir.dt.float32r
ALU = mybir.AluOpType
ACT = mybir.ActivationFunctionType
AX_X = mybir.AxisListType.X

P = 128
T = 512
TT = T // P
D = 1024
KC = D // P
M = 256
LAYERS = 2
ALPHA = (2 * LAYERS) ** 0.25
UC = 256
HIDDEN_PARTS = (8, 8, 6)
FF = 2816
DIFF_H, DIL_H = 8, 16
LAMBDA_INIT = 0.8 - 0.6 * math.exp(-0.3 * 0)
LN_EPS = 1e-5
RMS_EPS = 1e-6
MASKED = -1e30
TAKEN = -3e38
EXPERTS, PART_EXPERTS, GROUPS, PER_GROUP = 32, 8, 4, 8
TOPK = 128
ZW = 7 * P
ZC = 3 * P
DILW = 515 + 2 * P

SPLITS = [256, 256, 512, 512, 16, 512, 512, 512, 256, 32, 8, 1024, 1024]
(C_QA, C_KA, C_VA, C_RA, C_AL, C_QB, C_KB, C_VB, C_QI, C_KI, C_WI, C_GA, C_GB, _) = [
    int(v) for v in np.cumsum([0] + SPLITS)]

R_LNG, R_LNB, R_GMIX, R_GFFN, R_SUBLN, R_GGLA, R_GQ, R_GK = 0, 48, 96, 104, 112, 113, 114, 115
R_CONVB = 66


class Lin:

    def __init__(self, base, step=0, reg=None):
        self.base, self.step, self.reg = base, step, reg

    def __add__(self, k):
        return Lin(self.base + k, self.step, self.reg)

    def __mul__(self, k):
        return Lin(self.base * k, self.step * k, self.reg)

    def half(self):
        assert self.step % 2 == 0
        return Lin(self.base // 2, self.step // 2, self.reg)

    @property
    def v(self):
        return self.base if self.reg is None or self.step == 0 else self.reg * self.step + self.base

    def at(self):
        return slice(self.base, self.base + 1) if self.reg is None or self.step == 0 else bass.ds(self.v, 1)


def tables():
    f = np.float32
    eye = np.eye(P, dtype=f)
    half = np.zeros((P, P), f)
    half[:64, :64] = half[64:, 64:] = 1 / 64
    t = np.arange(P)
    later = ((t[:, None] > t[None, :]) & (t[:, None] // 64 == t[None, :] // 64)).astype(f) / 16
    rep = (t[:, None] == t[None, :] % 32).astype(f)
    idx = np.tile(np.arange(PER_GROUP, dtype=f), 16)
    const = np.concatenate([eye, half, np.full((P, P), 1 / D, f), np.full((P, P), 1 / P, f), later, rep,
                            np.broadcast_to(idx, (P, P))], axis=1)
    p, m = t[:, None], np.arange(ZW)[None, :]
    dist = np.abs(m - ZC - p).astype(f)
    slopes = np.exp2(-8.0 * np.arange(1, DIFF_H + 1, dtype=f) / DIFF_H).astype(f)
    diff_bias = -8 * slopes[:, None, None] * dist
    slopes = np.exp2(-8.0 * np.arange(1, DIL_H + 1, dtype=f) / DIL_H).astype(f)
    near = np.abs(4 * p - (np.arange(515)[None, :] - 3))
    u = np.abs(p - t[None, :])
    dil_bias = np.zeros((DIL_H + 2, P, DILW), f)
    for h in range(DIL_H):
        dil_bias[h, :, :515] = np.where(near <= 64, -8 * slopes[h] * near, MASKED)
        dil_bias[h, :, 515:643] = np.where(u <= 64, -8 * slopes[h] * 4 * u, MASKED)
        dil_bias[h, :, 643:] = np.where(u % 4 == 0, -8 * slopes[h] * 4 * u, MASKED)
    rel = np.arange(-511, 512)
    n = np.abs(rel)
    large = 8 + sum((n >= b).astype(int) for b in (12, 16, 23, 32, 46, 64, 91))
    bucket = np.where(rel > 0, 16, 0) + np.where(n < 8, n, large)
    onehot = (np.arange(32)[:, None] == bucket[None, :]).astype(f) * 8
    onehot = np.concatenate([onehot, np.zeros((32, 1), f)], axis=1)
    return {"one_row": np.ones((1, T), f), "const": const, "diff_bias": diff_bias.astype(f), "dil_bias": dil_bias, "onehot": onehot}


def program(nc, a, out):
    with ExitStack() as ctx:
        base = (nc.sbuf_base + 31) // 32 * 32

        def at(name, kb, shape, dt=F32):
            return nc.alloc_sbuf_tensor_at(name, shape, dt, offset=base + int(kb * 1024))

        made = []

        def sem(name):
            made.append(name)
            return ctx.enter_context(nc.semaphore(name))

        X = at("X", 0, [P, KC, T])
        xh = at("xh", 16, [P, KC, T], F32R)
        xl = at("xl", 32, [P, KC, T], F32R)
        raw = at("raw", 48, [P, 2, KC, UC])
        wh = at("wh", 64, [P, 2, KC, UC], F32R)
        wl = at("wl", 80, [P, 2, KC, UC], F32R)
        const = at("const", 96, [P, 7, P])
        ident, half_mean, mean_d, mean_p, later, rep32, idx8 = (const[:, n, :] for n in range(7))
        par = at("par", 99.5, [P, 3, P])
        small = at("small", 101, [P, 128])
        ones = at("ones", 101.5, [P, P])
        mean = at("mean", 102, [P, T])
        rstd = at("rstd", 104, [P, T])
        t2 = at("t2", 106, [P, 2, T])
        zz = at("zz", 110, [P, 2, T])
        acc_s = at("acc_s", 203.75, [P, 1, T])
        acc_q = at("acc_q", 205.75, [P, T])
        ah = at("ah", 114, [P, KC, T], F32R)
        al = at("al", 130, [P, KC, T], F32R)
        A0 = 146
        xrows = at("xrows", 0, [P, TT, D])
        prow = at("prow", A0, [P, 3, P])
        lamb = at("lamb", A0 + 2, [P, 4, 64])
        hot = at("hot", A0 + 4, [32, 1024])
        relb = at("relb", A0 + 8, [32, 8])
        zline = at("zline", 203.75, [8, 1024])
        d_q = at("d_q", A0, [P, 2, T])
        d_k = at("d_k", A0 + 4, [P, 2, T])
        d_v = at("d_v", A0 + 8, [P, TT, UC])
        d_bias = at("d_bias", A0 + 12, [P, 2, ZW])
        d_t = at("d_t", A0 + 19, [P, 2, 2, T])
        d_e = at("d_e", A0 + 27, [P, 3, T])
        d_e1 = at("d_e1", A0 + 55, [P, 2, T])
        d_pt = at("d_pt", A0 + 35, [P, 2, TT, T])
        d_o = at("d_o", A0 + 51, [P, T])
        d_sq = at("d_sq", A0 + 53, [P, T])
        l_q = at("l_q", A0, [P, 3, 2, T])
        l_k = at("l_k", A0 + 12, [P, 3, 2, T])
        l_v = at("l_v", A0 + 24, [P, 3, TT, UC])
        l_bias = at("l_bias", A0 + 36, [P, 2, DILW])
        l_t = at("l_t", A0 + 42.125, [P, 2, 768])
        l_e = at("l_e", A0 + 48.125, [P, 3, 768])
        l_pt = at("l_pt", 0, [P, 6, T])
        mrows = at("mrows", A0, [P, 2, D])
        mh = at("mh", A0 + 8, [P, KC, M], F32R)
        ml = at("ml", A0 + 16, [P, KC, M], F32R)
        x_k = at("x_k", A0 + 24, [P, KC, M])
        x_v = at("x_v", A0 + 32, [P, 2, D])
        x_q = at("x_q", A0, [P, KC, T])
        x_pt = at("x_pt", A0 + 40, [P, 8, T])
        x_e = at("x_e", A0 + 16, [P, 2, 4 * M])
        f_c = at("f_c", A0, [P, 2, T])
        f_g = at("f_g", A0 + 4, [P, 2, T])
        f_y = at("f_y", A0 + 8, [P, 2, T])
        m_w = at("m_w", A0 + 12, [P, 2, T])
        i_q = at("i_q", A0, [P, 2, T])
        i_k = at("i_k", A0 + 4, [P, T])
        i_m = at("i_m", A0 + 6, [P, TT, T])
        s_k = at("s_k", A0 + 14, [P, TT, T])
        s_q = at("s_q", A0 + 22, [P, TT, T])
        s_v = at("s_v", A0 + 30, [P, TT, T])
        g_q = at("g_q", A0 + 38, [P, 2, T])
        g_k = at("g_k", A0 + 42, [P, TT, UC])
        g_v = at("g_v", A0 + 46, [P, TT, T])
        g_r = at("g_r", A0 + 30, [P, TT, T])
        g_a = at("g_a", 138, [P, TT, UC])
        g_d = at("g_d", 200, [P, TT, UC])
        g_dec = at("g_dec", 204, [P, 2, 8])
        walpha = at("walpha", 205, [P, UC])
        sm_t = at("sm_t", A0 + 14, [P, T])
        m_lg = at("m_lg", A0 + 16, [P, TT, 36])
        m_rb = at("m_rb", A0 + 17, [P, 36])
        m_cw = at("m_cw", A0 + 17.5, [P, TT, GROUPS, PER_GROUP])
        m_tmp = at("m_tmp", A0 + 18, [P, 2, TT, GROUPS, PER_GROUP])
        m_e = at("m_e", A0 + 19, [P, 5, TT, PER_GROUP])
        m_g = at("m_g", A0 + 20, [P, 16, TT])
        m_oh = at("m_oh", A0 + 20.5, [P, 3, TT, GROUPS])
        m_cwt = at("m_cwt", A0 + 22, [EXPERTS, T])
        orow = at("orow", 16, [P, TT, D])
        s_z = at("s_z", A0 + 38, [P, 2, ZW])
        s_b = at("s_b", A0 + 45, [P, 2, T])
        s_t = at("s_t", A0 + 49, [P, 2, T])
        s_e = at("s_e", A0 + 53, [P, 3, T])
        s_pt = at("s_pt", A0, [P, 2, T])
        gate_a = at("gate_a", A0 + 29.75, [P, KC, T])
        gate_b = at("gate_b", A0 + 45.75, [P, KC, T])
        gh = at("gh", 114, [P, TT, T], F32R)
        gl = at("gl", 122, [P, TT, T], F32R)
        sh = at("sh", 130, [P, TT, T], F32R)
        sl = at("sl", 138, [P, TT, T], F32R)
        g_st = at("g_st", 130, [P, 2, 8, P])
        i_r = at("i_r", 142, [P, 2, T])
        ps = ctx.enter_context(nc.psum_tensor("ps", [P, 8, T], F32))
        flat = ps[:, :, :].rearrange("p b n -> p (b n)")
        scratch = nc.dram_tensor("cw_scratch", [EXPERTS, T], F32).ap()
        zscratch = nc.dram_tensor("z_scratch", [8, 1024], F32).ap()
        zcopies = nc.dram_tensor("z_copies", [8, P, 1024], F32).ap()

        negm = small[:, 0:16].rearrange("p (b n) -> p b n", b=2)
        sums = small[:, 16:32].rearrange("p (b n) -> p b n", b=2)
        rec = small[:, 32:48].rearrange("p (b n) -> p b n", b=2)
        mx = small[:, 48:64].rearrange("p (b n) -> p b n", b=2)
        neglam = small[:, 64:65]
        lam_s = small[:, 65:67]
        lam_e = small[:, 67:69]
        subln8 = small[:, 69:70]
        idle = small[:, 120:121]
        m8 = small[:, 72:80]
        wi_row = small[:, 80:112].rearrange("p (t n) -> p t n", t=TT)

        U_ATT = (0, 66)
        N_GROUP = (3, 9)
        U_WO = (12, 102)
        U_MEM = (16, 106)
        U_MQ = (24, 114)
        U_MO = (28, 118)
        U_FF = (32, 122)
        U_QI, U_SM, U_QA, U_KA, U_VA, U_RA, U_QB, U_KB, U_VB, U_GA, U_GB, U_BR, U_OUT, U_RT, U_EX = (
            156, 157, 158, 159, 160, 162, 164, 166, 168, 170, 174, 178, 186, 190, 191)
        UNITS = 239

        raw_in = [sem("raw_in0"), sem("raw_in1")]
        hi_done, lo_done = sem("hi_done"), sem("lo_done")
        chunk_done = sem("chunk_done")
        drained = [sem("drained0"), sem("drained1")]
        x_in, p_in, m_in, lam_in, z_in, zs_out = (sem(n) for n in ("x_in", "p_in", "m_in", "lam_in", "z_in", "zs_out"))
        zc_out = sem("zc_out")
        xt_done, par_t, par_s = sem("xt_done"), sem("par_t"), sem("par_s")
        z_mm, z_cp = sem("z_mm"), sem("z_cp")
        lam_d, lam_x = sem("lam_d"), sem("lam_x")
        ones_set = sem("ones_set")
        xh_ready, xl_ready = sem("xh_ready"), sem("xl_ready")
        y_ready, sq_done, acc_s_done, acc_q_done = sem("y_ready"), sem("sq_done"), sem("acc_s_done"), sem("acc_q_done")
        stat_mm, ln_act, ln_dve = sem("stat_mm"), sem("ln_act"), sem("ln_dve")
        cent, nrm, z_ready = sem("cent"), sem("nrm"), sem("z_ready")
        dbias_in = [sem("dbias_in0"), sem("dbias_in1")]
        d_qk, d_scored, d_negm, d_exp, d_rec, d_mix = (sem("d_" + n) for n in ("qk", "scored", "negm", "exp", "rec", "mix"))
        d_half, d_tr, d_ptr, d_pv, d_osb, d_st, d_var, d_ln, d_on, d_z = (
            sem("d_" + n) for n in ("half", "tr", "ptr", "pv", "osb", "st", "var", "ln", "on", "z"))
        ah_ready, al_ready = sem("ah_ready"), sem("al_ready")
        lbias_in = [sem("lbias_in0"), sem("lbias_in1")]
        l_qk, l_scored, l_negm, l_exp, l_rec, l_mix, l_tr, l_ptr, l_pv, l_ah, l_al = (
            sem("l_" + n) for n in ("qk", "scored", "negm", "exp", "rec", "mix", "tr", "ptr", "pv", "ah", "al"))
        mt_done, mh_done, ml_done = sem("mt_done"), sem("mh_done"), sem("ml_done")
        x_qk, x_max, x_negm, x_exp, x_rec, x_mix, x_tr, x_ptr, x_pv, x_ah, x_al = (
            sem("x_" + n) for n in ("qk", "max", "negm", "exp", "rec", "mix", "tr", "ptr", "pv", "ah", "al"))
        sm_done, ik_mm, wi_tr, wi_s, i_qk, i_relu, i_acc, i_max, i_cut, i_mask, i_edge = (
            sem(n) for n in ("sm_done", "ik_mm", "wi_tr", "wi_s", "i_qk", "i_relu", "i_acc", "i_max", "i_cut",
                             "i_mask", "i_edge"))
        wa_in, g_z, g_abs, g_la, g_lat, g_tot, g_ex, g_kd, g_u, g_state, g_o, g_sq, g_st_mm, g_var, g_ln, g_n, g_y, \
            g_hh, g_ll = (sem(n) for n in ("wa_in", "g_z", "g_abs", "g_la", "g_lat", "g_tot", "g_ex", "g_kd", "g_u",
                                           "g_state", "g_o", "g_sq", "g_st_mm", "g_var", "g_ln", "g_n", "g_y", "g_hh",
                                           "g_ll"))
        q_sq, q_mm, q_var, q_ln, q_n = (sem("q_" + n) for n in ("sq", "mm", "var", "ln", "n"))
        sz_in = [sem("sz_in0"), sem("sz_in1")]
        s_bm, s_qk, s_scored, s_negm, s_exp, s_rec, s_mix, s_tr, s_ptr, s_pv, s_hh, s_ll = (
            sem("s_" + n) for n in ("bm", "qk", "scored", "negm", "exp", "rec", "mix", "tr", "ptr", "pv", "hh", "ll"))
        b_prod, b_sum = sem("b_prod"), sem("b_sum")
        rb_in, r_step, r_act, cw_tr, cw_cp, cw_out = (sem(n) for n in ("rb_in", "r_step", "r_act", "cw_tr", "cw_cp",
                                                                      "cw_out"))
        mw_in = [sem("mw_in0"), sem("mw_in1")]
        m_y, m_hh, m_hl, m_sum = sem("m_y"), sem("m_hh"), sem("m_hl"), sem("m_sum")
        o_tr, o_cp, o_out = sem("o_tr"), sem("o_cp"), sem("o_out")
        f_cd, f_left, f_gd, f_y_s, f_hh, f_hl = (sem("f_" + n) for n in ("c", "left", "g", "y", "hh", "hl"))

        NORM_AT = [(n + 1, 3 * n + 3, 3 * n + 3) for n in range(6)] + [(6, 20, 19), (8, 22, 20)]
        MIXED = 7

        def slot_of(u):
            assert u.step % 2 == 0
            return u.base % 2

        def emptied(eng, u):
            eng.wait_ge(drained[slot_of(u)], (u.half() * 2 + 2).v)

        def over(eng, u0, n, body, peel=2):
            peel = min(peel, n)
            for k in range(peel):
                body(Lin(u0 + k), Lin(k))
            pairs = (n - peel) // 2
            if pairs > 1:
                with eng.Fori(0, pairs) as i:
                    for k in range(peel, peel + 2):
                        body(Lin(u0 + k, 2, i), Lin(k, 2, i))
            else:
                for k in range(peel, peel + 2 * pairs):
                    body(Lin(u0 + k), Lin(k))
            for k in range(peel + 2 * pairs, n):
                body(Lin(u0 + k), Lin(k))

        block = ctx.enter_context(nc.Block())

        @block.sync
        def _(sp):
            def load(u, *parts):
                s = slot_of(u)
                if u.base >= 2:
                    sp.wait_ge(lo_done, (u + -1).v)
                for dst, src in parts:
                    sp.dma_start(dst(s), src).then_inc(raw_in[s], 16)

            def square(u, w, col, k0=0, kcs=KC):
                w3 = w.rearrange("(k p) n -> p k n", p=P)
                h = kcs // 2
                cols = bass.ds(col, UC)
                load(u, (lambda s: raw[:, s, 0:h, :], w3[:, k0:k0 + h, cols]),
                     (lambda s: raw[:, s, h:kcs, :], w3[:, k0 + h:k0 + kcs, cols]))

            def pair(u, w, c0, c1):
                w3 = w.rearrange("(k p) n -> p k n", p=P)
                load(u, (lambda s: raw[:, s, :, 0:P], w3[:, :, bass.ds(c0, P)]),
                     (lambda s: raw[:, s, :, P:UC], w3[:, :, bass.ds(c1, P)]))

            sp.dma_start(xrows[:], a["x"][0].rearrange("(t p) d -> p t d", p=P)).then_inc(x_in, 16)
            sp.dma_start(const[:], a["const"].rearrange("p (n m) -> p n m", m=P)).then_inc(x_in, 16)
            qkv = a["diff_w_qkv"][0]

            def prows(row, block_, name, view):
                n = view.shape[0]
                sp.dma_start(prow[row:row + n, block_, 0:view.shape[1]], view).then_inc(p_in, 16)

            prows(R_LNG, 0, "ln_g", a["ln_g"].rearrange("l s (c p) -> (l s c) p", p=P))
            prows(R_LNB, 0, "ln_b", a["ln_b"].rearrange("l s (c p) -> (l s c) p", p=P))
            prows(R_GMIX, 0, "g_mix", a["g_mix_2"][0].rearrange("(c p) -> c p", p=P))
            prows(R_GFFN, 0, "g_ffn", a["g_ffn_2"][0].rearrange("(c p) -> c p", p=P))
            prows(R_SUBLN, 0, "subln", a["diff_subln"])
            prows(R_GGLA, 0, "g_gla", a["g_gla_2"])
            for side in range(2):
                for row, name in ((R_GQ, "g_q_2"), (R_GK, "g_k_2")):
                    sp.dma_start(prow[row:row + 1, 0, 64 * side:64 * side + 64], a[name]).then_inc(p_in, 16)
            for layer in range(LAYERS):
                prows(0, 1 + layer, "conv_w", a["ffn_conv_w"][layer].rearrange("w (c p) -> (w c) p", p=P))
                prows(R_CONVB, 1 + layer, "conv_b", a["ffn_conv_b"][layer].rearrange("(c p) -> c p", p=P))
            sp.dma_start(lamb[:, :, :].rearrange("p a b -> p (a b)"),
                         a["diff_lambda"].rearrange("o a b -> o (a b)").to_broadcast([P, 256])).then_inc(lam_in, 16)
            sp.dma_start(hot[:], a["onehot"]).then_inc(z_in, 16)
            sp.dma_start(relb[:], a["rel_bias_2"]).then_inc(z_in, 16)
            def diff_group(g):
                for role in range(3):
                    u = g * 3 + role
                    square(u, qkv, (g * UC + role * D).v)
                for b in range(2):
                    h = g * 2 + b
                    sp.wait_ge(d_scored, (h * 8).v)
                    sp.dma_start(d_bias[:, b, :], a["diff_bias"].rearrange("h p n -> p h n")[:, bass.ds(h.v, 1), :]
                                 ).then_inc(dbias_in[b], 16)

            diff_group(Lin(0))
            diff_group(Lin(1))
            diff_group(Lin(2))
            diff_group(Lin(3))

            def after_attention(layer, w_o):
                for k in range(2):
                    square(Lin(U_WO[layer] + k), w_o, k * UC)
                sp.wait_ge((al_ready, l_al)[layer], 8 + 1)
                sp.dma_start(mrows[:], a["mem"][0].rearrange("(t p) d -> p t d", p=P)).then_inc(m_in, 16)
                for k in range(2, 4):
                    square(Lin(U_WO[layer] + k), w_o, k * UC)
                kv = a["xatt_w_kv"][layer]
                over(sp, U_MEM[layer], 8, lambda u, k: square(u, kv, (k * UC).v))
                over(sp, U_MQ[layer], 4, lambda u, k: square(u, a["xatt_w_q"][layer], (k * UC).v))
                over(sp, U_MO[layer], 4, lambda u, k: square(u, a["xatt_w_o"][layer], (k * UC).v))
                u0, f0 = U_FF[layer], 0
                for n in HIDDEN_PARTS:
                    win = a["ffn_w_in"][layer]
                    over(sp, u0, n, lambda u, k: pair(u, win, ((k + f0) * P).v, ((k + f0) * P + FF).v))
                    wout = a["ffn_w_out"][layer]
                    over(sp, u0 + n, 4, lambda u, k: square(u, wout, (k * UC).v, k0=f0, kcs=n))
                    u0, f0 = u0 + n + 4, f0 + n

            after_attention(0, a["diff_w_o"][0])
            sp.wait_ge(zs_out, 16)
            for h in range(8):
                sp.dma_start(zcopies[h:h + 1, :, :], zscratch[h:h + 1, :].unsqueeze(1).to_broadcast([1, P, 1024])
                             ).then_inc(zc_out, 16)
            lqkv = a["dil_w_qkv"][0]

            def dil_group(g):
                for n in range(9):
                    square(g * 9 + (n + U_ATT[1]), lqkv, (g * UC + n * D).v)
            sp.wait_ge(x_ptr, TT)
            for b in range(2):
                sp.dma_start(l_bias[:, b, :], a["dil_bias"][b]).then_inc(lbias_in[b], 16)
            with sp.Fori(0, 2) as i:
                dil_group(Lin(0, 2, i))
                dil_group(Lin(1, 2, i))
            after_attention(1, a["dil_w_o"][0])

            w_in = a["w_in_2"][0]
            w3 = w_in.rearrange("(k p) n -> p k n", p=P)
            square(Lin(U_QI), w_in, C_QI)
            load(Lin(U_SM), (lambda s: raw[:, s, :, 0:40], w3[:, :, C_KI:C_KI + 40]),
                 (lambda s: raw[:, s, :, 64:80], w3[:, :, C_AL:C_AL + 16]))
            square(Lin(U_QA), w_in, C_QA)
            sp.wait_ge(xh_ready, KC * 6 + 1)
            sp.dma_start(walpha[64:80, :], a["w_alpha2_2"][0]).then_inc(wa_in, 16)
            sp.dma_start(walpha[80:81, :], a["b_alpha_2"]).then_inc(wa_in, 16)
            sp.dma_start(sm_t[80:81, :], a["one_row"]).then_inc(wa_in, 16)
            square(Lin(U_KA), w_in, C_KA)
            for k in range(2):
                square(Lin(U_VA + k), w_in, C_VA + k * UC)
            for k in range(2):
                square(Lin(U_RA + k), w_in, C_RA + k * UC)
            for k in range(2):
                square(Lin(U_QB + k), w_in, C_QB + k * UC)
            for k in range(2):
                square(Lin(U_KB + k), w_in, C_KB + k * UC)
            for k in range(2):
                square(Lin(U_VB + k), w_in, C_VB + k * UC)
            for k in range(2):
                square(Lin(U_GA + k), w_in, C_GA + k * UC)
            for h in range(8):
                if h == 0:
                    sp.wait_ge(zc_out, 16 * 8)
                    sp.wait_ge(g_hh, 4)
                    sp.wait_ge(g_ll, 4)
                if h >= 2:
                    sp.wait_ge(s_bm, TT * (h - 1))
                z = zcopies[h:h + 1, :, :]
                shifted = bass.AP(tensor=z.tensor, offset=z.offset + P - 1, ap=[[1023, P], [1, ZW]])
                sp.dma_start(s_z[:, h % 2, :], shifted).then_inc(sz_in[h % 2], 16)
            for k in range(2, 4):
                square(Lin(U_GA + k), w_in, C_GA + k * UC)
            over(sp, U_GB, 4, lambda u, k: square(u, w_in, (k * UC + C_GB).v))
            br_g = a["w_br_gla_2"][0].rearrange("(k p) n -> p k n", p=P)
            br_s = a["w_br_att_2"][0].rearrange("(k p) n -> p k n", p=P)
            over(sp, U_BR, KC, lambda u, k: load(
                u, (lambda s: raw[:, s, 0:4, 0:P], br_g[:, :, bass.ds((k * P).v, P)]),
                (lambda s: raw[:, s, 4:8, 0:P], br_s[:, :, bass.ds((k * P).v, P)])))
            over(sp, U_OUT, 4, lambda u, k: square(u, a["w_out_2"][0], (k * UC).v))
            load(Lin(U_RT),
                 (lambda s: raw[:, s, :, 0:EXPERTS], a["w_re_2"][0].rearrange("(k p) n -> p k n", p=P)),
                 (lambda s: raw[:, s, :, EXPERTS:36], a["w_rg_2"][0].rearrange("(k p) n -> p k n", p=P)))
            w_gate = a["w_gate_2"][0].rearrange("e (k p) n -> p (e k) n", p=P)
            w_up = a["w_up_2"][0].rearrange("e (k p) n -> p (e k) n", p=P)
            w_down = a["w_down_2"][0].rearrange("e p n -> p e n")

            def expert_weights(u, e):
                load(u, (lambda s: raw[:, s, :, 0:P], w_gate[:, bass.ds((e * KC).v, KC), :]),
                     (lambda s: raw[:, s, :, P:UC], w_up[:, bass.ds((e * KC).v, KC), :]))

            def combine_weights(e):
                b = e.base % 2
                if e.base >= 2:
                    sp.wait_ge(m_y, (e + -1).v)
                sp.dma_start(m_w[:, b, :], scratch[e.at(), :].to_broadcast([P, T])).then_inc(mw_in[b], 16)

            for part in range(EXPERTS // PART_EXPERTS):
                u0, e0 = U_EX + part * (PART_EXPERTS + 4), part * PART_EXPERTS

                def expert(u, k):
                    expert_weights(u, k + e0)
                    combine_weights(k + e0)

                if part == 0:
                    expert_weights(Lin(u0), Lin(0))
                    expert_weights(Lin(u0 + 1), Lin(1))
                    sp.wait_ge(xh_ready, KC * 8 + 1)
                    sp.dma_start(m_rb[:, 0:EXPERTS], a["b_re_2"].to_broadcast([P, EXPERTS])).then_inc(rb_in, 16)
                    sp.dma_start(m_rb[:, EXPERTS:36], a["b_rg_2"].to_broadcast([P, GROUPS])).then_inc(rb_in, 16)
                    expert_weights(Lin(u0 + 2), Lin(2))
                    expert_weights(Lin(u0 + 3), Lin(3))
                    sp.wait_ge(cw_out, 16)
                    for k in range(4):
                        combine_weights(Lin(k))
                    over(sp, u0 + 4, PART_EXPERTS - 4, lambda u, k: expert(u, k + 4), peel=0)
                else:
                    over(sp, u0, PART_EXPERTS, expert)
                h = PART_EXPERTS // 2
                over(sp, u0 + PART_EXPERTS, 4, lambda u, k: load(
                    u, (lambda s: raw[:, s, 0:h, :], w_down[:, e0:e0 + h, bass.ds((k * UC).v, UC)]),
                    (lambda s: raw[:, s, h:KC, :], w_down[:, e0 + h:e0 + 2 * h, bass.ds((k * UC).v, UC)])))
            orows = out[0].rearrange("(t p) d -> p t d", p=P)
            for q in range(4):
                sp.wait_ge(o_cp, 2 * q + 2)
                sp.dma_start(orows[:, :, q * UC:(q + 1) * UC], orow[:, :, q * UC:(q + 1) * UC]).then_inc(o_out, 16)
            sp.wait_ge(o_out, 64)

        @block.gpsimd
        def _(pool):
            def low(u):
                s = slot_of(u)
                pool.wait_ge(hi_done, (u + 1).v)
                pool.tensor_tensor(wl[:, s], raw[:, s], wh[:, s].bitcast(F32), ALU.subtract).then_inc(lo_done, 1)

            def lows(first, last):
                assert (last - first) % 2 == 0 and first % 2 == 0
                with pool.Fori(0, (last - first) // 2) as i:
                    low(Lin(first, 2, i))
                    low(Lin(first + 1, 2, i))

            lows(0, U_GA + 2)
            for h in range(8):
                pool.wait_ge(sz_in[h % 2], 16 * (h // 2) + 16)
                for i in range(TT):
                    n, w = TT * h + i, P * (i + 1)
                    if n == 0:
                        pool.wait_ge(i_mask, TT)
                    if n >= 2:
                        pool.wait_ge(s_scored, n - 1)
                    z0 = ZC - P * i
                    pool.tensor_tensor(s_b[:, n % 2, 0:w], s_z[:, h % 2, z0:z0 + w], i_m[:, i, 0:w], ALU.add
                                       ).then_inc(s_bm, 1)
            lows(U_GA + 2, UNITS - 1)
            low(Lin(UNITS - 1))

        @block.scalar
        def _(act):
            def high(u):
                s = slot_of(u)
                if u.step == 0 and u.base >= UNITS:
                    return
                act.wait_ge(raw_in[s], (u.half() * 32 + 32).v)
                if u.base >= 2:
                    act.wait_ge(chunk_done, (u * 2 + -2).v)
                act.activation(wh[:, s], raw[:, s], ACT.Copy).then_inc(hi_done, 1)

            def bank(u, j):
                return ps[:, 2 * slot_of(u) + j]

            def done(u, j):
                act.wait_ge(chunk_done, (u * 2 + (j + 1)).v)

            def copy_out(u, dst, func=ACT.Copy, scale=1.0):
                for j in range(2):
                    done(u, j)
                    act.activation(dst(j), bank(u, j), func, scale=scale).then_inc(drained[slot_of(u)], 1)

            for ahead in (d_ptr, d_osb, d_z, l_ptr):
                act.sem_inc(ahead, 1)
            high(Lin(0))
            high(Lin(1))
            act.wait_ge(lam_d, 4)
            act.activation(lam_e, lam_s, ACT.Exp).then_inc(lam_x, 1)
            for c in range(KC):
                act.wait_ge(xt_done, c + 1)
                act.activation(xh[:, c], ps[:, c % 4], ACT.Copy).then_inc(xh_ready, 1)
            act.wait_ge(par_t, 1)
            for n, rows_ in enumerate((R_GK + 1, 88, 88)):
                act.activation(par[:, n, 0:rows_], ps[:, 4, n * P:n * P + rows_], ACT.Copy).then_inc(par_s, 1)
            act.wait_ge(par_s, 3)
            act.activation(subln8, par[:, 0, R_SUBLN:R_SUBLN + 1], ACT.Copy, scale=1 - LAMBDA_INIT).then_inc(par_s, 1)
            act.wait_ge(z_mm, 2)
            for j in range(2):
                act.activation(zline[:, j * T:(j + 1) * T], ps[0:8, 5 + j], ACT.Copy).then_inc(z_cp, 1)
            act.wait_ge(z_cp, 2)
            act.dma_start(zscratch, zline[:]).then_inc(zs_out, 16)
            act.wait_ge(zs_out, 16)

            def diff_group(g):
                u = g * 3
                high(u + 2)
                copy_out(u, lambda j: d_q[:, j])
                high(u + 3)
                copy_out(u + 1, lambda j: d_k[:, j])
                act.wait_ge(chunk_done, (u * 2 + 6).v)
                high(u + 4)
                for l in range(8 + 6):
                    if l < 8:
                        n = g * 8 + l
                        b = l % 2
                        act.wait_ge(d_negm, (n + 1).v)
                        act.wait_ge(d_tr, (n + (1 if l < 2 else 0)).v)
                        for c in range(2):
                            act.activation(d_e[:, l % 3] if c == 0 else d_e1[:, b], d_t[:, b, c], ACT.Exp, bias=negm[:, b, c:c + 1], scale=0.125,
                                           accum_out=sums[:, b, c:c + 1]).then_inc(d_exp, 1)
                    if 2 <= l <= 9:
                        n = g * 8 + (l - 2)
                        hh, i = (l - 2) // 4, (l - 2) % 4
                        act.wait_ge(d_tr, (n + 3).v)
                        if i == 0:
                            act.wait_ge(d_pv, (g * 2 + (hh + 1)).v)
                        act.activation(d_pt[:, hh, :, i * P:(i + 1) * P],
                                       ps[:, l % 2].rearrange("p (k q) -> p k q", k=TT), ACT.Copy
                                       ).then_inc(d_ptr, 1)
                    if l in (7, 11):
                        h = g * 2 + (l - 7) // 4
                        act.wait_ge(d_pv, (h + 3).v)
                        act.wait_ge(d_on, (h + 1).v)
                        act.activation(d_o[:], ps[:, 2], ACT.Copy).then_inc(d_osb, 1)
                        act.wait_ge(d_st, (h + 1).v)
                        act.activation(d_sq[:], ps[:, 2], ACT.Square).then_inc(d_osb, 1)
                    if l in (8, 12):
                        h = g * 2 + (l - 8) // 4
                        act.wait_ge(d_var, (h + 1 + 1).v)
                        act.activation(mean[:], mean[:], ACT.Ln).then_inc(d_ln, 1)
                        act.wait_ge(d_ln, (h * 2 + 1).v)
                        act.activation(rstd[:], mean[:], ACT.Exp, scale=-0.5).then_inc(d_ln, 1)
                    if l in (9, 13):
                        h = g * 2 + (l - 9) // 4
                        act.wait_ge(d_on, (h + 1 + 1).v)
                        act.wait_ge(al_ready, (h + 1).v)
                        act.activation(zz[:, 0], t2[:, 0], ACT.Copy, scale=subln8).then_inc(d_z, 1)
                        act.wait_ge(d_z, (h + 1 + 1).v)
                        act.activation(ah[:, h.at(), :], zz[:, 0:1, :], ACT.Copy).then_inc(ah_ready, 1)

            act.wait_ge(xl_ready, KC)
            with act.Fori(0, 2) as i:
                diff_group(Lin(0, 2, i))
                diff_group(Lin(1, 2, i))

            def dil_group(g):
                u0 = g * 9 + U_ATT[1]
                for n in range(9):
                    u = u0 + n
                    done(u, 1)
                    high(u + 2)
                    p, role = n // 3, n % 3
                    if role < 2:
                        copy_out(u, lambda j: (l_q, l_k)[role][:, p, j])
                for l in range(16 + 4):
                    if l < 16:
                        n = g * 16 + l
                        act.wait_ge(l_negm, (n + 1).v)
                        act.wait_ge(l_tr, (n + (2 if l == 0 else 0)).v)
                        act.activation(l_e[:, l % 3], l_t[:, l % 2], ACT.Exp, bias=negm[:, l % 2, 0:1], scale=0.125,
                                       accum_out=sums[:, l % 2, 0:1]).then_inc(l_exp, 1)
                        if l % 4 == 3:
                            hh = l // 4
                            act.dma_start(l_bias[:, hh % 2, :],
                                          a["dil_bias"].rearrange("h p n -> p h n")[:, bass.ds((g * 4 + (hh + 2)).v, 1), :]
                                          ).then_inc(lbias_in[hh % 2], 16)
                    if 2 <= l <= 17:
                        n = g * 16 + (l - 2)
                        hh, j = (l - 2) // 4, (l - 2) % 4
                        act.wait_ge(l_tr, (n + 3).v)
                        if j == 0:
                            act.wait_ge(l_pv, (g * 4 + hh + 1).v)
                        act.activation(l_pt[:, :, j * P:(j + 1) * P],
                                       flat[:, 0:768].rearrange("p (k q) -> p k q", k=6), ACT.Copy
                                       ).then_inc(l_ptr, 1)
                    if l in (11, 19):
                        c = g * 2 + (l - 11) // 8
                        act.wait_ge(l_pv, (g * 4 + ((l - 11) // 8 * 2 + 2) + 1).v)
                        act.activation(ah[:, c.at(), :].rearrange("p c (u j) -> p c j u", j=4),
                                       ps[:, 2:3].rearrange("p c (j u) -> p c j u", j=4), ACT.Copy).then_inc(l_ah, 1)

            def norm(n, g_row, b_row=None, keep=False, between=None):
                event, on_act, on_dve = NORM_AT[n]
                if b_row is not None:
                    act.wait_ge(stat_mm, n + 1)
                    act.activation(mean[:], ps[:, 4], ACT.Copy).then_inc(ln_act, 1)
                act.wait_ge(ln_dve, on_dve)
                act.activation(acc_s[:, 0], acc_s[:, 0], ACT.Ln).then_inc(ln_act, 1)
                act.wait_ge(ln_act, on_act - 1)
                act.activation(rstd[:], acc_s[:, 0], ACT.Exp, scale=-0.5).then_inc(ln_act, 1)
                for c in range(KC):
                    act.wait_ge(nrm, KC * n + c + 1)
                    z = X[:, c] if keep else zz[:, c % 2]
                    if not keep and c >= 2:
                        act.wait_ge(xl_ready, KC * event + c - 1)
                    if b_row is None:
                        act.activation(z, t2[:, c % 2], ACT.Copy, scale=par[:, 0, g_row + c:g_row + c + 1]
                                       ).then_inc(z_ready, 1)
                    else:
                        act.activation(z, t2[:, c % 2], ACT.Identity, scale=par[:, 0, g_row + c:g_row + c + 1],
                                       bias=par[:, 0, b_row + c:b_row + c + 1]).then_inc(z_ready, 1)
                    act.wait_ge(z_ready, KC * n + c + 1)
                    if keep:
                        if c >= 2:
                            act.wait_ge(acc_q_done, 9 * (n + 1) + c)
                        act.activation(zz[:, c % 2], z, ACT.Square).then_inc(sq_done, 1)
                    else:
                        act.activation(xh[:, c], z, ACT.Copy).then_inc(xh_ready, 1)
                    if between and c in between:
                        high(Lin(between[c]))

            def squares(u, k, n):
                for j in range(2):
                    c = k * 2 + j
                    act.wait_ge(y_ready, (c + (KC * min(n, 6) + 1)).v)
                    act.wait_ge(acc_q_done, (c + (9 * n)).v)
                    act.activation(t2[:, j:j + 1], X[:, c.at(), :], ACT.Square).then_inc(sq_done, 1)

            def residual(u0, n):
                def body(u, k):
                    done(u, 1)
                    high(u + 2)
                    squares(u, k, n)
                over(act, u0, 4, body)

            def skip(u, k):
                done(u, 1)
                high(u + 2)

            def memory(layer):
                for b in range(4):
                    act.wait_ge(mt_done, 4 * layer + b + 1)
                    act.activation(mh[:, 2 * b:2 * b + 2, :], ps[:, 4 + b].rearrange("p (k t) -> p k t", k=2), ACT.Copy
                                   ).then_inc(mh_done, 1)

            def after_attention(layer):
                n0 = n = 3 * layer
                u0 = U_WO[layer]
                for k in range(2):
                    done(Lin(u0 + k), 1)
                    high(Lin(u0 + k + 2))
                    squares(Lin(u0 + k), Lin(k), n)
                memory(layer)
                for k in range(2, 4):
                    done(Lin(u0 + k), 1)
                    high(Lin(u0 + k + 2))
                    squares(Lin(u0 + k), Lin(k), n)
                u0 = U_MEM[layer]
                norm(n, R_LNG + 8 * n, R_LNB + 8 * n, between={3: u0 + 2, 7: u0 + 3})
                for k in range(8):
                    u = Lin(u0 + k)
                    if k >= 2:
                        done(u, 1)
                        high(u + 2)
                    for j in range(2 if k < 4 else 0):
                        done(u, j)
                        act.activation(x_k[:, 2 * k + j], bank(u, j)[:, 0:M], ACT.Copy).then_inc(drained[slot_of(u)], 1)

                def queries(u, k):
                    done(u, 1)
                    high(u + 2)
                    for j in range(2):
                        act.activation(x_q[:, (k * 2 + j).at(), :], ps[:, 2 * slot_of(u) + j:2 * slot_of(u) + j + 1],
                                       ACT.Copy).then_inc(drained[slot_of(u)], 1)

                over(act, U_MQ[layer], 4, queries)
                for i in range(TT + 1):
                    if i < TT:
                        n = TT * layer + i
                        act.wait_ge(x_negm, n + 1)
                        if i >= 2:
                            act.wait_ge(x_tr, n - 1)
                        for h in range(4):
                            act.activation(x_e[:, i % 2, h * M:(h + 1) * M],
                                           flat[:, 2048 + 1024 * (i % 2) + h * M:2048 + 1024 * (i % 2) + (h + 1) * M],
                                           ACT.Exp, bias=negm[:, i % 2, h:h + 1], scale=1 / 16,
                                           accum_out=sums[:, i % 2, h:h + 1]).then_inc(x_exp, 1)
                    if i >= 1:
                        n = TT * layer + i - 1
                        act.wait_ge(x_tr, n + 1)
                        s = 1024 * ((i - 1) % 2)
                        act.activation(x_pt[:, :, (i - 1) * P:i * P],
                                       flat[:, s:s + 1024].rearrange("p (k q) -> p k q", k=8), ACT.Copy
                                       ).then_inc(x_ptr, 1)
                for c in range(KC):
                    act.wait_ge(x_pv, KC * layer + c + 1)
                    act.activation(ah[:, c], ps[:, 4 + c % 4], ACT.Copy).then_inc(x_ah, 1)
                residual(U_MO[layer], n0 + 1)
                norm(n0 + 1, R_LNG + 8 * (n0 + 1), R_LNB + 8 * (n0 + 1))

                u0, f0 = U_FF[layer], 0
                for part, width in enumerate(HIDDEN_PARTS):
                    def hidden(u, k):
                        F = k + (FF // P * layer + f0)
                        s, b = slot_of(u), k.base % 2
                        w1 = par[:, 1 + layer, bass.ds((k + (FF // P + f0)).v, 1)]
                        bias = par[:, 1 + layer, bass.ds((k + (R_CONVB + f0)).v, 1)]
                        done(u, 0)
                        act.activation(f_c[:, b], bank(u, 0), ACT.Identity, scale=w1, bias=bias).then_inc(f_cd, 1)
                        done(u, 1)
                        high(u + 2)
                        act.wait_ge(drained[s], (u.half() * 2 + 1).v)
                        act.activation(f_g[:, b], f_c[:, b], ACT.Gelu).then_inc(f_gd, 1)
                        act.wait_ge(drained[s], (u.half() * 2 + 2).v)
                        act.activation(ah[:, k.at(), :], f_y[:, b:b + 1], ACT.Copy).then_inc(f_hh, 1)
                    over(act, u0, width, hidden)
                    if part < 2:
                        over(act, u0 + width, 4, skip)
                    else:
                        residual(u0 + width, n0 + 2)
                    u0, f0 = u0 + width + 4, f0 + width
                norm(n0 + 2, R_LNG + 8 * (n0 + 2), R_LNB + 8 * (n0 + 2), keep=layer == 1)

            after_attention(0)
            act.wait_ge(xl_ready, 4 * KC)
            with act.Fori(0, 2) as i:
                dil_group(Lin(0, 2, i))
                dil_group(Lin(1, 2, i))
            after_attention(1)

            norm(6, R_GMIX)

            def unit(u, dst, func=ACT.Copy, scale=1.0):
                done(Lin(u), 1)
                high(Lin(u + 2))
                copy_out(Lin(u), dst, func, scale)

            def pairs_of(x):
                return lambda j: x[:, 2 * j:2 * j + 2, :].rearrange("p t n -> p (t n)")

            unit(U_QI, lambda j: i_q[:, j])
            s = U_SM % 2
            done(Lin(U_SM), 0)
            act.activation(sm_t[0:80, :], ps[0:80, 2 * s, :], ACT.Copy).then_inc(sm_done, 1)
            done(Lin(U_SM), 1)
            high(Lin(U_SM + 2))
            act.activation(i_k[:], ps[:, 2 * s + 1], ACT.Copy).then_inc(drained[s], 1)
            act.sem_inc(drained[s], 1)
            act.wait_ge(wi_tr, 1)
            act.activation(wi_row, ps[:, 4, 0:32].rearrange("p (t n) -> p t n", t=TT), ACT.Copy, scale=1 / 16
                           ).then_inc(wi_s, 1)
            for m in range(8 * (TT - 1)):
                i = m // 8 + 1
                act.wait_ge(i_qk, m + 1)
                if m >= 2:
                    act.wait_ge(i_acc, m - 1)
                act.activation(i_r[:, m % 2, 0:P * (i + 1)], ps[:, 4 + m % 4, 0:P * (i + 1)], ACT.Relu
                               ).then_inc(i_relu, 1)
            unit(U_QA, lambda j: g_q[:, j], scale=1 / 8)
            unit(U_KA, pairs_of(g_k))
            for k in range(2):
                u = Lin(U_VA + k)
                done(u, 1)
                high(u + 2)
                for j in range(2):
                    act.activation(g_v[:, 2 * j:2 * j + 2, k * UC:(k + 1) * UC],
                                   bank(u, j).rearrange("p (t n) -> p t n", t=2), ACT.Copy
                                   ).then_inc(drained[slot_of(u)], 1)
            for k in range(2):
                unit(U_RA + k, lambda j: g_r[:, 2 * k + j], ACT.Silu)
            for j in range(2):
                act.wait_ge(g_z, j + 1)
                act.activation(pairs_of(g_d)(j), ps[:, 4 + j], ACT.Abs).then_inc(g_abs, 1)
            for j in range(2):
                act.wait_ge(g_abs, 1 + j)
                act.activation(pairs_of(g_d)(j), pairs_of(g_d)(j), ACT.Exp, scale=-1.0).then_inc(g_abs, 1)
            for j in range(2):
                act.wait_ge(g_abs, 3 + j)
                act.activation(pairs_of(g_d)(j), pairs_of(g_d)(j), ACT.Ln, bias=ones[:, 0:1]).then_inc(g_abs, 1)
            unit(U_QB, lambda j: s_q[:, j])
            for j in range(2):
                act.wait_ge(g_lat, j + 1)
                act.activation(pairs_of(g_d)(j), ps[:, 6 + j], ACT.Exp).then_inc(g_ex, 1)
            act.wait_ge(g_tot, 1)
            for j in range(2):
                act.activation(g_dec[:, j], ps[:, 4 + j, 0:8], ACT.Exp, scale=1 / 16).then_inc(g_ex, 1)
            unit(U_QB + 1, lambda j: s_q[:, 2 + j])
            unit(U_KB, lambda j: s_k[:, j])

            def gla_squares(h):
                act.wait_ge(g_o, h + 1)
                if h >= 2:
                    act.wait_ge(g_ll, h - 1)
                act.activation(zz[:, h % 2], ps[:, 4 + h], ACT.Copy).then_inc(g_sq, 1)
                act.activation(t2[:, h % 2], ps[:, 4 + h], ACT.Square).then_inc(g_sq, 1)

            def gla_rstd(h):
                act.wait_ge(g_var, h + 1)
                act.activation(mean[:], mean[:], ACT.Ln).then_inc(g_ln, 1)
                act.wait_ge(g_ln, 2 * h + 1)
                if h >= 1:
                    act.wait_ge(g_n, h)
                act.activation(rstd[:], mean[:], ACT.Exp, scale=-0.5).then_inc(g_ln, 1)

            def gla_high(h):
                act.wait_ge(g_y, h + 1)
                act.activation(gh[:, h], zz[:, h % 2], ACT.Copy).then_inc(g_hh, 1)

            gla_squares(0)
            gla_squares(1)
            unit(U_KB + 1, lambda j: s_k[:, 2 + j])
            gla_rstd(0)
            gla_rstd(1)
            for h in range(2):
                gla_high(h)
                gla_squares(h + 2)
            done(Lin(U_VB), 1)
            high(Lin(U_VB + 2))
            gla_rstd(2)
            gla_rstd(3)
            gla_high(2)
            gla_high(3)
            for k in range(2):
                u = Lin(U_VB + k)
                if k == 1:
                    done(u, 1)
                    high(u + 2)
                for j in range(2):
                    act.activation(s_v[:, 2 * j:2 * j + 2, k * UC:(k + 1) * UC],
                                   bank(u, j).rearrange("p (t n) -> p t n", t=2), ACT.Copy
                                   ).then_inc(drained[slot_of(u)], 1)

            for n in range(9):
                if n < 8:
                    if n >= 2:
                        act.wait_ge(q_mm, n - 1)
                    else:
                        act.wait_ge(g_ll, TT)
                    act.activation(t2[:, n % 2], (s_q, s_k)[n // 4][:, n % 4], ACT.Square).then_inc(q_sq, 1)
                if n >= 1:
                    act.wait_ge(q_var, n)
                    act.activation(mean[:], mean[:], ACT.Ln).then_inc(q_ln, 1)
                    act.wait_ge(q_ln, 2 * n - 1)
                    if n >= 2:
                        act.wait_ge(q_n, n - 1)
                    act.activation(rstd[:], mean[:], ACT.Exp, scale=-0.5).then_inc(q_ln, 1)
            ITEMS = 8 * TT
            for l in range(ITEMS + 4):
                if l < ITEMS:
                    w = P * (l % TT + 1)
                    act.wait_ge(s_negm, l + 1)
                    if l >= 3:
                        act.wait_ge(s_tr, l - 2)
                    act.activation(s_e[:, l % 3, 0:w], s_t[:, l % 2, 0:w], ACT.Exp, bias=negm[:, l % 2, 0:1],
                                   scale=0.125, accum_out=sums[:, l % 2, 0:1]).then_inc(s_exp, 1)
                if 2 <= l <= ITEMS + 1:
                    n = l - 2
                    w = P * (n % TT + 1)
                    act.wait_ge(s_tr, n + 1)
                    if n >= 2:
                        act.wait_ge(s_pv, n - 1)
                    act.activation(s_pt[:, n % 2, 0:w], ps[:, 6 + n % 2, 0:w], ACT.Copy).then_inc(s_ptr, 1)
                if l >= 11 and l % 8 == 3:
                    c = (l - 11) // 8
                    act.wait_ge(s_pv, 8 * c + 8)
                    act.activation(sh[:, c], ps[:, c % 2], ACT.Copy).then_inc(s_hh, 1)

            def gate(u, k, dst):
                done(u, 1)
                high(u + 2)
                for j in range(2):
                    act.activation(dst[:, (k * 2 + j).at(), :], ps[:, 2 * slot_of(u) + j:2 * slot_of(u) + j + 1],
                                   ACT.Sigmoid).then_inc(drained[slot_of(u)], 1)

            over(act, U_GA, 4, lambda u, k: gate(u, k, gate_a))
            over(act, U_GB, 4, lambda u, k: gate(u, k, gate_b))

            def branch(u, k):
                done(u, 1)
                high(u + 2)
                act.wait_ge(b_sum, (k + 1).v)
                act.activation(xh[:, k.at(), :], zz[:, k.base % 2:k.base % 2 + 1, :], ACT.Copy).then_inc(xh_ready, 1)

            over(act, U_BR, KC, branch)
            residual(U_OUT, 7)
            norm(7, R_GFFN)

            skip(Lin(U_RT), None)
            act.wait_ge(r_step, 8)
            act.activation(m_oh[:, 2], m_oh[:, 1], ACT.Exp).then_inc(r_act, 1)
            act.wait_ge(r_step, 22)
            act.activation(m_g[:, 7], m_g[:, 6], ACT.Exp).then_inc(r_act, 1)

            def expert(u, e):
                s, b = slot_of(u), e.base % 2
                done(u, 0)
                act.activation(f_g[:, b], bank(u, 0), ACT.Silu).then_inc(drained[s], 1)
                done(u, 1)
                high(u + 2)
                act.wait_ge(m_y, (e + 1).v)
                act.activation(ah[:, Lin(e.base % 8, e.step, e.reg).at(), :], f_y[:, b:b + 1], ACT.Copy).then_inc(m_hh, 1)

            for part in range(EXPERTS // PART_EXPERTS):
                u0, e0 = U_EX + part * (PART_EXPERTS + 4), part * PART_EXPERTS
                if part == 0:
                    for k in range(2):
                        s = (u0 + k) % 2
                        done(Lin(u0 + k), 0)
                        act.activation(f_g[:, k], ps[:, 2 * s], ACT.Silu).then_inc(drained[s], 1)
                        done(Lin(u0 + k), 1)
                        high(Lin(u0 + k + 2))
                    act.wait_ge(cw_tr, 1)
                    act.activation(m_cwt[:], ps[0:EXPERTS, 4, :], ACT.Copy).then_inc(cw_cp, 1)
                    act.wait_ge(cw_cp, 1)
                    act.dma_start(scratch, m_cwt[:]).then_inc(cw_out, 16)
                    for k in range(2):
                        act.wait_ge(m_y, k + 1)
                        act.activation(ah[:, k], f_y[:, k], ACT.Copy).then_inc(m_hh, 1)
                    over(act, u0 + 2, PART_EXPERTS - 2, lambda u, k: expert(u, k + 2), peel=0)
                else:
                    over(act, u0, PART_EXPERTS, lambda u, k: expert(u, k + e0))
                over(act, u0 + PART_EXPERTS, 4, skip)
            for c in range(KC):
                act.wait_ge(o_tr, c + 1)
                act.activation(orow[:, :, c * P:(c + 1) * P], ps[:, 4 + c % 4].rearrange("p (t n) -> p t n", t=TT),
                               ACT.Copy).then_inc(o_cp, 1)

        @block.vector
        def _(dve):
            def bank(u, j):
                return ps[:, 2 * slot_of(u) + j]

            def done(u, j):
                dve.wait_ge(chunk_done, (u * 2 + (j + 1)).v)

            def own(sem_, value):
                dve.wait_ge(sem_, value.v if isinstance(value, Lin) else value)

            dve.sem_inc(d_scored, 8)
            dve.sem_inc(l_scored, 8)
            for ahead in (d_var, d_on, al_ready, l_al):
                dve.sem_inc(ahead, 1)
            dve.memset(ones[:], 1.0).then_inc(ones_set, 1)
            dve.wait_ge(lam_in, 16)
            for n in range(2):
                dve.tensor_tensor(lamb[:, 2 * n, :], lamb[:, 2 * n, :], lamb[:, 2 * n + 1, :], ALU.mult).then_inc(lam_d, 1)
            own(lam_d, 2)
            for n in range(2):
                dve.reduce_sum(lam_s[:, n:n + 1], lamb[:, 2 * n, :], axis=AX_X).then_inc(lam_d, 1)
            dve.wait_ge(lam_x, 1)
            dve.tensor_tensor(neglam, lam_e[:, 1:2], lam_e[:, 0:1], ALU.subtract).then_inc(lam_d, 1)
            own(lam_d, 5)
            dve.tensor_scalar(neglam, neglam, LAMBDA_INIT, None, ALU.subtract).then_inc(lam_d, 1)
            for c in range(KC):
                dve.wait_ge(xh_ready, c + 1)
                dve.tensor_tensor(xl[:, c], ps[:, c % 4], xh[:, c].bitcast(F32), ALU.subtract).then_inc(xl_ready, 1)
            own(lam_d, 6)

            def diff_group(g):
                u = g * 3 + 2
                for j in range(2):
                    done(u, j)
                    dve.tensor_copy(d_v[:, 2 * j:2 * j + 2, :], bank(u, j).rearrange("p (t n) -> p t n", t=2)
                                    ).then_inc(drained[slot_of(u)], 1)
                for l in range(8 + 7):
                    if l < 8:
                        n = g * 8 + l
                        hh, i, b = l // 4, l % 4, l % 2
                        h = g * 2 + hh
                        dve.wait_ge(d_qk, (n * 2 + 2).v)
                        if i == 0:
                            dve.wait_ge(dbias_in[hh], (h.half() * 16 + 16).v)
                        dve.memset(idle, 0.0)
                        for c in range(2):
                            dve.tensor_tensor_reduce(d_t[:, b, c], ps[:, 4 + 2 * b + c],
                                                     d_bias[:, hh, ZC - P * i:ZC - P * i + T], 1.0, TAKEN,
                                                     ALU.add, ALU.max, accum_out=mx[:, b, c:c + 1]
                                                     ).then_inc(d_scored, 1)
                        own(d_scored, n * 2 + 10)
                        dve.tensor_scalar(negm[:, b, 0:2], mx[:, b, 0:2], -0.125, None, ALU.mult).then_inc(d_negm, 1)
                    if 1 <= l <= 8:
                        n = g * 8 + (l - 1)
                        b = (l - 1) % 2
                        dve.wait_ge(d_exp, (n * 2 + 2).v)
                        dve.reciprocal(rec[:, b, 0:2], sums[:, b, 0:2]).then_inc(d_rec, 1)
                        own(d_rec, n * 2 + 1)
                        dve.tensor_scalar(rec[:, b, 1:2], rec[:, b, 1:2], neglam, None, ALU.mult).then_inc(d_rec, 1)
                        e0 = d_e[:, (l - 1) % 3]
                        dve.tensor_scalar(e0, e0, rec[:, b, 0:1], None, ALU.mult).then_inc(d_half, 1)
                        own(d_rec, n * 2 + 2)
                        own(d_half, n + 1)
                        dve.scalar_tensor_tensor(out=e0, in0=d_e1[:, b], scalar=rec[:, b, 1:2], in1=e0,
                                                 op0=ALU.mult, op1=ALU.add).then_inc(d_mix, 1)
                    if l in (8, 12):
                        h = g * 2 + (l - 8) // 4
                        dve.wait_ge(d_st, (h + 1 + 1).v)
                        own(d_on, h + 1)
                        dve.tensor_scalar(mean[:], ps[:, 3], LN_EPS, None, ALU.add).then_inc(d_var, 1)
                    if l in (9, 13):
                        h = g * 2 + (l - 9) // 4
                        dve.wait_ge(d_ln, (h * 2 + 2).v)
                        dve.wait_ge(d_z, (h + 1).v)
                        dve.tensor_tensor(t2[:, 0], d_o[:], rstd[:], ALU.mult).then_inc(d_on, 1)
                    if l in (10, 14):
                        h = g * 2 + (l - 10) // 4
                        dve.wait_ge(ah_ready, (h + 1).v)
                        dve.tensor_tensor(al[:, h.at(), :], zz[:, 0:1, :], ah[:, h.at(), :].bitcast(F32),
                                          ALU.subtract).then_inc(al_ready, 1)

            with dve.Fori(0, 2) as i:
                diff_group(Lin(0, 2, i))
                diff_group(Lin(1, 2, i))

            def dil_group(g):
                for p in range(3):
                    u = g * 9 + (U_ATT[1] + 3 * p + 2)
                    for j in range(2):
                        done(u, j)
                        dve.tensor_copy(l_v[:, p, 2 * j:2 * j + 2, :], bank(u, j).rearrange("p (t n) -> p t n", t=2)
                                        ).then_inc(drained[slot_of(u)], 1)
                for l in range(16 + 4):
                    if l < 16:
                        n = g * 16 + l
                        hh, j, b = l // 4, l % 4, l % 2
                        h = g * 4 + hh
                        if j == 0:
                            dve.wait_ge(lbias_in[hh % 2], (g * 32 + (16 * (hh // 2) + 16)).v)
                        dve.wait_ge(l_qk, (n + 1).v)
                        dve.memset(idle, 0.0)
                        dve.tensor_tensor_reduce(l_t[:, b, 0:T], ps[:, 4 + 2 * b], l_bias[:, hh % 2, 3 - j:3 - j + T],
                                                 1.0, TAKEN, ALU.add, ALU.max, accum_out=mx[:, b, 0:1]
                                                 ).then_inc(l_scored, 1)
                        dve.tensor_tensor_reduce(l_t[:, b, T:768], ps[:, 5 + 2 * b, 0:256], l_bias[:, hh % 2, 515:DILW],
                                                 1.0, TAKEN, ALU.add, ALU.max, accum_out=mx[:, b, 1:2]
                                                 ).then_inc(l_scored, 1)
                        own(l_scored, n * 2 + 10)
                        dve.tensor_scalar(negm[:, b, 0:1], mx[:, b, 0:1], mx[:, b, 1:2], -0.125, ALU.max, ALU.mult
                                          ).then_inc(l_negm, 1)
                    if 1 <= l <= 16:
                        n = g * 16 + (l - 1)
                        b = (l - 1) % 2
                        dve.wait_ge(l_exp, (n + 1).v)
                        dve.reciprocal(rec[:, b, 0:1], sums[:, b, 0:1]).then_inc(l_rec, 1)
                        own(l_rec, n + 1)
                        dve.tensor_scalar(l_e[:, (l - 1) % 3], l_e[:, (l - 1) % 3], rec[:, b, 0:1], None, ALU.mult).then_inc(l_mix, 1)
                    if l in (11, 19):
                        c = g * 2 + (l - 11) // 8
                        dve.wait_ge(l_ah, (c + 1).v)
                        dve.tensor_tensor(al[:, c.at(), :].rearrange("p c (u j) -> p c j u", j=4),
                                          ps[:, 2:3].rearrange("p c (j u) -> p c j u", j=4),
                                          ah[:, c.at(), :].bitcast(F32).rearrange("p c (u j) -> p c j u", j=4),
                                          ALU.subtract).then_inc(l_al, 1)

            def update(u, k, first, n=None):
                s = slot_of(u)
                for j in range(2):
                    c = k * 2 + j
                    done(u, j)
                    xc, psum = X[:, c.at(), :], ps[:, 2 * s + j:2 * s + j + 1]
                    if first:
                        dve.scalar_tensor_tensor(out=xc, in0=xh[:, c.at(), :].bitcast(F32), scalar=ALPHA, in1=psum,
                                                 op0=ALU.mult, op1=ALU.add).then_inc(drained[s], 1)
                        own(drained[s], u.half() * 2 + (j + 1))
                        last = dve.scalar_tensor_tensor(out=xc, in0=xl[:, c.at(), :].bitcast(F32), scalar=ALPHA,
                                                        in1=xc, op0=ALU.mult, op1=ALU.add)
                        if n is not None:
                            last.then_inc(y_ready, 1)
                    else:
                        dve.tensor_tensor(xc, xc, psum, ALU.add).then_inc(drained[s], 1)
                        if n is not None:
                            own(drained[s], u.half() * 2 + (j + 1))
                            dve.sem_inc(y_ready, 1)
                    if n is not None:
                        own(y_ready, c + (KC * min(n, 6) + 1))
                        if n < 6:
                            own(acc_s_done, c + (9 * n + 1))
                            dve.tensor_tensor(acc_s[:], acc_s[:], xc, ALU.add).then_inc(acc_s_done, 1)
                        dve.wait_ge(sq_done, (c + (KC * n + 1)).v)
                        own(acc_q_done, c + (9 * n + 1))
                        dve.tensor_tensor(acc_q[:], acc_q[:], t2[:, j], ALU.add).then_inc(acc_q_done, 1)

            def clear_sums():
                dve.memset(acc_s[:], 0.0).then_inc(acc_s_done, 1)
                dve.memset(acc_q[:], 0.0).then_inc(acc_q_done, 1)

            def norm(n, rms=False, keep=False):
                event, on_act, on_dve = NORM_AT[n]
                if rms:
                    dve.wait_ge(stat_mm, n + 1)
                    dve.tensor_scalar(acc_s[:, 0], ps[:, 5], RMS_EPS, None, ALU.add).then_inc(ln_dve, 1)
                else:
                    dve.wait_ge(ln_act, on_act - 2)
                    dve.tensor_tensor(acc_q[:], mean[:], mean[:], ALU.mult).then_inc(ln_dve, 1)
                    own(ln_dve, on_dve - 2)
                    dve.scalar_tensor_tensor(out=acc_s[:, 0], in0=acc_q[:], scalar=-1.0, in1=ps[:, 5],
                                             op0=ALU.mult, op1=ALU.add).then_inc(ln_dve, 1)
                    own(ln_dve, on_dve - 1)
                    dve.tensor_scalar(acc_s[:], acc_s[:], 0.0, LN_EPS, ALU.max, ALU.add).then_inc(ln_dve, 1)
                if keep:
                    dve.memset(acc_q[:], 0.0).then_inc(acc_q_done, 1)
                dve.wait_ge(ln_act, on_act)
                for c in range(KC + 1):
                    if c < KC:
                        if c >= 2:
                            dve.wait_ge(z_ready, KC * n + c - 1)
                        if not rms:
                            dve.tensor_tensor(t2[:, c % 2], X[:, c], mean[:], ALU.subtract).then_inc(cent, 1)
                            own(cent, KC * n + c + 1)
                            dve.tensor_tensor(t2[:, c % 2], t2[:, c % 2], rstd[:], ALU.mult).then_inc(nrm, 1)
                        else:
                            dve.tensor_tensor(t2[:, c % 2], X[:, c], rstd[:], ALU.mult).then_inc(nrm, 1)
                    e = c - 1
                    if keep and e >= 0:
                        dve.wait_ge(sq_done, KC * (n + 1) + e + 1)
                        own(acc_q_done, 9 * (n + 1) + e + 1)
                        dve.tensor_tensor(acc_q[:], acc_q[:], zz[:, e % 2], ALU.add).then_inc(acc_q_done, 1)
                    elif e >= 0:
                        dve.wait_ge(xh_ready, KC * event + e + 1)
                        dve.tensor_tensor(xl[:, e], zz[:, e % 2], xh[:, e].bitcast(F32), ALU.subtract
                                          ).then_inc(xl_ready, 1)

            def after_attention(layer):
                n0 = 3 * layer
                u0 = U_WO[layer]
                clear_sums()
                for k in range(2):
                    update(Lin(u0 + k), Lin(k), True, n0)
                for b in range(4):
                    dve.wait_ge(mh_done, 4 * layer + b + 1)
                    dve.tensor_tensor(ml[:, 2 * b:2 * b + 2, :], ps[:, 4 + b].rearrange("p (k t) -> p k t", k=2),
                                      mh[:, 2 * b:2 * b + 2, :].bitcast(F32), ALU.subtract).then_inc(ml_done, 1)
                for k in range(2, 4):
                    update(Lin(u0 + k), Lin(k), True, n0)
                norm(n0)
                if layer == 1:
                    dve.wait_ge(lbias_in[0], 144)
                    dve.wait_ge(lbias_in[1], 144)
                for k in range(4):
                    u = Lin(U_MEM[layer] + 4 + k)
                    for j in range(2):
                        if j == 0:
                            done(u, 1)
                            dve.tensor_copy(x_v[:, :, k * UC:(k + 1) * UC], bank(u, 0).rearrange("p (t n) -> p t n", t=2)
                                            ).then_inc(drained[slot_of(u)], 1)
                        else:
                            dve.sem_inc(drained[slot_of(u)], 1)
                for i in range(TT + 1):
                    if i < TT:
                        n = TT * layer + i
                        dve.wait_ge(x_qk, n + 1)
                        s = 2048 + 1024 * (i % 2)
                        if n >= 2:
                            dve.wait_ge(x_exp, 4 * (n - 1))
                        dve.tensor_reduce(mx[:, i % 2, 0:4], flat[:, s:s + 1024].rearrange("p (h k) -> p h k", h=4),
                                          AX_X, ALU.max).then_inc(x_max, 1)
                        own(x_max, n + 1)
                        dve.tensor_scalar(negm[:, i % 2, 0:4], mx[:, i % 2, 0:4], -1 / 16, None, ALU.mult
                                          ).then_inc(x_negm, 1)
                    if i >= 1:
                        n = TT * layer + i - 1
                        b = (i - 1) % 2
                        dve.wait_ge(x_exp, 4 * n + 4)
                        dve.reciprocal(rec[:, b, 0:4], sums[:, b, 0:4]).then_inc(x_rec, 1)
                        own(x_rec, n + 1)
                        for h in range(4):
                            dve.tensor_scalar(x_e[:, b, h * M:(h + 1) * M], x_e[:, b, h * M:(h + 1) * M],
                                              rec[:, b, h:h + 1], None, ALU.mult).then_inc(x_mix, 1)
                for c in range(KC):
                    dve.wait_ge(x_ah, KC * layer + c + 1)
                    dve.tensor_tensor(al[:, c], ps[:, 4 + c % 4], ah[:, c].bitcast(F32), ALU.subtract).then_inc(x_al, 1)
                clear_sums()
                over(dve, U_MO[layer], 4, lambda u, k: update(u, k, True, n0 + 1))
                norm(n0 + 1)
                u0, f0 = U_FF[layer], 0
                for part, width in enumerate(HIDDEN_PARTS):
                    def hidden(u, k):
                        F = k + (FF // P * layer + f0)
                        s, b = slot_of(u), k.base % 2
                        w0 = par[:, 1 + layer, bass.ds((k + f0).v, 1)]
                        w2 = par[:, 1 + layer, bass.ds((k + (2 * (FF // P) + f0)).v, 1)]
                        dve.wait_ge(f_cd, (F + 1).v)
                        dve.scalar_tensor_tensor(out=f_c[:, b, 1:T], in0=bank(u, 0)[:, 0:T - 1], scalar=w0,
                                                 in1=f_c[:, b, 1:T], op0=ALU.mult, op1=ALU.add).then_inc(f_left, 1)
                        own(f_left, F + 1)
                        dve.scalar_tensor_tensor(out=f_c[:, b, 0:T - 1], in0=bank(u, 0)[:, 1:T], scalar=w2,
                                                 in1=f_c[:, b, 0:T - 1], op0=ALU.mult, op1=ALU.add
                                                 ).then_inc(drained[s], 1)
                        done(u, 1)
                        dve.wait_ge(f_gd, (F + 1).v)
                        dve.tensor_tensor(f_y[:, b], f_g[:, b], bank(u, 1), ALU.mult).then_inc(drained[s], 1)
                        dve.wait_ge(f_hh, (F + 1).v)
                        dve.tensor_tensor(al[:, k.at(), :], f_y[:, b:b + 1], ah[:, k.at(), :].bitcast(F32), ALU.subtract
                                          ).then_inc(f_hl, 1)
                    over(dve, u0, width, hidden)
                    if part == 2:
                        clear_sums()
                    over(dve, u0 + width, 4, lambda u, k: update(u, k, part == 0, n0 + 2 if part == 2 else None))
                    u0, f0 = u0 + width + 4, f0 + width
                norm(n0 + 2, keep=layer == 1)

            after_attention(0)
            with dve.Fori(0, 2) as i:
                dil_group(Lin(0, 2, i))
                dil_group(Lin(1, 2, i))
            after_attention(1)

            norm(6, rms=True)
            dve.memset(i_m[:, 0, 0:P], 0.0).then_inc(i_edge, 1)
            own(i_edge, 1)
            dve.memset(i_m[0:64, 0, 64:P], MASKED).then_inc(i_edge, 1)
            dve.wait_ge(wi_s, 1)
            for m in range(8 * (TT - 1)):
                i, h = m // 8 + 1, m % 8
                w = P * (i + 1)
                dve.wait_ge(i_relu, m + 1)
                if h == 0:
                    dve.tensor_scalar(i_m[:, i, 0:w], i_r[:, m % 2, 0:w], wi_row[:, i, h:h + 1], None, ALU.mult
                                      ).then_inc(i_acc, 1)
                else:
                    own(i_acc, m)
                    dve.scalar_tensor_tensor(out=i_m[:, i, 0:w], in0=i_r[:, m % 2, 0:w], scalar=wi_row[:, i, h:h + 1],
                                             in1=i_m[:, i, 0:w], op0=ALU.mult, op1=ALU.add).then_inc(i_acc, 1)
                if h == 7:
                    own(i_acc, m + 1)
                    dve.memset(i_m[0:64, i, w - 64:w], MASKED).then_inc(i_edge, 1)
            ROUNDS = TOPK // 8
            own(i_edge, 2)
            dve.tensor_copy(idle, ones[:, 0:1]).then_inc(i_mask, 1)
            for i in range(1, TT):
                w = P * (i + 1)
                row = i_m[:, i, 0:w]
                own(i_edge, i + 2)
                for r in range(ROUNDS):
                    n = (i - 1) * ROUNDS + r
                    own(i_cut, n)
                    dve.max(m8, row).then_inc(i_max, 1)
                    own(i_max, n + 1)
                    dve.match_replace(row, m8, row, TAKEN).then_inc(i_cut, 1)
                own(i_cut, i * ROUNDS)
                dve.tensor_scalar(row, row, -2e38, MASKED, ALU.is_gt, ALU.mult).then_inc(i_mask, 1)

            for j in range(2):
                dve.wait_ge(g_abs, 5 + j)
                dve.scalar_tensor_tensor(out=g_a[:, 2 * j:2 * j + 2, :], in0=ps[:, 4 + j].rearrange("p (t n) -> p t n", t=2),
                                         scalar=0.0, in1=g_d[:, 2 * j:2 * j + 2, :], op0=ALU.min, op1=ALU.subtract
                                         ).then_inc(g_la, 1)
            for j in range(2):
                dve.wait_ge(g_ex, j + 1)
                half = slice(2 * j, 2 * j + 2)
                dve.tensor_tensor(g_d[:, half, :], g_d[:, half, :], g_k[:, half, :], ALU.mult).then_inc(g_kd, 1)
            dve.wait_ge(g_ex, 4)
            for p in range(2):
                dve.wait_ge(g_u, p + 1)
                for c in range(8):
                    gain = ps[:, 4 + 2 * p + c % 2, c // 2 * P:(c // 2 + 1) * P]
                    if c == 0:
                        dve.tensor_copy(g_st[:, p, 0], gain).then_inc(g_state, 1)
                    else:
                        own(g_state, 8 * p + c)
                        dve.scalar_tensor_tensor(out=g_st[:, p, c], in0=g_st[:, p, c - 1],
                                                 scalar=g_dec[:, c % 2, p * 4 + c // 2:p * 4 + c // 2 + 1], in1=gain,
                                                 op0=ALU.mult, op1=ALU.add).then_inc(g_state, 1)

            def gla_var(h):
                dve.wait_ge(g_st_mm, h + 1)
                if h >= 1:
                    dve.wait_ge(g_ln, 2 * h)
                dve.tensor_scalar(mean[:], ps[:, 4 + h], RMS_EPS, None, ALU.add).then_inc(g_var, 1)

            def gla_scale(h):
                dve.wait_ge(g_ln, 2 * h + 2)
                z = zz[:, h % 2]
                dve.tensor_tensor(z, z, rstd[:], ALU.mult).then_inc(g_n, 1)
                own(g_n, h + 1)
                dve.scalar_tensor_tensor(out=z, in0=z, scalar=par[:, 0, R_GGLA:R_GGLA + 1], in1=g_r[:, h],
                                         op0=ALU.mult, op1=ALU.mult).then_inc(g_y, 1)

            def gla_low(h):
                dve.wait_ge(g_hh, h + 1)
                dve.tensor_tensor(gl[:, h], zz[:, h % 2], gh[:, h].bitcast(F32), ALU.subtract).then_inc(g_ll, 1)

            for first in (0, 2):
                for h in (first, first + 1):
                    gla_var(h)
                    gla_scale(h)
                gla_low(first)
                gla_low(first + 1)

            for n in range(8):
                dve.wait_ge(q_mm, n + 1)
                if n >= 1:
                    dve.wait_ge(q_ln, 2 * n)
                dve.tensor_scalar(mean[:], ps[:, 4 + n % 4], RMS_EPS, None, ALU.add).then_inc(q_var, 1)
                dve.wait_ge(q_ln, 2 * n + 2)
                x, row = ((s_q, R_GQ), (s_k, R_GK))[n // 4]
                dve.scalar_tensor_tensor(out=x[:, n % 4], in0=x[:, n % 4], scalar=par[:, 0, row:row + 1], in1=rstd[:],
                                         op0=ALU.mult, op1=ALU.mult).then_inc(q_n, 1)
            ITEMS = 8 * TT
            for l in range(ITEMS + 5):
                if l < ITEMS:
                    b, w = l % 2, P * (l % TT + 1)
                    dve.wait_ge(s_qk, l + 1)
                    dve.wait_ge(s_bm, l + 1)
                    if l >= 2:
                        dve.wait_ge(s_exp, l - 1)
                    dve.memset(idle, 0.0)
                    dve.tensor_tensor_reduce(s_t[:, b, 0:w], ps[:, 4 + b, 0:w], s_b[:, b, 0:w], 1.0, TAKEN, ALU.add,
                                             ALU.max, accum_out=mx[:, b, 0:1]).then_inc(s_scored, 1)
                    own(s_scored, l + 1)
                    dve.tensor_scalar(negm[:, b, 0:1], mx[:, b, 0:1], -0.125, None, ALU.mult).then_inc(s_negm, 1)
                if 1 <= l <= ITEMS:
                    n = l - 1
                    b, w = n % 2, P * (n % TT + 1)
                    dve.wait_ge(s_exp, n + 1)
                    dve.reciprocal(rec[:, b, 0:1], sums[:, b, 0:1]).then_inc(s_rec, 1)
                    own(s_rec, n + 1)
                    dve.tensor_scalar(s_e[:, n % 3, 0:w], s_e[:, n % 3, 0:w], rec[:, b, 0:1], None, ALU.mult).then_inc(s_mix, 1)
                if l >= 12 and l % 8 == 4:
                    c = (l - 12) // 8
                    dve.wait_ge(s_hh, c + 1)
                    dve.tensor_tensor(sl[:, c], ps[:, c % 2], sh[:, c].bitcast(F32), ALU.subtract).then_inc(s_ll, 1)

            def branch(u, k):
                s, b = slot_of(u), k.base % 2
                for j in range(2):
                    done(u, j)
                    dve.tensor_tensor(t2[:, j:j + 1], (gate_a, gate_b)[j][:, k.at(), :],
                                      ps[:, 2 * s + j:2 * s + j + 1], ALU.mult).then_inc(drained[s], 1)
                own(drained[s], u.half() * 2 + 2)
                dve.tensor_tensor(zz[:, b], t2[:, 0], t2[:, 1], ALU.add).then_inc(b_sum, 1)
                dve.wait_ge(xh_ready, (k + (KC * MIXED + 1)).v)
                dve.tensor_tensor(xl[:, k.at(), :], zz[:, b:b + 1], xh[:, k.at(), :].bitcast(F32), ALU.subtract
                                  ).then_inc(xl_ready, 1)

            over(dve, U_BR, KC, branch)
            dve.memset(acc_q[:], 0.0).then_inc(acc_q_done, 1)
            over(dve, U_OUT, 4, lambda u, k: update(u, k, False, 7))
            norm(7, rms=True)

            dve.wait_ge(rb_in, 32)
            for t in range(TT):
                done(Lin(U_RT), t // 2)
                add = dve.tensor_tensor(m_lg[:, t], bank(Lin(U_RT), t // 2)[:, (t % 2) * UC:(t % 2) * UC + 36], m_rb[:],
                                        ALU.add)
                if t % 2:
                    add.then_inc(drained[U_RT % 2], 1)
                else:
                    add.then_inc(r_step, 1)
            own(drained[U_RT % 2], U_RT + 2)
            own(r_step, 2)
            idx = idx8.rearrange("p (t n) -> p t n", n=PER_GROUP)[:, 0:TT, :]
            groups = m_lg[:, :, EXPERTS:36]

            def over_last(x, n):
                return x.unsqueeze(2).to_broadcast([P, TT, n])

            def first_of(value, hot, best, low, n, at_step):
                own(r_step, at_step)
                dve.tensor_reduce(best, value, AX_X, ALU.max).then_inc(r_step, 1)
                own(r_step, at_step + 1)
                dve.tensor_tensor(hot, value, over_last(best, n), ALU.is_equal).then_inc(r_step, 1)
                own(r_step, at_step + 2)
                dve.scalar_tensor_tensor(out=hot, in0=hot, scalar=-64.0, in1=idx[:, :, 0:n], op0=ALU.mult, op1=ALU.add
                                         ).then_inc(r_step, 1)
                own(r_step, at_step + 3)
                dve.tensor_reduce(low, hot, AX_X, ALU.min).then_inc(r_step, 1)
                own(r_step, at_step + 4)
                dve.tensor_tensor(hot, hot, over_last(low, n), ALU.is_equal).then_inc(r_step, 1)

            g_hot = m_oh[:, 0]
            first_of(groups, g_hot, m_g[:, 0], m_g[:, 1], GROUPS, 2)
            own(r_step, 7)
            dve.tensor_tensor(m_oh[:, 1], groups, over_last(m_g[:, 0], GROUPS), ALU.subtract).then_inc(r_step, 1)
            logits = m_lg[:, :, 0:EXPERTS].rearrange("p t (g e) -> p t g e", g=GROUPS)
            hot4 = g_hot.unsqueeze(3).to_broadcast([P, TT, GROUPS, PER_GROUP])
            dve.tensor_tensor(m_tmp[:, 0], logits, hot4, ALU.mult).then_inc(r_step, 1)
            own(r_step, 9)
            dve.tensor_reduce(m_e[:, 0], m_tmp[:, 0].rearrange("p t g e -> p t e g"), AX_X, ALU.add).then_inc(r_step, 1)
            first_of(m_e[:, 0], m_e[:, 1], m_g[:, 4], m_g[:, 1], PER_GROUP, 10)
            own(r_step, 15)
            dve.scalar_tensor_tensor(out=m_e[:, 2], in0=m_e[:, 1], scalar=TAKEN, in1=m_e[:, 0], op0=ALU.mult, op1=ALU.add
                                     ).then_inc(r_step, 1)
            first_of(m_e[:, 2], m_e[:, 3], m_g[:, 5], m_g[:, 1], PER_GROUP, 16)
            own(r_step, 21)
            dve.tensor_tensor(m_g[:, 6], m_g[:, 5], m_g[:, 4], ALU.subtract).then_inc(r_step, 1)
            dve.wait_ge(r_act, 1)
            dve.tensor_reduce(m_g[:, 2], m_oh[:, 2], AX_X, ALU.add).then_inc(r_step, 1)
            own(r_step, 23)
            dve.reciprocal(m_g[:, 3], m_g[:, 2]).then_inc(r_step, 1)
            dve.wait_ge(r_act, 2)
            dve.tensor_scalar(m_g[:, 8], m_g[:, 7], 1.0, None, ALU.add).then_inc(r_step, 1)
            own(r_step, 25)
            dve.reciprocal(m_g[:, 9], m_g[:, 8]).then_inc(r_step, 1)
            own(r_step, 26)
            dve.tensor_tensor(m_g[:, 10], m_g[:, 9], m_g[:, 3], ALU.mult).then_inc(r_step, 1)
            own(r_step, 27)
            dve.tensor_tensor(m_g[:, 11], m_g[:, 10], m_g[:, 7], ALU.mult).then_inc(r_step, 1)
            own(r_step, 28)
            for n, share in ((1, 10), (3, 11)):
                dve.tensor_tensor(m_e[:, n], m_e[:, n], over_last(m_g[:, share], PER_GROUP), ALU.mult).then_inc(r_step, 1)
            own(r_step, 30)
            dve.tensor_tensor(m_e[:, 4], m_e[:, 1], m_e[:, 3], ALU.add).then_inc(r_step, 1)
            own(r_step, 31)
            dve.tensor_tensor(m_cw[:], hot4, m_e[:, 4].unsqueeze(2).to_broadcast([P, TT, GROUPS, PER_GROUP]), ALU.mult
                              ).then_inc(r_step, 1)

            def expert_product(u, e):
                s, b = slot_of(u), e.base % 2
                dve.wait_ge(drained[s], (u.half() * 2 + 1).v)
                done(u, 1)
                if e.base >= 2:
                    own(m_hl, e + -1)
                dve.tensor_tensor(f_y[:, b], f_g[:, b], bank(u, 1), ALU.mult).then_inc(drained[s], 1)

            def expert_weight(u, e):
                s, b = slot_of(u), e.base % 2
                own(drained[s], u.half() * 2 + 2)
                dve.wait_ge(mw_in[b], (e.half() * 16 + 16).v)
                dve.tensor_tensor(f_y[:, b], f_y[:, b], m_w[:, b], ALU.mult).then_inc(m_y, 1)

            def expert_low(e):
                b = e.base % 2
                k = Lin(e.base % 8, e.step, e.reg)
                dve.wait_ge(m_hh, (e + 1).v)
                dve.tensor_tensor(al[:, k.at(), :], f_y[:, b:b + 1], ah[:, k.at(), :].bitcast(F32), ALU.subtract
                                  ).then_inc(m_hl, 1)

            def expert(u, e):
                expert_product(u, e)
                expert_weight(u, e)
                expert_low(e)

            for part in range(EXPERTS // PART_EXPERTS):
                u0, e0 = U_EX + part * (PART_EXPERTS + 4), part * PART_EXPERTS
                if part == 0:
                    for k in range(2):
                        expert_product(Lin(u0 + k), Lin(k))
                    for k in range(2):
                        expert_weight(Lin(u0 + k), Lin(k))
                    for k in range(2):
                        expert_low(Lin(k))
                    over(dve, u0 + 2, PART_EXPERTS - 2, lambda u, k: expert(u, k + 2), peel=0)
                else:
                    over(dve, u0, PART_EXPERTS, lambda u, k: expert(u, k + e0))
                over(dve, u0 + PART_EXPERTS, 4, lambda u, k: update(u, k, False))

        @block.tensor
        def _(pe):
            def begin(u):
                s = slot_of(u)
                pe.wait_ge(lo_done, (u + 1).v)
                if u.base >= 2:
                    pe.wait_ge(drained[s], (u.half() * 2).v)
                return s

            def triple(dst, stat_h, stat_l, mov_h, mov_l, first, last):
                pe.matmul(dst, stat_h, mov_h, start=first, stop=False)
                pe.matmul(dst, stat_l, mov_h, start=False, stop=False)
                return pe.matmul(dst, stat_h, mov_l, start=False, stop=last)

            def columns(u, hi, lo, kcs=KC, width=T, ready=None, count=2, k0=(0, 0), passes=None):
                s = begin(u)
                for j in range(count):
                    for kc in range(kcs):
                        if ready and j == 0:
                            ready(kc)
                        cols = slice(j * P, (j + 1) * P)
                        mm = triple(ps[:, 2 * s + j, 0:width], wh[:, s, kc, cols], wl[:, s, kc, cols],
                                    hi[:, kc], lo[:, kc], kc == 0, kc == kcs - 1)
                    mm.then_inc(chunk_done, 1)

            def rows(u, hi, lo, tiles=TT, n=UC, take=None):
                s = begin(u)
                take = take or (lambda x, kc, t: x[:, kc, t * P:(t + 1) * P])
                for t in range(tiles):
                    for kc in range(KC):
                        mm = triple(ps[:, 2 * s + t // 2, (t % 2) * UC:(t % 2) * UC + n],
                                    take(hi, kc, t), take(lo, kc, t), wh[:, s, kc, 0:n], wl[:, s, kc, 0:n],
                                    kc == 0, kc == KC - 1)
                    if t % 2 or tiles == 2:
                        mm.then_inc(chunk_done, 1)

            pe.sem_inc(d_tr, 2)
            pe.sem_inc(l_tr, 2)
            pe.sem_inc(d_pv, 2)
            pe.sem_inc(d_st, 1)
            pe.sem_inc(l_pv, 1)
            pe.wait_ge(x_in, 32)
            for c in range(KC):
                if c >= 4:
                    pe.wait_ge(xl_ready, c - 3)
                for t in range(TT):
                    tr = pe.transpose(ps[:, c % 4, t * P:(t + 1) * P], xrows[:, t, c * P:(c + 1) * P], ident)
                tr.then_inc(xt_done, 1)
            pe.wait_ge(p_in, 16 * 14)
            pe.transpose(ps[:, 4, 0:R_GK + 1], prow[0:R_GK + 1, 0, :], ident[0:R_GK + 1, 0:R_GK + 1])
            pe.transpose(ps[:, 4, P:P + 88], prow[0:88, 1, :], ident[0:88, 0:88])
            pe.transpose(ps[:, 4, 2 * P:2 * P + 88], prow[0:88, 2, :], ident[0:88, 0:88]).then_inc(par_t, 1)
            pe.wait_ge(z_in, 32)
            for j in range(2):
                pe.matmul(ps[0:8, 5 + j, :], relb[:], hot[:, j * T:(j + 1) * T], start=True, stop=True).then_inc(z_mm, 1)
            pe.wait_ge(par_s, 3)
            pe.wait_ge(z_cp, 2)
            pe.wait_ge(xl_ready, KC)

            def split_ready(event):
                return lambda kc: pe.wait_ge(xl_ready, KC * event + kc + 1)

            def diff_group(g, first):
                u = g * 3
                s = slot_of(u)
                pe.wait_ge(d_ptr, (g * 8 + 1).v)
                pe.wait_ge(d_var, (g * 2 + 1).v)
                columns(u, xh, xl, ready=first)
                columns(u + 1, xh, xl)
                rows(u + 2, xh, xl)
                emptied(pe, u + 1)
                emptied(pe, u + 2)
                for l in range(8 + 4):
                    if l < 8:
                        n = g * 8 + l
                        hh, i, b = l // 4, l % 4, l % 2
                        pe.wait_ge(d_scored, (n * 2 + 6).v)
                        for c in range(2):
                            half = slice(64 * c, 64 * c + 64)
                            pe.matmul(ps[:, 4 + 2 * b + c], d_q[half, hh, i * P:(i + 1) * P], d_k[half, hh, :],
                                      start=True, stop=True).then_inc(d_qk, 1)
                    if 2 <= l <= 9:
                        n = g * 8 + (l - 2)
                        b = l % 2
                        pe.wait_ge(d_mix, (n + 1).v)
                        if l >= 4:
                            pe.wait_ge(d_ptr, (n + -1 + 1).v)
                        for k in range(TT):
                            tr = pe.transpose(ps[:, b, k * P:(k + 1) * P], d_e[:, (l - 2) % 3, k * P:(k + 1) * P], ident)
                        tr.then_inc(d_tr, 1)
                    if l in (6, 10):
                        hh = (l - 6) // 4
                        h = g * 2 + hh
                        pe.wait_ge(d_ptr, (h * 4 + 4 + 1).v)
                        pe.wait_ge(d_osb, (h * 2 + 1).v)
                        for k in range(TT):
                            mm = pe.matmul(ps[:, 2], d_v[:, k, hh * P:(hh + 1) * P], d_pt[:, hh, k, :],
                                           start=k == 0, stop=k == TT - 1)
                        mm.then_inc(d_pv, 1)
                    if l in (7, 11):
                        h = g * 2 + (l - 7) // 4
                        pe.wait_ge(d_osb, (h * 2 + 2 + 1).v)
                        pe.wait_ge(d_var, (h + 1).v)
                        pe.matmul(ps[:, 3], mean_p, d_sq[:], start=True, stop=True).then_inc(d_st, 1)

            with pe.Fori(0, 2) as i:
                diff_group(Lin(0, 2, i), split_ready(0))
                diff_group(Lin(1, 2, i), None)

            def dil_group(g, first):
                pe.wait_ge(l_ptr, (g * 16 + 1).v)
                pe.wait_ge(l_al, (g * 2 + 1).v)
                for p in range(3):
                    u = g * 9 + (U_ATT[1] + 3 * p)
                    columns(u, xh, xl, ready=first if p == 0 else None)
                    columns(u + 1, xh, xl)
                    rows(u + 2, xh, xl, take=None if p == 0 else
                         lambda x, kc, t: x[:, kc, :].rearrange("p (u j) -> p j u", j=4)[:, t])
                emptied(pe, u + 1)
                emptied(pe, u + 2)

                def of_class(x, p, pb, ch, j):
                    return x[pb:pb + 64, p, ch, :].rearrange("p (u j) -> p j u", j=4)[:, j]

                for l in range(16 + 3):
                    if l < 16:
                        n = g * 16 + l
                        hh, j, b = l // 4, l % 4, l % 2
                        pb, ch = 64 * (hh % 2), hh // 2
                        pe.wait_ge(l_scored, (n * 2 + 6).v)
                        pe.matmul(ps[:, 4 + 2 * b], of_class(l_q, 0, pb, ch, j), l_k[pb:pb + 64, 0, ch, :],
                                  start=True, stop=True)
                        for p in (1, 2):
                            mm = pe.matmul(ps[:, 5 + 2 * b, (p - 1) * P:p * P], of_class(l_q, p, pb, ch, j),
                                           of_class(l_k, p, pb, ch, j), start=True, stop=True)
                        mm.then_inc(l_qk, 1)
                    if 2 <= l <= 17:
                        n = g * 16 + (l - 2)
                        pe.wait_ge(l_mix, (n + 1).v)
                        if l >= 3:
                            pe.wait_ge(l_ptr, (n + 1).v)
                        for k in range(6):
                            tr = pe.transpose(ps[:, k // 4, (k % 4) * P:(k % 4 + 1) * P],
                                              l_e[:, (l - 2) % 3, k * P:(k + 1) * P], ident)
                        tr.then_inc(l_tr, 1)
                    if l >= 6 and l % 4 == 2:
                        hh = (l - 6) // 4
                        pb = 64 * (hh % 2)
                        pe.wait_ge(l_ptr, (g * 16 + (hh * 4 + 4) + 1).v)
                        if hh == 2:
                            pe.wait_ge(l_al, (g * 2 + 1 + 1).v)
                        cols = slice(64 * hh, 64 * hh + 64)
                        for k in range(TT):
                            pe.matmul(ps[pb:pb + 64, 2, :], l_v[:, 0, k, cols], l_pt[:, k, :], start=k == 0, stop=False)
                        for p in (1, 2):
                            for j in range(4):
                                mm = pe.matmul(ps[pb:pb + 64, 2, j * P:(j + 1) * P], l_v[:, p, j, cols],
                                               l_pt[:, 3 + p, j * P:(j + 1) * P], start=False, stop=p == 2 and j == 3)
                        mm.then_inc(l_pv, 1)

            def stats(n):
                pe.wait_ge(acc_s_done, 9 * n + 9)
                pe.matmul(ps[:, 4], mean_d, acc_s[:, 0], start=True, stop=True)
                pe.wait_ge(acc_q_done, 9 * n + 9)
                pe.matmul(ps[:, 5], mean_d, acc_q[:], start=True, stop=True).then_inc(stat_mm, 1)

            def after_attention(layer):
                n0 = 3 * layer
                u0 = U_WO[layer]
                got = (al_ready, l_al)[layer]
                columns(Lin(u0), ah, al, ready=lambda kc: pe.wait_ge(got, kc + 2))
                columns(Lin(u0 + 1), ah, al)
                pe.wait_ge(m_in, 16 * (layer + 1))
                for b in range(4):
                    for k in range(2):
                        for t in range(2):
                            tr = pe.transpose(ps[:, 4 + b, k * M + t * P:k * M + (t + 1) * P],
                                              mrows[:, t, (2 * b + k) * P:(2 * b + k + 1) * P], ident)
                    tr.then_inc(mt_done, 1)
                columns(Lin(u0 + 2), ah, al)
                columns(Lin(u0 + 3), ah, al)
                pe.wait_ge(ml_done, 4 * (layer + 1))
                stats(n0)
                for k in range(4):
                    columns(Lin(U_MEM[layer] + k), mh, ml, width=M)
                for k in range(4):
                    rows(Lin(U_MEM[layer] + 4 + k), mh, ml, tiles=2)
                first = split_ready(n0 + 1)
                over(pe, U_MQ[layer], 4, lambda u, k: columns(u, xh, xl, ready=first if k.base == 0 else None))
                emptied(pe, Lin(U_MQ[layer] + 2))
                emptied(pe, Lin(U_MQ[layer] + 3))
                for i in range(TT + 1):
                    if i < TT:
                        n = TT * layer + i
                        if i >= 2:
                            pe.wait_ge(x_exp, 4 * (n - 1))
                        for h in range(4):
                            for e in range(2):
                                mm = pe.matmul(ps[:, 4 + 2 * (i % 2) + h // 2, (h % 2) * M:(h % 2 + 1) * M],
                                               x_q[:, 2 * h + e, i * P:(i + 1) * P], x_k[:, 2 * h + e, :],
                                               start=e == 0, stop=e == 1)
                        mm.then_inc(x_qk, 1)
                    if i >= 1:
                        n = TT * layer + i - 1
                        b = (i - 1) % 2
                        pe.wait_ge(x_mix, 4 * n + 4)
                        if i >= 3:
                            pe.wait_ge(x_ptr, n - 1)
                        for k in range(8):
                            tr = pe.transpose(ps[:, 2 * b + k // 4, (k % 4) * P:(k % 4 + 1) * P],
                                              x_e[:, b, k * P:(k + 1) * P], ident)
                        tr.then_inc(x_tr, 1)
                pe.wait_ge(x_ptr, TT * (layer + 1))
                for c in range(KC):
                    if c >= 4:
                        pe.wait_ge(x_al, KC * layer + c - 3)
                    for k in range(2):
                        mm = pe.matmul(ps[:, 4 + c % 4], x_v[:, k, c * P:(c + 1) * P], x_pt[:, 2 * (c // 2) + k, :],
                                       start=k == 0, stop=k == 1)
                    mm.then_inc(x_pv, 1)
                over(pe, U_MO[layer], 4, lambda u, k: columns(
                    u, ah, al, ready=(lambda kc: pe.wait_ge(x_al, KC * layer + kc + 1)) if k.base == 0 else None))
                stats(n0 + 1)
                u0, f0 = U_FF[layer], FF // P * layer
                for part, width in enumerate(HIDDEN_PARTS):
                    first = split_ready(n0 + 2) if part == 0 else None
                    over(pe, u0, width, lambda u, k: columns(u, xh, xl, ready=first if k.base == 0 else None))
                    over(pe, u0 + width, 4, lambda u, k: columns(
                        u, ah, al, kcs=width,
                        ready=(lambda kc: pe.wait_ge(f_hl, f0 + kc + 1)) if k.base == 0 else None))
                    u0, f0 = u0 + width + 4, f0 + width
                stats(n0 + 2)

            after_attention(0)
            with pe.Fori(0, 2) as i:
                dil_group(Lin(0, 2, i), split_ready(3))
                dil_group(Lin(1, 2, i), None)
            after_attention(1)

            def square_stats(n):
                pe.wait_ge(acc_q_done, 9 * n + 9)
                pe.matmul(ps[:, 5], mean_d, acc_q[:], start=True, stop=True).then_inc(stat_mm, 1)

            square_stats(6)
            columns(Lin(U_QI), xh, xl, ready=split_ready(6))
            columns(Lin(U_SM), xh, xl, count=1)
            pe.wait_ge(sm_done, 1)
            pe.matmul(ps[:, 2 * (U_SM % 2) + 1], rep32[0:32, :], sm_t[0:32, :], start=True, stop=True
                      ).then_inc(chunk_done, 1)
            for t in range(TT):
                tr = pe.transpose(ps[:, 4, t * 8:(t + 1) * 8], sm_t[32:40, t * P:(t + 1) * P], ident[32:40, 32:40])
            tr.then_inc(wi_tr, 1)
            pe.wait_ge(wi_s, 1)
            for m in range(8 * (TT - 1)):
                i, h = m // 8 + 1, m % 8
                rows_ = slice(32 * (h % 4), 32 * (h % 4) + 32)
                if m >= 4:
                    pe.wait_ge(i_relu, m - 3)
                pe.matmul(ps[:, 4 + m % 4, 0:P * (i + 1)], i_q[rows_, h // 4, i * P:(i + 1) * P],
                          i_k[rows_, 0:P * (i + 1)], start=True, stop=True).then_inc(i_qk, 1)
            columns(Lin(U_QA), xh, xl)
            rows(Lin(U_KA), xh, xl)
            for k in range(2):
                rows(Lin(U_VA + k), xh, xl)
            for k in range(2):
                columns(Lin(U_RA + k), xh, xl)
            pe.wait_ge(i_relu, 8 * (TT - 1))
            pe.wait_ge(wa_in, 48)
            for t in range(TT):
                mm = pe.matmul(ps[:, 4 + t // 2, (t % 2) * UC:(t % 2 + 1) * UC], sm_t[64:81, t * P:(t + 1) * P],
                               walpha[64:81, :], start=True, stop=True)
                if t % 2:
                    mm.then_inc(g_z, 1)
            columns(Lin(U_QB), xh, xl)
            for t in range(TT):
                pe.wait_ge(g_la, t // 2 + 1)
                mm = pe.matmul(ps[:, 6 + t // 2, (t % 2) * UC:(t % 2 + 1) * UC], later, g_a[:, t, :],
                               start=True, stop=True)
                if t % 2:
                    mm.then_inc(g_lat, 1)
            for b in range(2):
                for p in range(2):
                    for ch in range(TT):
                        part = slice(64 * b, 64 * b + 64)
                        mm = pe.matmul(ps[:, 4 + b, p * 4 + ch:p * 4 + ch + 1], g_a[part, ch, p * P:(p + 1) * P],
                                       ones[part, 0:1], start=True, stop=True)
            mm.then_inc(g_tot, 1)
            columns(Lin(U_QB + 1), xh, xl)
            pe.wait_ge(g_kd, 2)
            pe.wait_ge(g_ex, 4)
            for p in range(2):
                for h in (2 * p, 2 * p + 1):
                    for c in range(8):
                        part = slice(64 * (c % 2), 64 * (c % 2) + 64)
                        mm = pe.matmul(ps[64 * (h % 2):64 * (h % 2) + 64, 4 + 2 * p + c % 2, c // 2 * P:(c // 2 + 1) * P],
                                       g_d[part, c // 2, 64 * h:64 * h + 64], g_v[part, c // 2, P * h:P * (h + 1)],
                                       start=True, stop=True)
                mm.then_inc(g_u, 1)
            columns(Lin(U_KB), xh, xl)
            pe.wait_ge(g_state, 16)
            for h in range(TT):
                part = slice(64 * (h % 2), 64 * (h % 2) + 64)
                for c in range(8):
                    mm = pe.matmul(ps[:, 4 + h, 64 * c:64 * (c + 1)], g_st[part, h // 2, c, :],
                                   g_q[part, h // 2, 64 * c:64 * (c + 1)], start=True, stop=True)
                mm.then_inc(g_o, 1)

            def gla_stats(h):
                pe.wait_ge(g_sq, 2 * h + 2)
                pe.matmul(ps[:, 4 + h], mean_p, t2[:, h % 2], start=True, stop=True).then_inc(g_st_mm, 1)

            columns(Lin(U_KB + 1), xh, xl)
            gla_stats(0)
            gla_stats(1)
            rows(Lin(U_VB), xh, xl)
            gla_stats(2)
            gla_stats(3)
            rows(Lin(U_VB + 1), xh, xl)

            for n in range(8):
                pe.wait_ge(q_sq, n + 1)
                if n < 4:
                    pe.wait_ge(g_var, n + 1)
                else:
                    pe.wait_ge(q_var, n - 3)
                pe.matmul(ps[:, 4 + n % 4], half_mean, t2[:, n % 2], start=True, stop=True).then_inc(q_mm, 1)
            emptied(pe, Lin(U_VB))
            emptied(pe, Lin(U_VB + 1))
            pe.wait_ge(q_n, 8)
            ITEMS = 8 * TT
            for l in range(ITEMS + 3):
                if l < ITEMS:
                    h, i = l // TT, l % TT
                    part = slice(64 * (h % 2), 64 * (h % 2) + 64)
                    if l >= 2:
                        pe.wait_ge(s_scored, l - 1)
                    pe.matmul(ps[:, 4 + l % 2, 0:P * (i + 1)], s_q[part, h // 2, i * P:(i + 1) * P],
                              s_k[part, h // 2, 0:P * (i + 1)], start=True, stop=True).then_inc(s_qk, 1)
                if 2 <= l <= ITEMS + 1:
                    n = l - 2
                    pe.wait_ge(s_mix, n + 1)
                    if n >= 2:
                        pe.wait_ge(s_ptr, n - 1)
                    for k in range(n % TT + 1):
                        tr = pe.transpose(ps[:, 6 + n % 2, k * P:(k + 1) * P], s_e[:, n % 3, k * P:(k + 1) * P], ident)
                    tr.then_inc(s_tr, 1)
                if l >= 3:
                    n = l - 3
                    h, i = n // TT, n % TT
                    pe.wait_ge(s_ptr, n + 1)
                    if h >= 4 and h % 2 == 0 and i == 0:
                        pe.wait_ge(s_ll, h // 2 - 1)
                    for k in range(i + 1):
                        mm = pe.matmul(ps[64 * (h % 2):64 * (h % 2) + 64, (h // 2) % 2, i * P:(i + 1) * P],
                                       s_v[:, k, 64 * h:64 * h + 64], s_pt[:, n % 2, k * P:(k + 1) * P],
                                       start=k == 0, stop=k == i)
                    mm.then_inc(s_pv, 1)
            pe.wait_ge(s_ll, TT)

            over(pe, U_GA, 4, lambda u, k: columns(u, xh, xl))
            over(pe, U_GB, 4, lambda u, k: columns(u, xh, xl))
            pe.wait_ge(g_ll, TT)

            def branch(u, k):
                s = begin(u)
                for j, (hi, lo) in enumerate(((gh, gl), (sh, sl))):
                    for kc in range(4):
                        mm = triple(ps[:, 2 * s + j], wh[:, s, 4 * j + kc, 0:P], wl[:, s, 4 * j + kc, 0:P],
                                    hi[:, kc], lo[:, kc], kc == 0, kc == 3)
                    mm.then_inc(chunk_done, 1)

            over(pe, U_BR, KC, branch)
            first = split_ready(MIXED)
            over(pe, U_OUT, 4, lambda u, k: columns(u, xh, xl, ready=first if k.base == 0 else None))
            square_stats(7)

            pe.wait_ge(xl_ready, KC * 9)
            rows(Lin(U_RT), xh, xl, n=36)
            for part in range(EXPERTS // PART_EXPERTS):
                u0, e0 = U_EX + part * (PART_EXPERTS + 4), part * PART_EXPERTS
                if part == 0:
                    columns(Lin(u0), xh, xl)
                    columns(Lin(u0 + 1), xh, xl)
                    pe.wait_ge(r_step, 32)
                    for t in range(TT):
                        tr = pe.transpose(ps[0:EXPERTS, 4, t * P:(t + 1) * P],
                                          m_cw[:, t].rearrange("p g e -> p (g e)"), ident)
                    tr.then_inc(cw_tr, 1)
                    over(pe, u0 + 2, PART_EXPERTS - 2, lambda u, k: columns(u, xh, xl), peel=0)
                else:
                    over(pe, u0, PART_EXPERTS, lambda u, k: columns(u, xh, xl))
                over(pe, u0 + PART_EXPERTS, 4, lambda u, k: columns(
                    u, ah, al, ready=(lambda kc: pe.wait_ge(m_hl, e0 + kc + 1)) if k.base == 0 else None))
            emptied(pe, Lin(UNITS - 2))
            emptied(pe, Lin(UNITS - 1))
            for c in range(KC):
                if c >= 4:
                    pe.wait_ge(o_cp, c - 3)
                for t in range(TT):
                    tr = pe.transpose(ps[:, 4 + c % 4, t * P:(t + 1) * P], X[:, c, t * P:(t + 1) * P], ident)
                tr.then_inc(o_tr, 1)


_INS = ["x", "mem", "diff_w_qkv", "diff_lambda", "diff_subln", "diff_w_o", "dil_w_qkv", "dil_w_o", "xatt_w_q",
        "xatt_w_kv", "xatt_w_o", "ffn_w_in", "ffn_conv_w", "ffn_conv_b", "ffn_w_out", "ln_g", "ln_b", "g_mix_2",
        "w_in_2", "w_alpha2_2", "b_alpha_2", "g_gla_2", "w_br_gla_2", "g_q_2", "g_k_2", "rel_bias_2", "w_br_att_2",
        "w_out_2", "g_ffn_2", "w_rg_2", "b_rg_2", "w_re_2", "b_re_2", "w_gate_2", "w_up_2", "w_down_2"]


def kernel(**inputs):
    import concourse.bacc as bacc
    from concourse.bass_utils import run_bass_kernel_spmd

    nc = bacc.Bacc("TRN2", target_bir_lowering=False, num_devices=1)
    host = {name: np.ascontiguousarray(inputs[name]) for name in _INS}
    host.update(tables())
    arrays, aps = {}, {}
    for name, value in host.items():
        arrays[f"in_{name}"] = value
        aps[name] = nc.dram_tensor(f"in_{name}", value.shape, mybir.dt.from_np(value.dtype), kind="ExternalInput").ap()
    out = nc.dram_tensor("out", (1, T, D), F32, kind="ExternalOutput").ap()
    program(nc, aps, out)
    result = run_bass_kernel_spmd(nc, [arrays], core_ids=[0])
    return result.results[0]["out"]
```

```python
import math
from contextlib import ExitStack

import numpy as np

import concourse.bass as bass
from concourse import mybir

F32 = mybir.dt.float32
F32R = mybir.dt.float32r
ALU = mybir.AluOpType
ACT = mybir.ActivationFunctionType
AX_X = mybir.AxisListType.X

P = 128
T = 512
TT = T // P
D = 1024
KC = D // P
M = 256
LAYERS = 2
ALPHA = (2 * LAYERS) ** 0.25
UC = 256
HIDDEN_PARTS = (8, 8, 6)
FF = 2816
DIFF_H, DIL_H = 8, 16
LAMBDA_INIT = 0.8 - 0.6 * math.exp(-0.3 * 0)
LN_EPS = 1e-5
RMS_EPS = 1e-6
MASKED = -1e30
TAKEN = -3e38
EXPERTS, PART_EXPERTS, GROUPS, PER_GROUP = 32, 8, 4, 8
TOPK = 128
ZW = 7 * P
ZC = 3 * P
DILW = 515 + 2 * P

SPLITS = [256, 256, 512, 512, 16, 512, 512, 512, 256, 32, 8, 1024, 1024]
(C_QA, C_KA, C_VA, C_RA, C_AL, C_QB, C_KB, C_VB, C_QI, C_KI, C_WI, C_GA, C_GB, _) = [
    int(v) for v in np.cumsum([0] + SPLITS)]

R_LNG, R_LNB, R_GMIX, R_GFFN, R_SUBLN, R_GGLA, R_GQ, R_GK = 0, 48, 96, 104, 112, 113, 114, 115
R_CONVB = 66


class Lin:

    def __init__(self, base, step=0, reg=None):
        self.base, self.step, self.reg = base, step, reg

    def __add__(self, k):
        return Lin(self.base + k, self.step, self.reg)

    def __mul__(self, k):
        return Lin(self.base * k, self.step * k, self.reg)

    def half(self):
        assert self.step % 2 == 0
        return Lin(self.base // 2, self.step // 2, self.reg)

    @property
    def v(self):
        return self.base if self.reg is None or self.step == 0 else self.reg * self.step + self.base

    def at(self):
        return slice(self.base, self.base + 1) if self.reg is None or self.step == 0 else bass.ds(self.v, 1)


def tables():
    f = np.float32
    eye = np.eye(P, dtype=f)
    half = np.zeros((P, P), f)
    half[:64, :64] = half[64:, 64:] = 1 / 64
    t = np.arange(P)
    later = ((t[:, None] > t[None, :]) & (t[:, None] // 64 == t[None, :] // 64)).astype(f) / 16
    rep = (t[:, None] == t[None, :] % 32).astype(f)
    idx = np.tile(np.arange(PER_GROUP, dtype=f), 16)
    const = np.concatenate([eye, half, np.full((P, P), 1 / D, f), np.full((P, P), 1 / P, f), later, rep,
                            np.broadcast_to(idx, (P, P))], axis=1)
    p, m = t[:, None], np.arange(ZW)[None, :]
    dist = np.abs(m - ZC - p).astype(f)
    slopes = np.exp2(-8.0 * np.arange(1, DIFF_H + 1, dtype=f) / DIFF_H).astype(f)
    diff_bias = -8 * slopes[:, None, None] * dist
    slopes = np.exp2(-8.0 * np.arange(1, DIL_H + 1, dtype=f) / DIL_H).astype(f)
    near = np.abs(4 * p - (np.arange(515)[None, :] - 3))
    u = np.abs(p - t[None, :])
    dil_bias = np.zeros((DIL_H + 2, P, DILW), f)
    for h in range(DIL_H):
        dil_bias[h, :, :515] = np.where(near <= 64, -8 * slopes[h] * near, MASKED)
        dil_bias[h, :, 515:643] = np.where(u <= 64, -8 * slopes[h] * 4 * u, MASKED)
        dil_bias[h, :, 643:] = np.where(u % 4 == 0, -8 * slopes[h] * 4 * u, MASKED)
    rel = np.arange(-511, 512)
    n = np.abs(rel)
    large = 8 + sum((n >= b).astype(int) for b in (12, 16, 23, 32, 46, 64, 91))
    bucket = np.where(rel > 0, 16, 0) + np.where(n < 8, n, large)
    onehot = (np.arange(32)[:, None] == bucket[None, :]).astype(f) * 8
    onehot = np.concatenate([onehot, np.zeros((32, 1), f)], axis=1)
    return {"one_row": np.ones((1, T), f), "const": const, "diff_bias": diff_bias.astype(f), "dil_bias": dil_bias,
            "onehot": onehot}


def program(nc, a, out):
    with ExitStack() as ctx:
        base = (nc.sbuf_base + 31) // 32 * 32

        def at(name, kb, shape, dt=F32):
            return nc.alloc_sbuf_tensor_at(name, shape, dt, offset=base + int(kb * 1024))

        def sem(name):
            return ctx.enter_context(nc.semaphore(name))

        LAG = 3

        X = at("X", 0, [P, KC, T])
        xh = at("xh", 16, [P, KC, T], F32R)
        xl = at("xl", 32, [P, KC, T], F32R)
        raw = at("raw", 48, [P, 2, KC, UC])
        wh = at("wh", 64, [P, 2, KC, UC], F32R)
        wl = at("wl", 80, [P, 2, KC, UC], F32R)
        const = at("const", 96, [P, 7, P])
        ident, half_mean, mean_d, mean_p, later, rep32, idx8 = (const[:, n, :] for n in range(7))
        par = at("par", 99.5, [P, 3, P])
        small = at("small", 101, [P, 128])
        ones = at("ones", 101.5, [P, P])
        mean = at("mean", 102, [P, T])
        rstd = at("rstd", 104, [P, T])
        t2 = at("t2", 106, [P, 2, T])
        zz = at("zz", 110, [P, 2, T])
        acc_s = at("acc_s", 203.75, [P, 1, T])
        acc_q = at("acc_q", 205.75, [P, T])
        ah = at("ah", 114, [P, KC, T], F32R)
        al = at("al", 130, [P, KC, T], F32R)
        A0 = 146
        xrows = at("xrows", 0, [P, TT, D])
        prow = at("prow", A0, [P, 3, P])
        lamb = at("lamb", A0 + 2, [P, 4, 64])
        hot = at("hot", A0 + 4, [32, 1024])
        relb = at("relb", A0 + 8, [32, 8])
        zline = at("zline", 203.75, [8, 1024])
        d_q = at("d_q", A0, [P, 2, T])
        d_k = at("d_k", A0 + 4, [P, 2, T])
        d_v = at("d_v", A0 + 8, [P, TT, UC])
        d_bias = at("d_bias", A0 + 12, [P, 2, ZW])
        d_t = at("d_t", A0 + 19, [P, 2, 2, T])
        d_e = at("d_e", A0 + 27, [P, LAG + 1, T])
        d_e1 = at("d_e1", A0 + 55, [P, 2, T])
        d_pt = at("d_pt", A0 + 35, [P, 2, TT, T])
        d_o = at("d_o", A0 + 51, [P, T])
        d_sq = at("d_sq", A0 + 53, [P, T])
        l_q = at("l_q", A0, [P, 3, 2, T])
        l_k = at("l_k", A0 + 12, [P, 3, 2, T])
        l_v = at("l_v", A0 + 24, [P, 3, TT, UC])
        l_bias = at("l_bias", A0 + 36, [P, 2, DILW])
        l_t = at("l_t", A0 + 42.125, [P, 2, 768])
        l_e = at("l_e", A0 + 48.125, [P, LAG + 1, 768])
        l_pt = at("l_pt", 0, [P, 6, T])
        mrows = at("mrows", A0, [P, 2, D])
        mh = at("mh", A0 + 8, [P, KC, M], F32R)
        ml = at("ml", A0 + 16, [P, KC, M], F32R)
        x_k = at("x_k", A0 + 24, [P, KC, M])
        x_v = at("x_v", A0 + 32, [P, 2, D])
        x_q = at("x_q", A0, [P, KC, T])
        x_pt = at("x_pt", A0 + 40, [P, 8, T])
        x_e = at("x_e", A0 + 16, [P, 2, 4 * M])
        f_c = at("f_c", A0, [P, 2, T])
        f_g = at("f_g", A0 + 4, [P, 2, T])
        f_y = at("f_y", A0 + 8, [P, 2, T])
        m_w = at("m_w", A0 + 12, [P, 2, T])
        i_q = at("i_q", A0, [P, 2, T])
        i_k = at("i_k", A0 + 4, [P, T])
        i_m = at("i_m", A0 + 6, [P, TT, T])
        s_k = at("s_k", A0 + 14, [P, TT, T])
        s_q = at("s_q", A0 + 22, [P, TT, T])
        q_n4 = at("q_n4", A0 + 38, [P, 2, TT, T])
        s_v = at("s_v", A0 + 30, [P, TT, T])
        g_q = at("g_q", A0 + 38, [P, 2, T])
        g_k = at("g_k", A0 + 42, [P, TT, UC])
        g_v = at("g_v", A0 + 46, [P, TT, T])
        g_r = at("g_r", A0 + 30, [P, TT, T])
        g_a = at("g_a", 138, [P, TT, UC])
        g_d = at("g_d", 200, [P, TT, UC])
        g_dec = at("g_dec", 204, [P, 2, 8])
        walpha = at("walpha", 205, [P, UC])
        sm_t = at("sm_t", A0 + 14, [P, T])
        rt_t = at("rt_t", A0 + 24, [36, T])
        m_lg = at("m_lg", A0 + 16, [P, TT, 36])
        m_rb = at("m_rb", A0 + 17, [P, 36])
        m_cw = at("m_cw", A0 + 17.5, [P, TT, GROUPS, PER_GROUP])
        m_tmp = at("m_tmp", A0 + 18, [P, 2, TT, GROUPS, PER_GROUP])
        m_e = at("m_e", A0 + 19, [P, 5, TT, PER_GROUP])
        m_g = at("m_g", A0 + 20, [P, 16, TT])
        m_oh = at("m_oh", A0 + 20.5, [P, 3, TT, GROUPS])
        m_cwt = at("m_cwt", A0 + 22, [EXPERTS, T])
        orow = at("orow", 16, [P, TT, D])
        s_z = at("s_z", A0 + 38, [P, 2, ZW])
        s_b = at("s_b", A0 + 45, [P, 2, T])
        s_t = at("s_t", A0 + 49, [P, 2, T])
        s_e = at("s_e", A0 + 53, [P, LAG + 1, T])
        s_pt = at("s_pt", A0, [P, 2, T])
        gate_a = at("gate_a", A0 + 29.75, [P, KC, T])
        gate_b = at("gate_b", A0 + 45.75, [P, KC, T])
        gh = at("gh", 114, [P, TT, T], F32R)
        gl = at("gl", 122, [P, TT, T], F32R)
        sh = at("sh", 130, [P, TT, T], F32R)
        sl = at("sl", 138, [P, TT, T], F32R)
        g_st = at("g_st", 130, [P, 2, 8, P])
        i_r = at("i_r", 142, [P, 2, T])
        ps = ctx.enter_context(nc.psum_tensor("ps", [P, 8, T], F32))
        flat = ps[:, :, :].rearrange("p b n -> p (b n)")
        scratch = nc.dram_tensor("cw_scratch", [EXPERTS, T], F32).ap()
        zscratch = nc.dram_tensor("z_scratch", [8, 1024], F32).ap()
        zcopies = nc.dram_tensor("z_copies", [8, P, 1024], F32).ap()

        negm = small[:, 0:16].rearrange("p (b n) -> p b n", b=2)
        sums = small[:, 16:32].rearrange("p (b n) -> p b n", b=2)
        rec = small[:, 32:48].rearrange("p (b n) -> p b n", b=2)
        mx = small[:, 48:64].rearrange("p (b n) -> p b n", b=2)
        neglam = small[:, 64:65]
        lam_s = small[:, 65:67]
        lam_e = small[:, 67:69]
        subln8 = small[:, 69:70]
        idle = small[:, 120:121]
        eps_ln, eps_rms = small[:, 121:122], small[:, 122:123]
        m8 = small[:, 72:80]
        wi_row = small[:, 80:112].rearrange("p (t n) -> p t n", t=TT)

        U_ATT = (0, 66)
        U_WO = (12, 102)
        U_MEM = (16, 106)
        U_MQ = (24, 114)
        U_MO = (28, 118)
        U_FF = (32, 122)
        U_QI, U_SM, U_QA, U_KA, U_VA, U_RA, U_QB, U_KB, U_VB, U_GA, U_GB, U_BR, U_OUT, U_RT, U_EX = (
            156, 157, 158, 159, 160, 162, 164, 166, 168, 170, 174, 178, 186, 190, 191)
        UNITS = 239

        raw_in = [sem("raw_in0"), sem("raw_in1")]
        hi_done, lo_done = sem("hi_done"), sem("lo_done")
        chunk_done = sem("chunk_done")
        drained = [sem("drained0"), sem("drained1")]
        x_in, p_in, m_in, lam_in, z_in, zs_out = (sem(n) for n in ("x_in", "p_in", "m_in", "lam_in", "z_in", "zs_out"))
        zc_out, mean_mm, keep_mm = sem("zc_out"), sem("mean_mm"), sem("keep_mm")
        xt_done, par_t, par_s = sem("xt_done"), sem("par_t"), sem("par_s")
        z_mm, z_cp = sem("z_mm"), sem("z_cp")
        lam_d, lam_x = sem("lam_d"), sem("lam_x")
        ones_set = sem("ones_set")
        xh_ready, xl_ready = sem("xh_ready"), sem("xl_ready")
        y_ready, sq_done, acc_s_done, acc_q_done = sem("y_ready"), sem("sq_done"), sem("acc_s_done"), sem("acc_q_done")
        stat_mm, ln_act, ln_dve = sem("stat_mm"), sem("ln_act"), sem("ln_dve")
        cent, nrm, z_ready = sem("cent"), sem("nrm"), sem("z_ready")
        dbias_in = [sem("dbias_in0"), sem("dbias_in1")]
        d_qk, d_scored, d_negm, d_exp, d_rec, d_mix = (sem("d_" + n) for n in ("qk", "scored", "negm", "exp", "rec", "mix"))
        d_half, d_tr, d_ptr, d_pv, d_osb, d_st, d_ln, d_on, d_z = (
            sem("d_" + n) for n in ("half", "tr", "ptr", "pv", "osb", "st", "ln", "on", "z"))
        ah_ready, al_ready = sem("ah_ready"), sem("al_ready")
        lbias_in = [sem("lbias_in0"), sem("lbias_in1")]
        l_qk, l_scored, l_negm, l_exp, l_rec, l_mix, l_tr, l_ptr, l_pv, l_ah, l_al = (
            sem("l_" + n) for n in ("qk", "scored", "negm", "exp", "rec", "mix", "tr", "ptr", "pv", "ah", "al"))
        mt_done, mh_done, ml_done = sem("mt_done"), sem("mh_done"), sem("ml_done")
        x_qk, x_max, x_negm, x_exp, x_rec, x_mix, x_tr, x_ptr, x_pv, x_ah, x_al = (
            sem("x_" + n) for n in ("qk", "max", "negm", "exp", "rec", "mix", "tr", "ptr", "pv", "ah", "al"))
        sm_done, wi_tr, wi_s, i_qk, i_relu, i_acc, i_max, i_cut, i_mask, i_edge = (
            sem(n) for n in ("sm_done", "wi_tr", "wi_s", "i_qk", "i_relu", "i_acc", "i_max", "i_cut",
                             "i_mask", "i_edge"))
        wa_in, g_z, g_abs, g_la, g_lat, g_tot, g_ex, g_kd, g_u, g_state, g_o, g_sq, g_st_mm, g_ln, g_n, g_y, \
            g_hh, g_ll = (sem(n) for n in ("wa_in", "g_z", "g_abs", "g_la", "g_lat", "g_tot", "g_ex", "g_kd", "g_u",
                                           "g_state", "g_o", "g_sq", "g_st_mm", "g_ln", "g_n", "g_y", "g_hh",
                                           "g_ll"))
        q_sq, q_mm, q_ln, q_n = (sem("q_" + n) for n in ("sq", "mm", "ln", "n"))
        sz_in = [sem("sz_in0"), sem("sz_in1")]
        s_bm, s_qk, s_scored, s_negm, s_exp, s_rec, s_mix, s_tr, s_ptr, s_pv, s_hh, s_ll = (
            sem("s_" + n) for n in ("bm", "qk", "scored", "negm", "exp", "rec", "mix", "tr", "ptr", "pv", "hh", "ll"))
        b_sum = sem("b_sum")
        rt_cp = sem("rt_cp")
        rb_in, r_step, r_act, cw_tr, cw_cp, cw_out = (sem(n) for n in ("rb_in", "r_step", "r_act", "cw_tr", "cw_cp",
                                                                      "cw_out"))
        mw_in = [sem("mw_in0"), sem("mw_in1")]
        m_y, m_hh, m_hl = sem("m_y"), sem("m_hh"), sem("m_hl")
        o_tr, o_cp, o_out = sem("o_tr"), sem("o_cp"), sem("o_out")
        f_cd, f_left, f_gd, f_hh, f_hl = (sem("f_" + n) for n in ("c", "left", "g", "hh", "hl"))

        NORM_AT = [(n + 1, 3 * n + 3, 3 * n + 3) for n in range(6)] + [(6, 20, None), (8, 22, None)]
        MIXED = 7

        def slot_of(u):
            assert u.step % 2 == 0
            return u.base % 2

        def emptied(eng, u):
            eng.wait_ge(drained[slot_of(u)], (u.half() * 2 + 2).v)

        def over(eng, u0, n, body, peel=2):
            peel = min(peel, n)
            for k in range(peel):
                body(Lin(u0 + k), Lin(k))
            pairs = (n - peel) // 2
            if pairs > 1:
                with eng.Fori(0, pairs) as i:
                    for k in range(peel, peel + 2):
                        body(Lin(u0 + k, 2, i), Lin(k, 2, i))
            else:
                for k in range(peel, peel + 2 * pairs):
                    body(Lin(u0 + k), Lin(k))
            for k in range(peel + 2 * pairs, n):
                body(Lin(u0 + k), Lin(k))

        block = ctx.enter_context(nc.Block())

        @block.sync
        def _(sp):
            def load(u, *parts):
                s = slot_of(u)
                if u.base >= 2:
                    sp.wait_ge(lo_done, (u + -1).v)
                for dst, src in parts:
                    sp.dma_start(dst(s), src).then_inc(raw_in[s], 16)

            def square(u, w, col, k0=0, kcs=KC):
                w3 = w.rearrange("(k p) n -> p k n", p=P)
                h = kcs // 2
                cols = bass.ds(col, UC)
                load(u, (lambda s: raw[:, s, 0:h, :], w3[:, k0:k0 + h, cols]),
                     (lambda s: raw[:, s, h:kcs, :], w3[:, k0 + h:k0 + kcs, cols]))

            def pair(u, w, c0, c1):
                w3 = w.rearrange("(k p) n -> p k n", p=P)
                load(u, (lambda s: raw[:, s, :, 0:P], w3[:, :, bass.ds(c0, P)]),
                     (lambda s: raw[:, s, :, P:UC], w3[:, :, bass.ds(c1, P)]))

            sp.dma_start(xrows[:], a["x"][0].rearrange("(t p) d -> p t d", p=P)).then_inc(x_in, 16)
            sp.dma_start(const[:], a["const"].rearrange("p (n m) -> p n m", m=P)).then_inc(x_in, 16)
            sp.dma_start(lamb[:, :, :].rearrange("p a b -> p (a b)"),
                         a["diff_lambda"].rearrange("o a b -> o (a b)").to_broadcast([P, 256])).then_inc(lam_in, 16)
            qkv = a["diff_w_qkv"][0]
            for role in range(2):
                square(Lin(role), qkv, role * D)

            def prows(row, block_, view):
                n = view.shape[0]
                sp.dma_start(prow[row:row + n, block_, 0:view.shape[1]], view).then_inc(p_in, 16)

            prows(R_LNG, 0, a["ln_g"].rearrange("l s (c p) -> (l s c) p", p=P))
            prows(R_LNB, 0, a["ln_b"].rearrange("l s (c p) -> (l s c) p", p=P))
            prows(R_GMIX, 0, a["g_mix_2"][0].rearrange("(c p) -> c p", p=P))
            prows(R_GFFN, 0, a["g_ffn_2"][0].rearrange("(c p) -> c p", p=P))
            prows(R_SUBLN, 0, a["diff_subln"])
            prows(R_GGLA, 0, a["g_gla_2"])
            for side in range(2):
                for row, name in ((R_GQ, "g_q_2"), (R_GK, "g_k_2")):
                    sp.dma_start(prow[row:row + 1, 0, 64 * side:64 * side + 64], a[name]).then_inc(p_in, 16)
            for layer in range(LAYERS):
                prows(0, 1 + layer, a["ffn_conv_w"][layer].rearrange("w (c p) -> (w c) p", p=P))
                prows(R_CONVB, 1 + layer, a["ffn_conv_b"][layer].rearrange("(c p) -> c p", p=P))
            sp.dma_start(hot[:], a["onehot"]).then_inc(z_in, 16)
            sp.dma_start(relb[:], a["rel_bias_2"]).then_inc(z_in, 16)
            def diff_group(g):
                for role in range(2 if g.base == 0 else 0, 3):
                    u = g * 3 + role
                    square(u, qkv, (g * UC + role * D).v)
                for b in range(2):
                    h = g * 2 + b
                    sp.wait_ge(d_scored, (h * 8).v)
                    sp.dma_start(d_bias[:, b, :], a["diff_bias"].rearrange("h p n -> p h n")[:, bass.ds(h.v, 1), :]
                                 ).then_inc(dbias_in[b], 16)

            diff_group(Lin(0))
            diff_group(Lin(1))
            diff_group(Lin(2))
            diff_group(Lin(3))

            def after_attention(layer, w_o):
                for k in range(2):
                    square(Lin(U_WO[layer] + k), w_o, k * UC)
                sp.wait_ge((al_ready, l_al)[layer], 8 + 1)
                sp.dma_start(mrows[:], a["mem"][0].rearrange("(t p) d -> p t d", p=P)).then_inc(m_in, 16)
                for k in range(2, 4):
                    square(Lin(U_WO[layer] + k), w_o, k * UC)
                kv = a["xatt_w_kv"][layer]
                over(sp, U_MEM[layer], 8, lambda u, k: square(u, kv, (k * UC).v))
                over(sp, U_MQ[layer], 4, lambda u, k: square(u, a["xatt_w_q"][layer], (k * UC).v))
                over(sp, U_MO[layer], 4, lambda u, k: square(u, a["xatt_w_o"][layer], (k * UC).v))
                u0, f0 = U_FF[layer], 0
                for n in HIDDEN_PARTS:
                    win = a["ffn_w_in"][layer]
                    over(sp, u0, n, lambda u, k: pair(u, win, ((k + f0) * P).v, ((k + f0) * P + FF).v))
                    wout = a["ffn_w_out"][layer]
                    over(sp, u0 + n, 4, lambda u, k: square(u, wout, (k * UC).v, k0=f0, kcs=n))
                    u0, f0 = u0 + n + 4, f0 + n

            after_attention(0, a["diff_w_o"][0])
            sp.wait_ge(zs_out, 16)
            for h in range(8):
                sp.dma_start(zcopies[h:h + 1, :, :], zscratch[h:h + 1, :].unsqueeze(1).to_broadcast([1, P, 1024])
                             ).then_inc(zc_out, 16)
            lqkv = a["dil_w_qkv"][0]

            def dil_group(g):
                for n in range(9):
                    square(g * 9 + (n + U_ATT[1]), lqkv, (g * UC + n * D).v)
            sp.wait_ge(x_ptr, TT)
            for b in range(2):
                sp.dma_start(l_bias[:, b, :], a["dil_bias"][b]).then_inc(lbias_in[b], 16)
            with sp.Fori(0, 2) as i:
                dil_group(Lin(0, 2, i))
                dil_group(Lin(1, 2, i))
            after_attention(1, a["dil_w_o"][0])

            w_in = a["w_in_2"][0]
            w3 = w_in.rearrange("(k p) n -> p k n", p=P)
            square(Lin(U_QI), w_in, C_QI)
            load(Lin(U_SM), (lambda s: raw[:, s, :, 0:40], w3[:, :, C_KI:C_KI + 40]),
                 (lambda s: raw[:, s, :, 64:80], w3[:, :, C_AL:C_AL + 16]))
            square(Lin(U_QA), w_in, C_QA)
            sp.wait_ge(xh_ready, KC * 6 + 1)
            sp.dma_start(walpha[64:80, :], a["w_alpha2_2"][0]).then_inc(wa_in, 16)
            sp.dma_start(walpha[80:81, :], a["b_alpha_2"]).then_inc(wa_in, 16)
            sp.dma_start(sm_t[80:81, :], a["one_row"]).then_inc(wa_in, 16)
            square(Lin(U_KA), w_in, C_KA)
            for k in range(2):
                square(Lin(U_VA + k), w_in, C_VA + k * UC)
            for k in range(2):
                square(Lin(U_RA + k), w_in, C_RA + k * UC)
            for k in range(2):
                square(Lin(U_QB + k), w_in, C_QB + k * UC)
            for k in range(2):
                square(Lin(U_KB + k), w_in, C_KB + k * UC)
            for k in range(2):
                square(Lin(U_VB + k), w_in, C_VB + k * UC)
            for k in range(2):
                square(Lin(U_GA + k), w_in, C_GA + k * UC)
            for h in range(8):
                if h == 0:
                    sp.wait_ge(zc_out, 16 * 8)
                    sp.wait_ge(q_n, 4)
                if h >= 2:
                    sp.wait_ge(s_bm, TT * (h - 1))
                z = zcopies[h:h + 1, :, :]
                shifted = bass.AP(tensor=z.tensor, offset=z.offset + P - 1, ap=[[1023, P], [1, ZW]])
                sp.dma_start(s_z[:, h % 2, :], shifted).then_inc(sz_in[h % 2], 16)
            for k in range(2, 4):
                square(Lin(U_GA + k), w_in, C_GA + k * UC)
            over(sp, U_GB, 4, lambda u, k: square(u, w_in, (k * UC + C_GB).v))
            br_g = a["w_br_gla_2"][0].rearrange("(k p) n -> p k n", p=P)
            br_s = a["w_br_att_2"][0].rearrange("(k p) n -> p k n", p=P)
            over(sp, U_BR, KC, lambda u, k: load(
                u, (lambda s: raw[:, s, 0:4, 0:P], br_g[:, :, bass.ds((k * P).v, P)]),
                (lambda s: raw[:, s, 4:8, 0:P], br_s[:, :, bass.ds((k * P).v, P)])))
            over(sp, U_OUT, 4, lambda u, k: square(u, a["w_out_2"][0], (k * UC).v))
            load(Lin(U_RT),
                 (lambda s: raw[:, s, :, 0:EXPERTS], a["w_re_2"][0].rearrange("(k p) n -> p k n", p=P)),
                 (lambda s: raw[:, s, :, EXPERTS:36], a["w_rg_2"][0].rearrange("(k p) n -> p k n", p=P)))
            w_gate = a["w_gate_2"][0].rearrange("e (k p) n -> p (e k) n", p=P)
            w_up = a["w_up_2"][0].rearrange("e (k p) n -> p (e k) n", p=P)
            w_down = a["w_down_2"][0].rearrange("e p n -> p e n")

            def expert_weights(u, e):
                load(u, (lambda s: raw[:, s, :, 0:P], w_gate[:, bass.ds((e * KC).v, KC), :]),
                     (lambda s: raw[:, s, :, P:UC], w_up[:, bass.ds((e * KC).v, KC), :]))

            def combine_weights(e):
                b = e.base % 2
                if e.base >= 2:
                    sp.wait_ge(m_y, (e + -1).v)
                sp.dma_start(m_w[:, b, :], scratch[e.at(), :].to_broadcast([P, T])).then_inc(mw_in[b], 16)

            for part in range(EXPERTS // PART_EXPERTS):
                u0, e0 = U_EX + part * (PART_EXPERTS + 4), part * PART_EXPERTS

                def expert(u, k):
                    expert_weights(u, k + e0)
                    combine_weights(k + e0)

                if part == 0:
                    expert_weights(Lin(u0), Lin(0))
                    expert_weights(Lin(u0 + 1), Lin(1))
                    sp.wait_ge(xh_ready, KC * 8 + 1)
                    sp.dma_start(m_rb[:, 0:EXPERTS], a["b_re_2"].to_broadcast([P, EXPERTS])).then_inc(rb_in, 16)
                    sp.dma_start(m_rb[:, EXPERTS:36], a["b_rg_2"].to_broadcast([P, GROUPS])).then_inc(rb_in, 16)
                    expert_weights(Lin(u0 + 2), Lin(2))
                    expert_weights(Lin(u0 + 3), Lin(3))
                    sp.wait_ge(cw_out, 16)
                    for k in range(4):
                        combine_weights(Lin(k))
                    over(sp, u0 + 4, PART_EXPERTS - 4, lambda u, k: expert(u, k + 4), peel=0)
                else:
                    over(sp, u0, PART_EXPERTS, expert)
                h = PART_EXPERTS // 2
                over(sp, u0 + PART_EXPERTS, 4, lambda u, k: load(
                    u, (lambda s: raw[:, s, 0:h, :], w_down[:, e0:e0 + h, bass.ds((k * UC).v, UC)]),
                    (lambda s: raw[:, s, h:KC, :], w_down[:, e0 + h:e0 + 2 * h, bass.ds((k * UC).v, UC)])))
            orows = out[0].rearrange("(t p) d -> p t d", p=P)
            for q in range(4):
                sp.wait_ge(o_cp, 2 * q + 2)
                sp.dma_start(orows[:, :, q * UC:(q + 1) * UC], orow[:, :, q * UC:(q + 1) * UC]).then_inc(o_out, 16)
            sp.wait_ge(o_out, 64)

        @block.gpsimd
        def _(pool):
            def low(u, n=UC):
                s = slot_of(u)
                pool.wait_ge(hi_done, (u + 1).v)
                pool.tensor_tensor(wl[:, s, :, 0:n], raw[:, s, :, 0:n], wh[:, s, :, 0:n].bitcast(F32), ALU.subtract
                                   ).then_inc(lo_done, 1)

            def lows(first, last, n=UC):
                assert (last - first) % 2 == 0 and first % 2 == 0
                with pool.Fori(0, (last - first) // 2) as i:
                    low(Lin(first, 2, i), n)
                    low(Lin(first + 1, 2, i), n)

            def low_parts(event):
                for c in range(KC):
                    pool.wait_ge(xh_ready, KC * event + c + 1)
                    pool.tensor_tensor(xl[:, c], zz[:, c % 2], xh[:, c].bitcast(F32), ALU.subtract).then_inc(xl_ready, 1)

            lows(0, U_FF[0] + 2)
            low_parts(2)
            lows(U_FF[0] + 2, U_ATT[1] + 2)
            low_parts(3)
            lows(U_ATT[1] + 2, U_FF[1] + 2)
            low_parts(5)
            lows(U_FF[1] + 2, U_QI + 2)
            low_parts(6)
            lows(U_QI + 2, U_GA + 2)
            for h in range(8):
                pool.wait_ge(sz_in[h % 2], 16 * (h // 2) + 16)
                for i in range(TT):
                    n, w = TT * h + i, P * (i + 1)
                    if n == 0:
                        pool.wait_ge(i_mask, TT)
                        pool.wait_ge(q_n, 8)
                    if n >= 2:
                        pool.wait_ge(s_scored, n - 1)
                    z0 = ZC - P * i
                    pool.tensor_tensor(s_b[:, n % 2, 0:w], s_z[:, h % 2, z0:z0 + w], i_m[:, i, 0:w], ALU.add
                                       ).then_inc(s_bm, 1)
            lows(U_GA + 2, U_BR)
            lows(U_BR, U_OUT, P)
            lows(U_OUT, U_RT + 2)
            low_parts(8)
            lows(U_RT + 2, UNITS - 1)
            low(Lin(UNITS - 1))

        @block.scalar
        def _(act):
            def high(u, n=UC):
                s = slot_of(u)
                if u.step == 0 and u.base >= UNITS:
                    return
                act.wait_ge(raw_in[s], (u.half() * 32 + 32).v)
                if u.base >= 2:
                    act.wait_ge(chunk_done, (u * 2 + -2).v)
                act.activation(wh[:, s, :, 0:n], raw[:, s, :, 0:n], ACT.Copy).then_inc(hi_done, 1)

            def bank(u, j):
                return ps[:, 2 * slot_of(u) + j]

            def done(u, j):
                act.wait_ge(chunk_done, (u * 2 + (j + 1)).v)

            def copy_out(u, dst, func=ACT.Copy, scale=1.0):
                for j in range(2):
                    done(u, j)
                    act.activation(dst(j), bank(u, j), func, scale=scale).then_inc(drained[slot_of(u)], 1)

            for ahead in (d_ptr, d_osb, d_z, d_ln, l_ptr):
                act.sem_inc(ahead, 1)
            act.wait_ge(lam_d, 4)
            act.activation(lam_e, lam_s, ACT.Exp).then_inc(lam_x, 1)
            for c in range(KC):
                act.wait_ge(xt_done, c + 1)
                act.activation(xh[:, c], ps[:, c % 4], ACT.Copy).then_inc(xh_ready, 1)
            high(Lin(0))
            high(Lin(1))
            act.wait_ge(par_t, 1)
            for n, rows_ in enumerate((R_GK + 1, 88, 88)):
                act.activation(par[:, n, 0:rows_], ps[:, 4, n * P:n * P + rows_], ACT.Copy).then_inc(par_s, 1)
            act.wait_ge(par_s, 3)
            act.activation(subln8, par[:, 0, R_SUBLN:R_SUBLN + 1], ACT.Copy, scale=1 - LAMBDA_INIT).then_inc(par_s, 1)
            act.wait_ge(z_mm, 2)
            for j in range(2):
                act.activation(zline[:, j * T:(j + 1) * T], ps[0:8, 5 + j], ACT.Copy).then_inc(z_cp, 1)
            act.wait_ge(z_cp, 2)
            act.dma_start(zscratch, zline[:]).then_inc(zs_out, 16)
            act.wait_ge(zs_out, 16)

            def diff_group(g):
                u = g * 3
                high(u + 2)
                copy_out(u, lambda j: d_q[:, j])
                high(u + 3)
                copy_out(u + 1, lambda j: d_k[:, j])
                act.wait_ge(chunk_done, (u * 2 + 6).v)
                high(u + 4)
                for l in range(8 + LAG + 4):
                    if LAG <= l < 8 + LAG:
                        n = g * 8 + (l - LAG)
                        hh, i = (l - LAG) // 4, (l - LAG) % 4
                        act.wait_ge(d_tr, (n + 5).v)
                        if i == 0:
                            act.wait_ge(d_pv, (g * 2 + (hh + 1)).v)
                        act.activation(d_pt[:, hh, :, i * P:(i + 1) * P],
                                       ps[:, (l - LAG) % 2].rearrange("p (k q) -> p k q", k=TT), ACT.Copy
                                       ).then_inc(d_ptr, 1)
                    if l < 8:
                        n = g * 8 + l
                        b = l % 2
                        act.wait_ge(d_negm, (n + 1).v)
                        act.wait_ge(d_tr, (n + 1).v)
                        for c in range(2):
                            act.activation(d_e[:, l % (LAG + 1)] if c == 0 else d_e1[:, b], d_t[:, b, c], ACT.Exp, bias=negm[:, b, c:c + 1], scale=0.125,
                                           accum_out=sums[:, b, c:c + 1]).then_inc(d_exp, 1)
                    if l in (LAG + 5, LAG + 9):
                        h = g * 2 + (l - LAG - 5) // 4
                        act.wait_ge(d_pv, (h + 3).v)
                        act.wait_ge(d_on, (h + 1).v)
                        act.activation(d_o[:], ps[:, 2], ACT.Copy).then_inc(d_osb, 1)
                        act.wait_ge(d_st, (h + 1).v)
                        act.activation(d_sq[:], ps[:, 2], ACT.Square).then_inc(d_osb, 1)
                    if l in (LAG + 6, LAG + 10):
                        h = g * 2 + (l - LAG - 6) // 4
                        act.wait_ge(d_st, (h + 2).v)
                        act.activation(mean[:], ps[:, 3], ACT.Ln, bias=eps_ln).then_inc(d_ln, 1)
                        act.wait_ge(d_ln, (h * 2 + 2).v)
                        act.activation(rstd[:], mean[:], ACT.Exp, scale=-0.5).then_inc(d_ln, 1)
                    if l in (LAG + 7, LAG + 11):
                        h = g * 2 + (l - LAG - 7) // 4
                        act.wait_ge(d_on, (h + 1 + 1).v)
                        act.wait_ge(al_ready, (h + 1).v)
                        act.activation(zz[:, 0], t2[:, 0], ACT.Copy, scale=subln8).then_inc(d_z, 1)
                        act.wait_ge(d_z, (h + 1 + 1).v)
                        act.activation(ah[:, h.at(), :], zz[:, 0:1, :], ACT.Copy).then_inc(ah_ready, 1)

            act.wait_ge(xl_ready, KC)
            with act.Fori(0, 2) as i:
                diff_group(Lin(0, 2, i))
                diff_group(Lin(1, 2, i))

            def dil_group(g):
                u0 = g * 9 + U_ATT[1]
                for n in range(9):
                    u = u0 + n
                    done(u, 1)
                    high(u + 2)
                    p, role = n // 3, n % 3
                    if role < 2:
                        copy_out(u, lambda j: (l_q, l_k)[role][:, p, j])
                for l in range(16 + LAG + 2):
                    if LAG <= l < 16 + LAG:
                        n = g * 16 + (l - LAG)
                        hh, j = (l - LAG) // 4, (l - LAG) % 4
                        act.wait_ge(l_tr, (n + 5).v)
                        if j == 0:
                            act.wait_ge(l_pv, (g * 4 + hh + 1).v)
                        act.activation(l_pt[:, :, j * P:(j + 1) * P],
                                       flat[:, 0:768].rearrange("p (k q) -> p k q", k=6), ACT.Copy
                                       ).then_inc(l_ptr, 1)
                    if l < 16:
                        n = g * 16 + l
                        act.wait_ge(l_negm, (n + 1).v)
                        act.wait_ge(l_tr, (n + 1).v)
                        act.activation(l_e[:, l % (LAG + 1)], l_t[:, l % 2], ACT.Exp, bias=negm[:, l % 2, 0:1], scale=0.125,
                                       accum_out=sums[:, l % 2, 0:1]).then_inc(l_exp, 1)
                        if l % 4 == 3:
                            hh = l // 4
                            act.dma_start(l_bias[:, hh % 2, :],
                                          a["dil_bias"].rearrange("h p n -> p h n")[:, bass.ds((g * 4 + (hh + 2)).v, 1), :]
                                          ).then_inc(lbias_in[hh % 2], 16)
                    if l in (LAG + 9, LAG + 17):
                        c = g * 2 + (l - LAG - 9) // 8
                        act.wait_ge(l_pv, (g * 4 + ((l - LAG - 9) // 8 * 2 + 2) + 1).v)
                        act.activation(ah[:, c.at(), :].rearrange("p c (u j) -> p c j u", j=4),
                                       ps[:, 2:3].rearrange("p c (j u) -> p c j u", j=4), ACT.Copy).then_inc(l_ah, 1)

            def norm(n, g_row, b_row=None, keep=False, memory=None):
                event, on_act, on_dve = NORM_AT[n]
                if b_row is not None:
                    act.wait_ge(mean_mm, n + 1)
                    act.activation(mean[:], ps[:, 4], ACT.Copy).then_inc(ln_act, 1)
                    if memory is not None:
                        memory(0)
                    act.wait_ge(ln_dve, on_dve)
                    act.activation(acc_s[:, 0], acc_s[:, 0], ACT.Ln).then_inc(ln_act, 1)
                else:
                    if n == 6:
                        act.wait_ge(keep_mm, KC)
                    else:
                        act.wait_ge(stat_mm, n)
                    act.activation(acc_s[:, 0], ps[:, 5], ACT.Ln, bias=eps_rms).then_inc(ln_act, 1)
                act.wait_ge(ln_act, on_act - 1)
                act.activation(rstd[:], acc_s[:, 0], ACT.Exp, scale=-0.5).then_inc(ln_act, 1)
                for c in range(KC):
                    act.wait_ge(nrm, KC * n + c + 1)
                    z = X[:, c] if keep else zz[:, c % 2]
                    if not keep and c >= 2:
                        act.wait_ge(xl_ready, KC * event + c - 1)
                    if b_row is None:
                        act.activation(z, t2[:, c % 2], ACT.Copy, scale=par[:, 0, g_row + c:g_row + c + 1]
                                       ).then_inc(z_ready, 1)
                    else:
                        act.activation(z, t2[:, c % 2], ACT.Identity, scale=par[:, 0, g_row + c:g_row + c + 1],
                                       bias=par[:, 0, b_row + c:b_row + c + 1]).then_inc(z_ready, 1)
                    act.wait_ge(z_ready, KC * n + c + 1)
                    if keep:
                        if c >= 2:
                            act.wait_ge(keep_mm, c - 1)
                        act.activation(zz[:, c % 2], z, ACT.Square).then_inc(sq_done, 1)
                    else:
                        act.activation(xh[:, c], z, ACT.Copy).then_inc(xh_ready, 1)
                    if memory is not None and c in (1, 4, 7):
                        memory((c + 2) // 3)

            def squares(u, k, n):
                for j in range(2):
                    c = k * 2 + j
                    act.wait_ge(y_ready, (c + (KC * min(n, 6) + 1)).v)
                    act.wait_ge(acc_q_done, (c + (9 * min(n, 6))).v)
                    act.activation(t2[:, j:j + 1], X[:, c.at(), :], ACT.Square).then_inc(sq_done, 1)

            def residual(u0, n):
                def body(u, k):
                    done(u, 1)
                    high(u + 2)
                    squares(u, k, n)
                for k in range(3):
                    body(Lin(u0 + k), Lin(k))
                squares(Lin(u0 + 3), Lin(3), n)
                done(Lin(u0 + 3), 1)
                high(Lin(u0 + 5))

            def skip(u, k):
                done(u, 1)
                high(u + 2)

            def memory(layer):
                for b in range(4):
                    act.wait_ge(mt_done, 4 * layer + b + 1)
                    act.activation(mh[:, 2 * b:2 * b + 2, :], ps[:, 4 + b].rearrange("p (k t) -> p k t", k=2), ACT.Copy
                                   ).then_inc(mh_done, 1)

            def after_attention(layer):
                n0 = n = 3 * layer
                u0 = U_WO[layer]
                for k in range(2):
                    done(Lin(u0 + k), 1)
                    high(Lin(u0 + k + 2))
                    squares(Lin(u0 + k), Lin(k), n)
                memory(layer)
                done(Lin(u0 + 2), 1)
                high(Lin(u0 + 4))
                squares(Lin(u0 + 2), Lin(2), n)
                squares(Lin(u0 + 3), Lin(3), n)
                done(Lin(u0 + 3), 1)
                high(Lin(u0 + 5))
                u0 = U_MEM[layer]

                def memory_unit(k):
                    u = Lin(u0 + k)
                    done(u, 1)
                    high(u + 2)
                    for j in range(2 if k < 4 else 0):
                        act.activation(x_k[:, 2 * k + j], bank(u, j)[:, 0:M], ACT.Copy).then_inc(drained[slot_of(u)], 1)

                norm(n, R_LNG + 8 * n, R_LNB + 8 * n, memory=memory_unit)
                for k in range(4, 8):
                    memory_unit(k)

                def queries(u, k):
                    done(u, 1)
                    high(u + 2)
                    for j in range(2):
                        act.activation(x_q[:, (k * 2 + j).at(), :], ps[:, 2 * slot_of(u) + j:2 * slot_of(u) + j + 1],
                                       ACT.Copy).then_inc(drained[slot_of(u)], 1)

                over(act, U_MQ[layer], 4, queries)
                for i in range(TT + 2):
                    if i < TT:
                        n = TT * layer + i
                        act.wait_ge(x_negm, n + 1)
                        if i >= 2:
                            act.wait_ge(x_tr, n - 1)
                        for h in range(4):
                            act.activation(x_e[:, i % 2, h * M:(h + 1) * M],
                                           flat[:, 2048 + 1024 * (i % 2) + h * M:2048 + 1024 * (i % 2) + (h + 1) * M],
                                           ACT.Exp, bias=negm[:, i % 2, h:h + 1], scale=1 / 16,
                                           accum_out=sums[:, i % 2, h:h + 1]).then_inc(x_exp, 1)
                    if i >= 2:
                        n = TT * layer + i - 2
                        act.wait_ge(x_tr, n + 1)
                        s = 1024 * (i % 2)
                        act.activation(x_pt[:, :, (i - 2) * P:(i - 1) * P],
                                       flat[:, s:s + 1024].rearrange("p (k q) -> p k q", k=8), ACT.Copy
                                       ).then_inc(x_ptr, 1)
                for c in range(KC):
                    act.wait_ge(x_pv, KC * layer + c + 1)
                    act.activation(ah[:, c], ps[:, 4 + c % 4], ACT.Copy).then_inc(x_ah, 1)
                residual(U_MO[layer], n0 + 1)
                norm(n0 + 1, R_LNG + 8 * (n0 + 1), R_LNB + 8 * (n0 + 1))

                u0, f0 = U_FF[layer], 0
                for part, width in enumerate(HIDDEN_PARTS):
                    def hidden(u, k):
                        s, b = slot_of(u), k.base % 2
                        w1 = par[:, 1 + layer, bass.ds((k + (FF // P + f0)).v, 1)]
                        bias = par[:, 1 + layer, bass.ds((k + (R_CONVB + f0)).v, 1)]
                        done(u, 0)
                        act.activation(f_c[:, b], bank(u, 0), ACT.Identity, scale=w1, bias=bias).then_inc(f_cd, 1)
                        done(u, 1)
                        high(u + 2)
                        act.wait_ge(drained[s], (u.half() * 2 + 1).v)
                        act.activation(f_g[:, b], f_c[:, b], ACT.Gelu).then_inc(f_gd, 1)
                        act.wait_ge(drained[s], (u.half() * 2 + 2).v)
                        act.activation(ah[:, k.at(), :], f_y[:, b:b + 1], ACT.Copy).then_inc(f_hh, 1)
                    over(act, u0, width, hidden)
                    if part < 2:
                        over(act, u0 + width, 4, skip)
                    else:
                        residual(u0 + width, n0 + 2)
                    u0, f0 = u0 + width + 4, f0 + width
                norm(n0 + 2, R_LNG + 8 * (n0 + 2), R_LNB + 8 * (n0 + 2), keep=layer == 1)

            after_attention(0)
            act.wait_ge(xl_ready, 4 * KC)
            with act.Fori(0, 2) as i:
                dil_group(Lin(0, 2, i))
                dil_group(Lin(1, 2, i))
            after_attention(1)

            norm(6, R_GMIX)

            def unit(u, dst, func=ACT.Copy, scale=1.0):
                done(Lin(u), 1)
                high(Lin(u + 2))
                copy_out(Lin(u), dst, func, scale)

            def pairs_of(x):
                return lambda j: x[:, 2 * j:2 * j + 2, :].rearrange("p t n -> p (t n)")

            unit(U_QI, lambda j: i_q[:, j])
            s = U_SM % 2
            done(Lin(U_SM), 0)
            act.activation(sm_t[0:80, :], ps[0:80, 2 * s, :], ACT.Copy).then_inc(sm_done, 1)
            done(Lin(U_SM), 1)
            high(Lin(U_SM + 2))
            act.activation(i_k[:], ps[:, 2 * s + 1], ACT.Copy).then_inc(drained[s], 1)
            act.sem_inc(drained[s], 1)
            act.wait_ge(wi_tr, 1)
            act.activation(wi_row, ps[:, 4, 0:32].rearrange("p (t n) -> p t n", t=TT), ACT.Copy, scale=1 / 16
                           ).then_inc(wi_s, 1)
            for m in range(8 * (TT - 1)):
                i = m // 8 + 1
                act.wait_ge(i_qk, m + 1)
                if m >= 2:
                    act.wait_ge(i_acc, m - 1)
                act.activation(i_r[:, m % 2, 0:P * (i + 1)], ps[:, 4 + m % 4, 0:P * (i + 1)], ACT.Relu
                               ).then_inc(i_relu, 1)
            unit(U_QA, lambda j: g_q[:, j], scale=1 / 8)
            unit(U_KA, pairs_of(g_k))
            for k in range(2):
                u = Lin(U_VA + k)
                done(u, 1)
                high(u + 2)
                for j in range(2):
                    act.activation(g_v[:, 2 * j:2 * j + 2, k * UC:(k + 1) * UC],
                                   bank(u, j).rearrange("p (t n) -> p t n", t=2), ACT.Copy
                                   ).then_inc(drained[slot_of(u)], 1)
            for k in range(2):
                unit(U_RA + k, lambda j: g_r[:, 2 * k + j], ACT.Silu)
            for j in range(2):
                act.wait_ge(g_z, j + 1)
                act.activation(pairs_of(g_d)(j), ps[:, 4 + j], ACT.Abs).then_inc(g_abs, 1)
            for j in range(2):
                act.wait_ge(g_abs, 1 + j)
                act.activation(pairs_of(g_d)(j), pairs_of(g_d)(j), ACT.Exp, scale=-1.0).then_inc(g_abs, 1)
            for j in range(2):
                act.wait_ge(g_abs, 3 + j)
                act.activation(pairs_of(g_d)(j), pairs_of(g_d)(j), ACT.Ln, bias=ones[:, 0:1]).then_inc(g_abs, 1)
            unit(U_QB, lambda j: s_q[:, j])
            for j in range(2):
                act.wait_ge(g_lat, j + 1)
                act.activation(pairs_of(g_d)(j), ps[:, 6 + j], ACT.Exp).then_inc(g_ex, 1)
            act.wait_ge(g_tot, 1)
            for j in range(2):
                act.activation(g_dec[:, j], ps[:, 4 + j, 0:8], ACT.Exp, scale=1 / 16).then_inc(g_ex, 1)
            unit(U_QB + 1, lambda j: s_q[:, 2 + j])
            unit(U_KB, lambda j: s_k[:, j])

            def gla_squares(h):
                act.wait_ge(g_o, h + 1)
                if h >= 2:
                    act.wait_ge(g_ll, h - 1)
                act.activation(zz[:, h % 2], ps[:, 4 + h], ACT.Copy).then_inc(g_sq, 1)
                act.activation(t2[:, h % 2], ps[:, 4 + h], ACT.Square).then_inc(g_sq, 1)

            def gla_rstd(h):
                act.wait_ge(g_st_mm, h + 1)
                if h >= 1:
                    act.wait_ge(g_ln, 2 * h)
                act.activation(mean[:], ps[:, 4 + h], ACT.Ln, bias=eps_rms).then_inc(g_ln, 1)
                act.wait_ge(g_ln, 2 * h + 1)
                if h >= 1:
                    act.wait_ge(g_n, h)
                act.activation(rstd[:], mean[:], ACT.Exp, scale=-0.5).then_inc(g_ln, 1)

            def gla_high(h):
                act.wait_ge(g_y, h + 1)
                act.activation(gh[:, h], zz[:, h % 2], ACT.Copy).then_inc(g_hh, 1)

            gla_squares(0)
            gla_squares(1)
            act.wait_ge(g_o, TT)
            for s in range(2):
                act.wait_ge(drained[s], (U_QB + s) // 2 * 2 + 2)
            act.activation(q_n4[:, 0], s_q[:], ACT.Square).then_inc(q_sq, 1)
            unit(U_KB + 1, lambda j: s_k[:, 2 + j])
            gla_rstd(0)
            gla_rstd(1)
            for s in range(2):
                act.wait_ge(drained[s], (U_KB + s) // 2 * 2 + 2)
            act.activation(q_n4[:, 1], s_k[:], ACT.Square).then_inc(q_sq, 1)
            for h in range(2):
                gla_high(h)
                gla_squares(h + 2)
            done(Lin(U_VB), 1)
            high(Lin(U_VB + 2))
            gla_rstd(2)
            gla_rstd(3)
            gla_high(2)
            gla_high(3)
            for k in range(2):
                u = Lin(U_VB + k)
                if k == 1:
                    done(u, 1)
                    high(u + 2)
                for j in range(2):
                    act.activation(s_v[:, 2 * j:2 * j + 2, k * UC:(k + 1) * UC],
                                   bank(u, j).rearrange("p (t n) -> p t n", t=2), ACT.Copy
                                   ).then_inc(drained[slot_of(u)], 1)

            for n in range(2):
                act.wait_ge(q_mm, 4 * n + 4)
                act.activation(q_n4[:, n], ps[:, 4 - 4 * n:8 - 4 * n], ACT.Ln, bias=eps_rms).then_inc(q_ln, 1)
            for n in range(2):
                act.wait_ge(q_ln, n + 1)
                act.activation(q_n4[:, n], q_n4[:, n], ACT.Exp, scale=-0.5).then_inc(q_ln, 1)
            ITEMS = 8 * TT
            for l in range(ITEMS + LAG + 2):
                if LAG <= l < ITEMS + LAG:
                    n = l - LAG
                    w = P * (n % TT + 1)
                    act.wait_ge(s_tr, n + 1)
                    if n >= 2:
                        act.wait_ge(s_pv, n - 1)
                    act.activation(s_pt[:, n % 2, 0:w], ps[:, 6 + n % 2, 0:w], ACT.Copy).then_inc(s_ptr, 1)
                if l < ITEMS:
                    w = P * (l % TT + 1)
                    act.wait_ge(s_negm, l + 1)
                    if l > LAG:
                        act.wait_ge(s_tr, l - LAG)
                    act.activation(s_e[:, l % (LAG + 1), 0:w], s_t[:, l % 2, 0:w], ACT.Exp, bias=negm[:, l % 2, 0:1],
                                   scale=0.125, accum_out=sums[:, l % 2, 0:1]).then_inc(s_exp, 1)
                if l >= LAG + 9 and (l - LAG - 9) % 8 == 0:
                    c = (l - LAG - 9) // 8
                    act.wait_ge(s_pv, 8 * c + 8)
                    act.activation(sh[:, c], ps[:, c % 2], ACT.Copy).then_inc(s_hh, 1)

            def gate(u, k, dst):
                done(u, 1)
                half = u.step == 0 and u.base + 2 >= U_BR
                high(u + 2, P if half else UC)
                for j in range(2):
                    act.activation(dst[:, (k * 2 + j).at(), :], ps[:, 2 * slot_of(u) + j:2 * slot_of(u) + j + 1],
                                   ACT.Sigmoid).then_inc(drained[slot_of(u)], 1)

            over(act, U_GA, 4, lambda u, k: gate(u, k, gate_a))
            over(act, U_GB, 4, lambda u, k: gate(u, k, gate_b))

            def branch(u, k, n=P):
                done(u, 1)
                high(u + 2, n)
                act.wait_ge(b_sum, (k + 1).v)
                act.activation(xh[:, k.at(), :], zz[:, k.base % 2:k.base % 2 + 1, :], ACT.Copy).then_inc(xh_ready, 1)

            over(act, U_BR, KC - 2, branch)
            for k in range(KC - 2, KC):
                branch(Lin(U_BR + k), Lin(k), UC)
            residual(U_OUT, 7)
            norm(7, R_GFFN)

            s = U_RT % 2
            done(Lin(U_RT), 0)
            act.activation(rt_t[:], ps[0:36, 2 * s, :], ACT.Copy).then_inc(rt_cp, 1)
            done(Lin(U_RT), 1)
            high(Lin(U_RT + 2))
            act.sem_inc(drained[s], 1)
            act.wait_ge(r_step, 6)
            act.activation(m_oh[:, 2], m_oh[:, 1], ACT.Exp).then_inc(r_act, 1)
            act.wait_ge(r_step, 20)
            act.activation(m_g[:, 7], m_g[:, 6], ACT.Exp).then_inc(r_act, 1)

            def expert(u, e):
                s, b = slot_of(u), e.base % 2
                done(u, 0)
                act.activation(f_g[:, b], bank(u, 0), ACT.Silu).then_inc(drained[s], 1)
                done(u, 1)
                high(u + 2)
                act.wait_ge(m_y, (e + 1).v)
                act.activation(ah[:, Lin(e.base % 8, e.step, e.reg).at(), :], f_y[:, b:b + 1], ACT.Copy).then_inc(m_hh, 1)

            for part in range(EXPERTS // PART_EXPERTS):
                u0, e0 = U_EX + part * (PART_EXPERTS + 4), part * PART_EXPERTS
                if part == 0:
                    for k in range(2):
                        s = (u0 + k) % 2
                        done(Lin(u0 + k), 0)
                        act.activation(f_g[:, k], ps[:, 2 * s], ACT.Silu).then_inc(drained[s], 1)
                        done(Lin(u0 + k), 1)
                        high(Lin(u0 + k + 2))
                    act.wait_ge(cw_tr, 1)
                    act.activation(m_cwt[:], ps[0:EXPERTS, 4, :], ACT.Copy).then_inc(cw_cp, 1)
                    act.wait_ge(cw_cp, 1)
                    act.dma_start(scratch, m_cwt[:]).then_inc(cw_out, 16)
                    for k in range(2):
                        act.wait_ge(m_y, k + 1)
                        act.activation(ah[:, k], f_y[:, k], ACT.Copy).then_inc(m_hh, 1)
                    over(act, u0 + 2, PART_EXPERTS - 2, lambda u, k: expert(u, k + 2), peel=0)
                else:
                    over(act, u0, PART_EXPERTS, lambda u, k: expert(u, k + e0))
                over(act, u0 + PART_EXPERTS, 4, skip)
            for c in range(KC):
                act.wait_ge(o_tr, c + 1)
                act.activation(orow[:, :, c * P:(c + 1) * P], ps[:, 4 + c % 4].rearrange("p (t n) -> p t n", t=TT),
                               ACT.Copy).then_inc(o_cp, 1)

        @block.vector
        def _(dve):
            def bank(u, j):
                return ps[:, 2 * slot_of(u) + j]

            def done(u, j):
                dve.wait_ge(chunk_done, (u * 2 + (j + 1)).v)

            def own(sem_, value):
                dve.wait_ge(sem_, value.v if isinstance(value, Lin) else value)

            dve.sem_inc(d_scored, 8)
            dve.sem_inc(l_scored, 8)
            for ahead in (d_on, al_ready, l_al):
                dve.sem_inc(ahead, 1)
            dve.memset(ones[:], 1.0).then_inc(ones_set, 1)
            dve.memset(eps_ln, LN_EPS).then_inc(ones_set, 1)
            dve.memset(eps_rms, RMS_EPS).then_inc(ones_set, 1)
            dve.wait_ge(lam_in, 16)
            for n in range(2):
                dve.tensor_tensor(lamb[:, 2 * n, :], lamb[:, 2 * n, :], lamb[:, 2 * n + 1, :], ALU.mult).then_inc(lam_d, 1)
            own(lam_d, 2)
            for n in range(2):
                dve.reduce_sum(lam_s[:, n:n + 1], lamb[:, 2 * n, :], axis=AX_X).then_inc(lam_d, 1)
            dve.wait_ge(lam_x, 1)
            dve.tensor_tensor(neglam, lam_e[:, 1:2], lam_e[:, 0:1], ALU.subtract).then_inc(lam_d, 1)
            own(lam_d, 5)
            dve.tensor_scalar(neglam, neglam, LAMBDA_INIT, None, ALU.subtract).then_inc(lam_d, 1)
            for c in range(KC):
                dve.wait_ge(xh_ready, c + 1)
                dve.tensor_tensor(xl[:, c], ps[:, c % 4], xh[:, c].bitcast(F32), ALU.subtract).then_inc(xl_ready, 1)
            own(lam_d, 6)

            def diff_group(g):
                u = g * 3 + 2
                for j in range(2):
                    done(u, j)
                    dve.tensor_copy(d_v[:, 2 * j:2 * j + 2, :], bank(u, j).rearrange("p (t n) -> p t n", t=2)
                                    ).then_inc(drained[slot_of(u)], 1)
                for l in range(8 + LAG + 5):
                    if l < 8:
                        n = g * 8 + l
                        hh, i, b = l // 4, l % 4, l % 2
                        h = g * 2 + hh
                        dve.wait_ge(d_qk, (n * 2 + 2).v)
                        if i == 0:
                            dve.wait_ge(dbias_in[hh], (h.half() * 16 + 16).v)
                        dve.memset(idle, 0.0)
                        for c in range(2):
                            dve.tensor_tensor_reduce(d_t[:, b, c], ps[:, 4 + 2 * b + c],
                                                     d_bias[:, hh, ZC - P * i:ZC - P * i + T], 1.0, TAKEN,
                                                     ALU.add, ALU.max, accum_out=mx[:, b, c:c + 1]
                                                     ).then_inc(d_scored, 1)
                        own(d_scored, n * 2 + 10)
                        dve.tensor_scalar(negm[:, b, 0:2], mx[:, b, 0:2], -0.125, None, ALU.mult).then_inc(d_negm, 1)
                    if 1 <= l <= 8:
                        n = g * 8 + (l - 1)
                        b = (l - 1) % 2
                        dve.wait_ge(d_exp, (n * 2 + 2).v)
                        dve.reciprocal(rec[:, b, 0:2], sums[:, b, 0:2]).then_inc(d_rec, 1)
                        own(d_rec, n * 2 + 1)
                        dve.tensor_scalar(rec[:, b, 1:2], rec[:, b, 1:2], neglam, None, ALU.mult).then_inc(d_rec, 1)
                        e0 = d_e[:, (l - 1) % (LAG + 1)]
                        dve.tensor_scalar(e0, e0, rec[:, b, 0:1], None, ALU.mult).then_inc(d_half, 1)
                        own(d_rec, n * 2 + 2)
                        own(d_half, n + 1)
                        dve.scalar_tensor_tensor(out=e0, in0=d_e1[:, b], scalar=rec[:, b, 1:2], in1=e0,
                                                 op0=ALU.mult, op1=ALU.add).then_inc(d_mix, 1)
                    if l in (LAG + 7, LAG + 11):
                        h = g * 2 + (l - LAG - 7) // 4
                        dve.wait_ge(d_ln, (h * 2 + 3).v)
                        dve.wait_ge(d_z, (h + 1).v)
                        dve.tensor_tensor(t2[:, 0], d_o[:], rstd[:], ALU.mult).then_inc(d_on, 1)
                    if l in (LAG + 8, LAG + 12):
                        h = g * 2 + (l - LAG - 8) // 4
                        dve.wait_ge(ah_ready, (h + 1).v)
                        dve.tensor_tensor(al[:, h.at(), :], zz[:, 0:1, :], ah[:, h.at(), :].bitcast(F32),
                                          ALU.subtract).then_inc(al_ready, 1)

            with dve.Fori(0, 2) as i:
                diff_group(Lin(0, 2, i))
                diff_group(Lin(1, 2, i))

            def dil_group(g):
                for p in range(3):
                    u = g * 9 + (U_ATT[1] + 3 * p + 2)
                    for j in range(2):
                        done(u, j)
                        dve.tensor_copy(l_v[:, p, 2 * j:2 * j + 2, :], bank(u, j).rearrange("p (t n) -> p t n", t=2)
                                        ).then_inc(drained[slot_of(u)], 1)
                for l in range(16 + LAG + 2):
                    if l < 16:
                        n = g * 16 + l
                        hh, j, b = l // 4, l % 4, l % 2
                        h = g * 4 + hh
                        if j == 0:
                            dve.wait_ge(lbias_in[hh % 2], (g * 32 + (16 * (hh // 2) + 16)).v)
                        dve.wait_ge(l_qk, (n + 1).v)
                        dve.memset(idle, 0.0)
                        dve.tensor_tensor_reduce(l_t[:, b, 0:T], ps[:, 4 + 2 * b], l_bias[:, hh % 2, 3 - j:3 - j + T],
                                                 1.0, TAKEN, ALU.add, ALU.max, accum_out=mx[:, b, 0:1]
                                                 ).then_inc(l_scored, 1)
                        dve.tensor_tensor_reduce(l_t[:, b, T:768], ps[:, 5 + 2 * b, 0:256], l_bias[:, hh % 2, 515:DILW],
                                                 1.0, TAKEN, ALU.add, ALU.max, accum_out=mx[:, b, 1:2]
                                                 ).then_inc(l_scored, 1)
                        own(l_scored, n * 2 + 10)
                        dve.tensor_scalar(negm[:, b, 0:1], mx[:, b, 0:1], mx[:, b, 1:2], -0.125, ALU.max, ALU.mult
                                          ).then_inc(l_negm, 1)
                    if 1 <= l <= 16:
                        n = g * 16 + (l - 1)
                        b = (l - 1) % 2
                        dve.wait_ge(l_exp, (n + 1).v)
                        dve.reciprocal(rec[:, b, 0:1], sums[:, b, 0:1]).then_inc(l_rec, 1)
                        own(l_rec, n + 1)
                        dve.tensor_scalar(l_e[:, (l - 1) % (LAG + 1)], l_e[:, (l - 1) % (LAG + 1)], rec[:, b, 0:1], None, ALU.mult).then_inc(l_mix, 1)
                    if l in (LAG + 9, LAG + 17):
                        c = g * 2 + (l - LAG - 9) // 8
                        dve.wait_ge(l_ah, (c + 1).v)
                        dve.tensor_tensor(al[:, c.at(), :].rearrange("p c (u j) -> p c j u", j=4),
                                          ps[:, 2:3].rearrange("p c (j u) -> p c j u", j=4),
                                          ah[:, c.at(), :].bitcast(F32).rearrange("p c (u j) -> p c j u", j=4),
                                          ALU.subtract).then_inc(l_al, 1)

            def update(u, k, first, n=None):
                s = slot_of(u)
                for j in range(2):
                    c = k * 2 + j
                    done(u, j)
                    xc, psum = X[:, c.at(), :], ps[:, 2 * s + j:2 * s + j + 1]
                    if first:
                        dve.scalar_tensor_tensor(out=xc, in0=xh[:, c.at(), :].bitcast(F32), scalar=ALPHA, in1=psum,
                                                 op0=ALU.mult, op1=ALU.add).then_inc(drained[s], 1)
                        own(drained[s], u.half() * 2 + (j + 1))
                        last = dve.scalar_tensor_tensor(out=xc, in0=xl[:, c.at(), :].bitcast(F32), scalar=ALPHA,
                                                        in1=xc, op0=ALU.mult, op1=ALU.add)
                        if n is not None:
                            last.then_inc(y_ready, 1)
                    else:
                        dve.tensor_tensor(xc, xc, psum, ALU.add).then_inc(drained[s], 1)
                        if n is not None:
                            own(drained[s], u.half() * 2 + (j + 1))
                            dve.sem_inc(y_ready, 1)
                    if n is not None:
                        own(y_ready, c + (KC * min(n, 6) + 1))
                        if n < 6:
                            own(acc_s_done, c + (9 * n + 1))
                            dve.tensor_tensor(acc_s[:], acc_s[:], xc, ALU.add).then_inc(acc_s_done, 1)
                        dve.wait_ge(sq_done, (c + (KC * n + 1)).v)
                        own(acc_q_done, c + (9 * min(n, 6) + 1))
                        dve.tensor_tensor(acc_q[:], acc_q[:], t2[:, j], ALU.add).then_inc(acc_q_done, 1)

            def clear_sums():
                dve.memset(acc_s[:], 0.0).then_inc(acc_s_done, 1)
                dve.memset(acc_q[:], 0.0).then_inc(acc_q_done, 1)

            def norm(n, rms=False, keep=False):
                event, on_act, on_dve = NORM_AT[n]
                if not rms:
                    dve.wait_ge(ln_act, on_act - 2)
                    dve.tensor_tensor(rstd[:], mean[:], mean[:], ALU.mult).then_inc(ln_dve, 1)
                    own(ln_dve, on_dve - 2)
                    dve.wait_ge(stat_mm, n + 1)
                    dve.scalar_tensor_tensor(out=acc_s[:, 0], in0=rstd[:], scalar=-1.0, in1=ps[:, 5],
                                             op0=ALU.mult, op1=ALU.add).then_inc(ln_dve, 1)
                    own(ln_dve, on_dve - 1)
                    dve.tensor_scalar(acc_s[:], acc_s[:], 0.0, LN_EPS, ALU.max, ALU.add).then_inc(ln_dve, 1)
                if not rms:
                    for c in range(2):
                        dve.tensor_tensor(t2[:, c], X[:, c], mean[:], ALU.subtract).then_inc(cent, 1)
                dve.wait_ge(ln_act, on_act)
                for c in range(KC + 1):
                    if c < KC:
                        if c >= 2:
                            dve.wait_ge(z_ready, KC * n + c - 1)
                        if not rms:
                            if c >= 2:
                                dve.tensor_tensor(t2[:, c % 2], X[:, c], mean[:], ALU.subtract).then_inc(cent, 1)
                            own(cent, KC * n + c + 1)
                            dve.tensor_tensor(t2[:, c % 2], t2[:, c % 2], rstd[:], ALU.mult).then_inc(nrm, 1)
                        else:
                            dve.tensor_tensor(t2[:, c % 2], X[:, c], rstd[:], ALU.mult).then_inc(nrm, 1)
                    e = c - 1
                    if e >= 0 and n in (0, 3):
                        dve.wait_ge(xh_ready, KC * event + e + 1)
                        dve.tensor_tensor(xl[:, e], zz[:, e % 2], xh[:, e].bitcast(F32), ALU.subtract
                                          ).then_inc(xl_ready, 1)

            def after_attention(layer):
                n0 = 3 * layer
                u0 = U_WO[layer]
                clear_sums()
                for k in range(2):
                    update(Lin(u0 + k), Lin(k), True, n0)
                for b in range(4):
                    dve.wait_ge(mh_done, 4 * layer + b + 1)
                    dve.tensor_tensor(ml[:, 2 * b:2 * b + 2, :], ps[:, 4 + b].rearrange("p (k t) -> p k t", k=2),
                                      mh[:, 2 * b:2 * b + 2, :].bitcast(F32), ALU.subtract).then_inc(ml_done, 1)
                for k in range(2, 4):
                    update(Lin(u0 + k), Lin(k), True, n0)
                norm(n0)
                if layer == 1:
                    dve.wait_ge(lbias_in[0], 144)
                    dve.wait_ge(lbias_in[1], 144)
                for k in range(4):
                    u = Lin(U_MEM[layer] + 4 + k)
                    for j in range(2):
                        if j == 0:
                            done(u, 1)
                            dve.tensor_copy(x_v[:, :, k * UC:(k + 1) * UC], bank(u, 0).rearrange("p (t n) -> p t n", t=2)
                                            ).then_inc(drained[slot_of(u)], 1)
                        else:
                            dve.sem_inc(drained[slot_of(u)], 1)
                for i in range(TT + 1):
                    if i < TT:
                        n = TT * layer + i
                        dve.wait_ge(x_qk, n + 1)
                        s = 2048 + 1024 * (i % 2)
                        if n >= 2:
                            dve.wait_ge(x_exp, 4 * (n - 1))
                        dve.tensor_reduce(mx[:, i % 2, 0:4], flat[:, s:s + 1024].rearrange("p (h k) -> p h k", h=4),
                                          AX_X, ALU.max).then_inc(x_max, 1)
                        own(x_max, n + 1)
                        dve.tensor_scalar(negm[:, i % 2, 0:4], mx[:, i % 2, 0:4], -1 / 16, None, ALU.mult
                                          ).then_inc(x_negm, 1)
                    if i >= 1:
                        n = TT * layer + i - 1
                        b = (i - 1) % 2
                        dve.wait_ge(x_exp, 4 * n + 4)
                        dve.reciprocal(rec[:, b, 0:4], sums[:, b, 0:4]).then_inc(x_rec, 1)
                        own(x_rec, n + 1)
                        for h in range(4):
                            dve.tensor_scalar(x_e[:, b, h * M:(h + 1) * M], x_e[:, b, h * M:(h + 1) * M],
                                              rec[:, b, h:h + 1], None, ALU.mult).then_inc(x_mix, 1)
                for c in range(KC):
                    dve.wait_ge(x_ah, KC * layer + c + 1)
                    dve.tensor_tensor(al[:, c], ps[:, 4 + c % 4], ah[:, c].bitcast(F32), ALU.subtract).then_inc(x_al, 1)
                clear_sums()
                over(dve, U_MO[layer], 4, lambda u, k: update(u, k, True, n0 + 1))
                norm(n0 + 1)
                u0, f0 = U_FF[layer], 0
                for part, width in enumerate(HIDDEN_PARTS):
                    def hidden(u, k):
                        F = k + (FF // P * layer + f0)
                        s, b = slot_of(u), k.base % 2
                        w0 = par[:, 1 + layer, bass.ds((k + f0).v, 1)]
                        w2 = par[:, 1 + layer, bass.ds((k + (2 * (FF // P) + f0)).v, 1)]
                        dve.wait_ge(f_cd, (F + 1).v)
                        dve.scalar_tensor_tensor(out=f_c[:, b, 1:T], in0=bank(u, 0)[:, 0:T - 1], scalar=w0,
                                                 in1=f_c[:, b, 1:T], op0=ALU.mult, op1=ALU.add).then_inc(f_left, 1)
                        own(f_left, F + 1)
                        dve.scalar_tensor_tensor(out=f_c[:, b, 0:T - 1], in0=bank(u, 0)[:, 1:T], scalar=w2,
                                                 in1=f_c[:, b, 0:T - 1], op0=ALU.mult, op1=ALU.add
                                                 ).then_inc(drained[s], 1)
                        done(u, 1)
                        dve.wait_ge(f_gd, (F + 1).v)
                        dve.tensor_tensor(f_y[:, b], f_g[:, b], bank(u, 1), ALU.mult).then_inc(drained[s], 1)
                        dve.wait_ge(f_hh, (F + 1).v)
                        dve.tensor_tensor(al[:, k.at(), :], f_y[:, b:b + 1], ah[:, k.at(), :].bitcast(F32), ALU.subtract
                                          ).then_inc(f_hl, 1)
                    over(dve, u0, width, hidden)
                    if part == 2:
                        clear_sums()
                    over(dve, u0 + width, 4, lambda u, k: update(u, k, part == 0, n0 + 2 if part == 2 else None))
                    u0, f0 = u0 + width + 4, f0 + width
                norm(n0 + 2, keep=layer == 1)

            after_attention(0)
            with dve.Fori(0, 2) as i:
                dil_group(Lin(0, 2, i))
                dil_group(Lin(1, 2, i))
            after_attention(1)

            norm(6, rms=True)
            dve.memset(i_m[:, 0, 0:P], 0.0).then_inc(i_edge, 1)
            own(i_edge, 1)
            dve.memset(i_m[0:64, 0, 64:P], MASKED).then_inc(i_edge, 1)
            dve.wait_ge(wi_s, 1)
            for m in range(8 * (TT - 1)):
                i, h = m // 8 + 1, m % 8
                w = P * (i + 1)
                dve.wait_ge(i_relu, m + 1)
                if h == 0:
                    dve.tensor_scalar(i_m[:, i, 0:w], i_r[:, m % 2, 0:w], wi_row[:, i, h:h + 1], None, ALU.mult
                                      ).then_inc(i_acc, 1)
                else:
                    own(i_acc, m)
                    dve.scalar_tensor_tensor(out=i_m[:, i, 0:w], in0=i_r[:, m % 2, 0:w], scalar=wi_row[:, i, h:h + 1],
                                             in1=i_m[:, i, 0:w], op0=ALU.mult, op1=ALU.add).then_inc(i_acc, 1)
                if h == 7:
                    own(i_acc, m + 1)
                    dve.memset(i_m[0:64, i, w - 64:w], MASKED).then_inc(i_edge, 1)
            ROUNDS = TOPK // 8
            own(i_edge, 2)
            dve.tensor_copy(idle, ones[:, 0:1]).then_inc(i_mask, 1)
            for i in range(1, TT):
                w = P * (i + 1)
                row = i_m[:, i, 0:w]
                own(i_edge, i + 2)
                for r in range(ROUNDS):
                    n = (i - 1) * ROUNDS + r
                    own(i_cut, n)
                    dve.max(m8, row).then_inc(i_max, 1)
                    own(i_max, n + 1)
                    dve.match_replace(row, m8, row, TAKEN).then_inc(i_cut, 1)
                own(i_cut, i * ROUNDS)
                dve.tensor_scalar(row, row, -2e38, MASKED, ALU.is_gt, ALU.mult).then_inc(i_mask, 1)

            for j in range(2):
                dve.wait_ge(g_abs, 5 + j)
                dve.scalar_tensor_tensor(out=g_a[:, 2 * j:2 * j + 2, :], in0=ps[:, 4 + j].rearrange("p (t n) -> p t n", t=2),
                                         scalar=0.0, in1=g_d[:, 2 * j:2 * j + 2, :], op0=ALU.min, op1=ALU.subtract
                                         ).then_inc(g_la, 1)
            for j in range(2):
                dve.wait_ge(g_ex, j + 1)
                half = slice(2 * j, 2 * j + 2)
                dve.tensor_tensor(g_d[:, half, :], g_d[:, half, :], g_k[:, half, :], ALU.mult).then_inc(g_kd, 1)
            dve.wait_ge(g_ex, 4)
            for p in range(2):
                dve.wait_ge(g_u, p + 1)
                for c in range(8):
                    gain = ps[:, 4 + 2 * p + c % 2, c // 2 * P:(c // 2 + 1) * P]
                    if c == 0:
                        dve.tensor_copy(g_st[:, p, 0], gain).then_inc(g_state, 1)
                    else:
                        own(g_state, 8 * p + c)
                        dve.scalar_tensor_tensor(out=g_st[:, p, c], in0=g_st[:, p, c - 1],
                                                 scalar=g_dec[:, c % 2, p * 4 + c // 2:p * 4 + c // 2 + 1], in1=gain,
                                                 op0=ALU.mult, op1=ALU.add).then_inc(g_state, 1)

            def gla_scale(h):
                dve.wait_ge(g_ln, 2 * h + 2)
                z = zz[:, h % 2]
                dve.tensor_tensor(z, z, rstd[:], ALU.mult).then_inc(g_n, 1)
                own(g_n, h + 1)
                dve.scalar_tensor_tensor(out=z, in0=z, scalar=par[:, 0, R_GGLA:R_GGLA + 1], in1=g_r[:, h],
                                         op0=ALU.mult, op1=ALU.mult).then_inc(g_y, 1)

            def gla_low(h):
                dve.wait_ge(g_hh, h + 1)
                dve.tensor_tensor(gl[:, h], zz[:, h % 2], gh[:, h].bitcast(F32), ALU.subtract).then_inc(g_ll, 1)

            for first in (0, 2):
                for h in (first, first + 1):
                    gla_scale(h)
                gla_low(first)
                gla_low(first + 1)

            for n in range(8):
                if n % 4 == 0:
                    dve.wait_ge(q_ln, 3 + n // 4)
                x, row = ((s_q, R_GQ), (s_k, R_GK))[n // 4]
                dve.scalar_tensor_tensor(out=x[:, n % 4], in0=x[:, n % 4], scalar=par[:, 0, row:row + 1],
                                         in1=q_n4[:, n // 4, n % 4], op0=ALU.mult, op1=ALU.mult).then_inc(q_n, 1)
            ITEMS = 8 * TT
            for l in range(ITEMS + LAG + 3):
                if l < ITEMS:
                    b, w = l % 2, P * (l % TT + 1)
                    dve.wait_ge(s_qk, l + 1)
                    dve.wait_ge(s_bm, l + 1)
                    if l >= 2:
                        dve.wait_ge(s_exp, l - 1)
                    dve.memset(idle, 0.0)
                    dve.tensor_tensor_reduce(s_t[:, b, 0:w], ps[:, 4 + b, 0:w], s_b[:, b, 0:w], 1.0, TAKEN, ALU.add,
                                             ALU.max, accum_out=mx[:, b, 0:1]).then_inc(s_scored, 1)
                    own(s_scored, l + 1)
                    dve.tensor_scalar(negm[:, b, 0:1], mx[:, b, 0:1], -0.125, None, ALU.mult).then_inc(s_negm, 1)
                if 1 <= l <= ITEMS:
                    n = l - 1
                    b, w = n % 2, P * (n % TT + 1)
                    dve.wait_ge(s_exp, n + 1)
                    dve.reciprocal(rec[:, b, 0:1], sums[:, b, 0:1]).then_inc(s_rec, 1)
                    own(s_rec, n + 1)
                    dve.tensor_scalar(s_e[:, n % (LAG + 1), 0:w], s_e[:, n % (LAG + 1), 0:w], rec[:, b, 0:1], None, ALU.mult).then_inc(s_mix, 1)
                if l >= LAG + 10 and (l - LAG - 10) % 8 == 0:
                    c = (l - LAG - 10) // 8
                    dve.wait_ge(s_hh, c + 1)
                    dve.tensor_tensor(sl[:, c], ps[:, c % 2], sh[:, c].bitcast(F32), ALU.subtract).then_inc(s_ll, 1)

            def branch(u, k):
                s, b = slot_of(u), k.base % 2
                for j in range(2):
                    done(u, j)
                    dve.tensor_tensor(t2[:, j:j + 1], (gate_a, gate_b)[j][:, k.at(), :],
                                      ps[:, 2 * s + j:2 * s + j + 1], ALU.mult).then_inc(drained[s], 1)
                own(drained[s], u.half() * 2 + 2)
                dve.tensor_tensor(zz[:, b], t2[:, 0], t2[:, 1], ALU.add).then_inc(b_sum, 1)
                dve.wait_ge(xh_ready, (k + (KC * MIXED + 1)).v)
                dve.tensor_tensor(xl[:, k.at(), :], zz[:, b:b + 1], xh[:, k.at(), :].bitcast(F32), ALU.subtract
                                  ).then_inc(xl_ready, 1)

            over(dve, U_BR, KC, branch)
            dve.memset(acc_q[:], 0.0).then_inc(acc_q_done, 1)
            over(dve, U_OUT, 4, lambda u, k: update(u, k, False, 7))
            norm(7, rms=True)

            dve.wait_ge(rb_in, 32)
            done(Lin(U_RT), 1)
            dve.tensor_tensor(m_lg[:], bank(Lin(U_RT), 1)[:, 0:TT * 36].rearrange("p (t n) -> p t n", t=TT),
                              m_rb[:].unsqueeze(1).to_broadcast([P, TT, 36]), ALU.add).then_inc(drained[U_RT % 2], 1)
            own(drained[U_RT % 2], U_RT + 2)
            idx = idx8.rearrange("p (t n) -> p t n", n=PER_GROUP)[:, 0:TT, :]
            groups = m_lg[:, :, EXPERTS:36]

            def over_last(x, n):
                return x.unsqueeze(2).to_broadcast([P, TT, n])

            def first_of(value, hot, best, low, n, at_step):
                if at_step:
                    own(r_step, at_step)
                dve.tensor_reduce(best, value, AX_X, ALU.max).then_inc(r_step, 1)
                own(r_step, at_step + 1)
                dve.tensor_tensor(hot, value, over_last(best, n), ALU.is_equal).then_inc(r_step, 1)
                own(r_step, at_step + 2)
                dve.scalar_tensor_tensor(out=hot, in0=hot, scalar=-64.0, in1=idx[:, :, 0:n], op0=ALU.mult, op1=ALU.add
                                         ).then_inc(r_step, 1)
                own(r_step, at_step + 3)
                dve.tensor_reduce(low, hot, AX_X, ALU.min).then_inc(r_step, 1)
                own(r_step, at_step + 4)
                dve.tensor_tensor(hot, hot, over_last(low, n), ALU.is_equal).then_inc(r_step, 1)

            g_hot = m_oh[:, 0]
            first_of(groups, g_hot, m_g[:, 0], m_g[:, 1], GROUPS, 0)
            own(r_step, 5)
            dve.tensor_tensor(m_oh[:, 1], groups, over_last(m_g[:, 0], GROUPS), ALU.subtract).then_inc(r_step, 1)
            logits = m_lg[:, :, 0:EXPERTS].rearrange("p t (g e) -> p t g e", g=GROUPS)
            hot4 = g_hot.unsqueeze(3).to_broadcast([P, TT, GROUPS, PER_GROUP])
            dve.tensor_tensor(m_tmp[:, 0], logits, hot4, ALU.mult).then_inc(r_step, 1)
            own(r_step, 7)
            dve.tensor_reduce(m_e[:, 0], m_tmp[:, 0].rearrange("p t g e -> p t e g"), AX_X, ALU.add).then_inc(r_step, 1)
            first_of(m_e[:, 0], m_e[:, 1], m_g[:, 4], m_g[:, 1], PER_GROUP, 8)
            own(r_step, 13)
            dve.scalar_tensor_tensor(out=m_e[:, 2], in0=m_e[:, 1], scalar=TAKEN, in1=m_e[:, 0], op0=ALU.mult, op1=ALU.add
                                     ).then_inc(r_step, 1)
            first_of(m_e[:, 2], m_e[:, 3], m_g[:, 5], m_g[:, 1], PER_GROUP, 14)
            own(r_step, 19)
            dve.tensor_tensor(m_g[:, 6], m_g[:, 5], m_g[:, 4], ALU.subtract).then_inc(r_step, 1)
            dve.wait_ge(r_act, 1)
            dve.tensor_reduce(m_g[:, 2], m_oh[:, 2], AX_X, ALU.add).then_inc(r_step, 1)
            own(r_step, 21)
            dve.reciprocal(m_g[:, 3], m_g[:, 2]).then_inc(r_step, 1)
            dve.wait_ge(r_act, 2)
            dve.tensor_scalar(m_g[:, 8], m_g[:, 7], 1.0, None, ALU.add).then_inc(r_step, 1)
            own(r_step, 23)
            dve.reciprocal(m_g[:, 9], m_g[:, 8]).then_inc(r_step, 1)
            own(r_step, 24)
            dve.tensor_tensor(m_g[:, 10], m_g[:, 9], m_g[:, 3], ALU.mult).then_inc(r_step, 1)
            own(r_step, 25)
            dve.tensor_tensor(m_g[:, 11], m_g[:, 10], m_g[:, 7], ALU.mult).then_inc(r_step, 1)
            own(r_step, 26)
            for n, share in ((1, 10), (3, 11)):
                dve.tensor_tensor(m_e[:, n], m_e[:, n], over_last(m_g[:, share], PER_GROUP), ALU.mult).then_inc(r_step, 1)
            own(r_step, 28)
            dve.tensor_tensor(m_e[:, 4], m_e[:, 1], m_e[:, 3], ALU.add).then_inc(r_step, 1)
            own(r_step, 29)
            dve.tensor_tensor(m_cw[:], hot4, m_e[:, 4].unsqueeze(2).to_broadcast([P, TT, GROUPS, PER_GROUP]), ALU.mult
                              ).then_inc(r_step, 1)

            def expert_product(u, e):
                s, b = slot_of(u), e.base % 2
                dve.wait_ge(drained[s], (u.half() * 2 + 1).v)
                done(u, 1)
                if e.base >= 2:
                    own(m_hl, e + -1)
                dve.tensor_tensor(f_y[:, b], f_g[:, b], bank(u, 1), ALU.mult).then_inc(drained[s], 1)

            def expert_weight(u, e):
                s, b = slot_of(u), e.base % 2
                own(drained[s], u.half() * 2 + 2)
                dve.wait_ge(mw_in[b], (e.half() * 16 + 16).v)
                dve.tensor_tensor(f_y[:, b], f_y[:, b], m_w[:, b], ALU.mult).then_inc(m_y, 1)

            def expert_low(e):
                b = e.base % 2
                k = Lin(e.base % 8, e.step, e.reg)
                dve.wait_ge(m_hh, (e + 1).v)
                dve.tensor_tensor(al[:, k.at(), :], f_y[:, b:b + 1], ah[:, k.at(), :].bitcast(F32), ALU.subtract
                                  ).then_inc(m_hl, 1)

            def expert(u, e):
                expert_product(u, e)
                expert_weight(u, e)
                expert_low(e)

            for part in range(EXPERTS // PART_EXPERTS):
                u0, e0 = U_EX + part * (PART_EXPERTS + 4), part * PART_EXPERTS
                if part == 0:
                    for k in range(2):
                        expert_product(Lin(u0 + k), Lin(k))
                    for k in range(2):
                        expert_weight(Lin(u0 + k), Lin(k))
                    for k in range(2):
                        expert_low(Lin(k))
                    over(dve, u0 + 2, PART_EXPERTS - 2, lambda u, k: expert(u, k + 2), peel=0)
                else:
                    over(dve, u0, PART_EXPERTS, lambda u, k: expert(u, k + e0))
                over(dve, u0 + PART_EXPERTS, 4, lambda u, k: update(u, k, False))

        @block.tensor
        def _(pe):
            def begin(u):
                s = slot_of(u)
                pe.wait_ge(lo_done, (u + 1).v)
                if u.base >= 2:
                    pe.wait_ge(drained[s], (u.half() * 2).v)
                return s

            def flip(dst, src):
                return pe.transpose(dst, src, ident)

            def triple(dst, stat_h, stat_l, mov_h, mov_l, first, last):
                pe.matmul(dst, stat_h, mov_h, start=first, stop=False)
                pe.matmul(dst, stat_l, mov_h, start=False, stop=False)
                return pe.matmul(dst, stat_h, mov_l, start=False, stop=last)

            def columns(u, hi, lo, kcs=KC, width=T, ready=None, count=2):
                s = begin(u)

                def product(j, kc):
                    cols = slice(j * P, (j + 1) * P)
                    mm = triple(ps[:, 2 * s + j, 0:width], wh[:, s, kc, cols], wl[:, s, kc, cols],
                                hi[:, kc], lo[:, kc], kc == 0, kc == kcs - 1)
                    if kc == kcs - 1:
                        mm.then_inc(chunk_done, 1)

                if ready:
                    for kc in range(kcs):
                        ready(kc)
                        for j in range(count):
                            product(j, kc)
                else:
                    for j in range(count):
                        for kc in range(kcs):
                            product(j, kc)

            def rows(u, hi, lo, tiles=TT, n=UC, take=None):
                s = begin(u)
                take = take or (lambda x, kc, t: x[:, kc, t * P:(t + 1) * P])
                for t in range(tiles):
                    for kc in range(KC):
                        mm = triple(ps[:, 2 * s + t // 2, (t % 2) * UC:(t % 2) * UC + n],
                                    take(hi, kc, t), take(lo, kc, t), wh[:, s, kc, 0:n], wl[:, s, kc, 0:n],
                                    kc == 0, kc == KC - 1)
                    if t % 2 or tiles == 2:
                        mm.then_inc(chunk_done, 1)

            pe.sem_inc(d_tr, 4)
            pe.sem_inc(l_tr, 4)
            pe.sem_inc(d_pv, 2)
            pe.sem_inc(d_st, 1)
            pe.sem_inc(l_pv, 1)
            pe.wait_ge(x_in, 32)
            for c in range(KC):
                if c >= 4:
                    pe.wait_ge(xl_ready, c - 3)
                for t in range(TT):
                    tr = flip(ps[:, c % 4, t * P:(t + 1) * P], xrows[:, t, c * P:(c + 1) * P])
                tr.then_inc(xt_done, 1)
            pe.wait_ge(p_in, 16 * 14)
            pe.transpose(ps[:, 4, 0:R_GK + 1], prow[0:R_GK + 1, 0, :], ident[0:R_GK + 1, 0:R_GK + 1])
            pe.transpose(ps[:, 4, P:P + 88], prow[0:88, 1, :], ident[0:88, 0:88])
            pe.transpose(ps[:, 4, 2 * P:2 * P + 88], prow[0:88, 2, :], ident[0:88, 0:88]).then_inc(par_t, 1)
            pe.wait_ge(z_in, 32)
            for j in range(2):
                pe.matmul(ps[0:8, 5 + j, :], relb[:], hot[:, j * T:(j + 1) * T], start=True, stop=True).then_inc(z_mm, 1)
            pe.wait_ge(par_s, 3)
            pe.wait_ge(z_cp, 2)
            pe.wait_ge(xl_ready, KC)

            def split_ready(event):
                return lambda kc: pe.wait_ge(xl_ready, KC * event + kc + 1)

            def diff_group(g, first):
                u = g * 3
                s = slot_of(u)
                pe.wait_ge(d_ptr, (g * 8 + 1).v)
                pe.wait_ge(d_ln, (g * 4 + 1).v)
                columns(u, xh, xl, ready=first)
                columns(u + 1, xh, xl)
                rows(u + 2, xh, xl)
                emptied(pe, u + 1)
                emptied(pe, u + 2)
                for l in range(8 + LAG + 3):
                    if l < 8:
                        n = g * 8 + l
                        hh, i, b = l // 4, l % 4, l % 2
                        pe.wait_ge(d_scored, (n * 2 + 6).v)
                        for c in range(2):
                            half = slice(64 * c, 64 * c + 64)
                            pe.matmul(ps[:, 4 + 2 * b + c], d_q[half, hh, i * P:(i + 1) * P], d_k[half, hh, :],
                                      start=True, stop=True).then_inc(d_qk, 1)
                    if LAG <= l < 8 + LAG:
                        n = g * 8 + (l - LAG)
                        b = (l - LAG) % 2
                        pe.wait_ge(d_mix, (n + 1).v)
                        if l >= LAG + 2:
                            pe.wait_ge(d_ptr, n.v)
                        for k in range(TT):
                            tr = flip(ps[:, b, k * P:(k + 1) * P], d_e[:, (l - LAG) % (LAG + 1), k * P:(k + 1) * P])
                        tr.then_inc(d_tr, 1)
                    if l in (LAG + 4, LAG + 8):
                        hh = (l - LAG - 4) // 4
                        h = g * 2 + hh
                        pe.wait_ge(d_ptr, (h * 4 + 4 + 1).v)
                        pe.wait_ge(d_osb, (h * 2 + 1).v)
                        for k in range(TT):
                            mm = pe.matmul(ps[:, 2], d_v[:, k, hh * P:(hh + 1) * P], d_pt[:, hh, k, :],
                                           start=k == 0, stop=k == TT - 1)
                        mm.then_inc(d_pv, 1)
                    if l in (LAG + 6, LAG + 10):
                        h = g * 2 + (l - LAG - 6) // 4
                        pe.wait_ge(d_osb, (h * 2 + 2 + 1).v)
                        pe.wait_ge(d_ln, (h * 2 + 1).v)
                        pe.matmul(ps[:, 3], mean_p, d_sq[:], start=True, stop=True).then_inc(d_st, 1)

            with pe.Fori(0, 2) as i:
                diff_group(Lin(0, 2, i), split_ready(0))
                diff_group(Lin(1, 2, i), None)

            def dil_group(g, first):
                pe.wait_ge(l_ptr, (g * 16 + 1).v)
                pe.wait_ge(l_al, (g * 2 + 1).v)
                for p in range(3):
                    u = g * 9 + (U_ATT[1] + 3 * p)
                    columns(u, xh, xl, ready=first if p == 0 else None)
                    columns(u + 1, xh, xl)
                    rows(u + 2, xh, xl, take=None if p == 0 else
                         lambda x, kc, t: x[:, kc, :].rearrange("p (u j) -> p j u", j=4)[:, t])
                emptied(pe, u + 1)
                emptied(pe, u + 2)

                def of_class(x, p, pb, ch, j):
                    return x[pb:pb + 64, p, ch, :].rearrange("p (u j) -> p j u", j=4)[:, j]

                for l in range(16 + LAG + 1):
                    if l < 16:
                        n = g * 16 + l
                        hh, j, b = l // 4, l % 4, l % 2
                        pb, ch = 64 * (hh % 2), hh // 2
                        pe.wait_ge(l_scored, (n * 2 + 6).v)
                        pe.matmul(ps[:, 4 + 2 * b], of_class(l_q, 0, pb, ch, j), l_k[pb:pb + 64, 0, ch, :],
                                  start=True, stop=True)
                        for p in (1, 2):
                            mm = pe.matmul(ps[:, 5 + 2 * b, (p - 1) * P:p * P], of_class(l_q, p, pb, ch, j),
                                           of_class(l_k, p, pb, ch, j), start=True, stop=True)
                        mm.then_inc(l_qk, 1)
                    if l >= LAG + 4 and (l - LAG) % 4 == 0:
                        hh = (l - LAG - 4) // 4
                        pb = 64 * (hh % 2)
                        pe.wait_ge(l_ptr, (g * 16 + (hh * 4 + 4) + 1).v)
                        if hh == 2:
                            pe.wait_ge(l_al, (g * 2 + 1 + 1).v)
                        cols = slice(64 * hh, 64 * hh + 64)
                        for k in range(TT):
                            pe.matmul(ps[pb:pb + 64, 2, :], l_v[:, 0, k, cols], l_pt[:, k, :], start=k == 0, stop=False)
                        for p in (1, 2):
                            for j in range(4):
                                mm = pe.matmul(ps[pb:pb + 64, 2, j * P:(j + 1) * P], l_v[:, p, j, cols],
                                               l_pt[:, 3 + p, j * P:(j + 1) * P], start=False, stop=p == 2 and j == 3)
                        mm.then_inc(l_pv, 1)
                    if LAG <= l < 16 + LAG:
                        n = g * 16 + (l - LAG)
                        pe.wait_ge(l_mix, (n + 1).v)
                        if l >= LAG + 1:
                            pe.wait_ge(l_ptr, (n + 1).v)
                        for k in range(6):
                            tr = flip(ps[:, k // 4, (k % 4) * P:(k % 4 + 1) * P],
                                              l_e[:, (l - LAG) % (LAG + 1), k * P:(k + 1) * P])
                        tr.then_inc(l_tr, 1)

            def stats(n):
                pe.wait_ge(acc_s_done, 9 * n + 9)
                pe.matmul(ps[:, 4], mean_d, acc_s[:, 0], start=True, stop=True).then_inc(mean_mm, 1)
                pe.wait_ge(acc_q_done, 9 * n + 9)
                pe.matmul(ps[:, 5], mean_d, acc_q[:], start=True, stop=True).then_inc(stat_mm, 1)

            def after_attention(layer):
                n0 = 3 * layer
                u0 = U_WO[layer]
                got = (al_ready, l_al)[layer]
                columns(Lin(u0), ah, al, ready=lambda kc: pe.wait_ge(got, kc + 2))
                columns(Lin(u0 + 1), ah, al)
                pe.wait_ge(m_in, 16 * (layer + 1))
                for b in range(4):
                    for k in range(2):
                        for t in range(2):
                            tr = flip(ps[:, 4 + b, k * M + t * P:k * M + (t + 1) * P],
                                              mrows[:, t, (2 * b + k) * P:(2 * b + k + 1) * P])
                    tr.then_inc(mt_done, 1)
                columns(Lin(u0 + 2), ah, al)
                columns(Lin(u0 + 3), ah, al)
                pe.wait_ge(ml_done, 4 * (layer + 1))
                stats(n0)
                for k in range(4):
                    columns(Lin(U_MEM[layer] + k), mh, ml, width=M)
                for k in range(4):
                    rows(Lin(U_MEM[layer] + 4 + k), mh, ml, tiles=2)
                first = split_ready(n0 + 1)
                over(pe, U_MQ[layer], 4, lambda u, k: columns(u, xh, xl, ready=first if k.base == 0 else None))
                emptied(pe, Lin(U_MQ[layer] + 2))
                emptied(pe, Lin(U_MQ[layer] + 3))
                for i in range(TT + 2):
                    if i < TT:
                        n = TT * layer + i
                        if i >= 2:
                            pe.wait_ge(x_exp, 4 * (n - 1))
                        for h in range(4):
                            for e in range(2):
                                mm = pe.matmul(ps[:, 4 + 2 * (i % 2) + h // 2, (h % 2) * M:(h % 2 + 1) * M],
                                               x_q[:, 2 * h + e, i * P:(i + 1) * P], x_k[:, 2 * h + e, :],
                                               start=e == 0, stop=e == 1)
                        mm.then_inc(x_qk, 1)
                    if i >= 2:
                        n = TT * layer + i - 2
                        b = i % 2
                        pe.wait_ge(x_mix, 4 * n + 4)
                        if i >= 4:
                            pe.wait_ge(x_ptr, n - 1)
                        for k in range(8):
                            tr = flip(ps[:, 2 * b + k // 4, (k % 4) * P:(k % 4 + 1) * P],
                                              x_e[:, b, k * P:(k + 1) * P])
                        tr.then_inc(x_tr, 1)
                pe.wait_ge(x_ptr, TT * (layer + 1))
                for c in range(KC):
                    if c >= 4:
                        pe.wait_ge(x_al, KC * layer + c - 3)
                    for k in range(2):
                        mm = pe.matmul(ps[:, 4 + c % 4], x_v[:, k, c * P:(c + 1) * P], x_pt[:, 2 * (c // 2) + k, :],
                                       start=k == 0, stop=k == 1)
                    mm.then_inc(x_pv, 1)
                over(pe, U_MO[layer], 4, lambda u, k: columns(
                    u, ah, al, ready=(lambda kc: pe.wait_ge(x_al, KC * layer + kc + 1)) if k.base == 0 else None))
                stats(n0 + 1)
                u0, f0 = U_FF[layer], FF // P * layer
                for part, width in enumerate(HIDDEN_PARTS):
                    first = split_ready(n0 + 2) if part == 0 else None
                    over(pe, u0, width, lambda u, k: columns(u, xh, xl, ready=first if k.base == 0 else None))
                    over(pe, u0 + width, 4, lambda u, k: columns(
                        u, ah, al, kcs=width,
                        ready=(lambda kc: pe.wait_ge(f_hl, f0 + kc + 1)) if k.base == 0 else None))
                    u0, f0 = u0 + width + 4, f0 + width
                stats(n0 + 2)

            after_attention(0)
            with pe.Fori(0, 2) as i:
                dil_group(Lin(0, 2, i), split_ready(3))
                dil_group(Lin(1, 2, i), None)
            after_attention(1)

            def square_stats():
                pe.wait_ge(acc_q_done, 9 * 6 + 9)
                pe.matmul(ps[:, 5], mean_d, acc_q[:], start=True, stop=True).then_inc(stat_mm, 1)

            for c in range(KC):
                pe.wait_ge(sq_done, KC * 6 + c + 1)
                pe.matmul(ps[:, 5], mean_d, zz[:, c % 2], start=c == 0, stop=c == KC - 1
                          ).then_inc(keep_mm, 1)
            columns(Lin(U_QI), xh, xl, ready=split_ready(6))
            columns(Lin(U_SM), xh, xl, count=1)
            pe.wait_ge(sm_done, 1)
            pe.matmul(ps[:, 2 * (U_SM % 2) + 1], rep32[0:32, :], sm_t[0:32, :], start=True, stop=True
                      ).then_inc(chunk_done, 1)
            for t in range(TT):
                tr = pe.transpose(ps[:, 4, t * 8:(t + 1) * 8], sm_t[32:40, t * P:(t + 1) * P], ident[32:40, 32:40])
            tr.then_inc(wi_tr, 1)
            pe.wait_ge(wi_s, 1)
            for m in range(8 * (TT - 1)):
                i, h = m // 8 + 1, m % 8
                rows_ = slice(32 * (h % 4), 32 * (h % 4) + 32)
                if m >= 4:
                    pe.wait_ge(i_relu, m - 3)
                pe.matmul(ps[:, 4 + m % 4, 0:P * (i + 1)], i_q[rows_, h // 4, i * P:(i + 1) * P],
                          i_k[rows_, 0:P * (i + 1)], start=True, stop=True).then_inc(i_qk, 1)
            columns(Lin(U_QA), xh, xl)
            rows(Lin(U_KA), xh, xl)
            for k in range(2):
                rows(Lin(U_VA + k), xh, xl)
            for k in range(2):
                columns(Lin(U_RA + k), xh, xl)
            pe.wait_ge(i_relu, 8 * (TT - 1))
            pe.wait_ge(wa_in, 48)
            for t in range(TT):
                mm = pe.matmul(ps[:, 4 + t // 2, (t % 2) * UC:(t % 2 + 1) * UC], sm_t[64:81, t * P:(t + 1) * P],
                               walpha[64:81, :], start=True, stop=True)
                if t % 2:
                    mm.then_inc(g_z, 1)
            columns(Lin(U_QB), xh, xl)
            for t in range(TT):
                pe.wait_ge(g_la, t // 2 + 1)
                mm = pe.matmul(ps[:, 6 + t // 2, (t % 2) * UC:(t % 2 + 1) * UC], later, g_a[:, t, :],
                               start=True, stop=True)
                if t % 2:
                    mm.then_inc(g_lat, 1)
            for b in range(2):
                for p in range(2):
                    for ch in range(TT):
                        part = slice(64 * b, 64 * b + 64)
                        mm = pe.matmul(ps[:, 4 + b, p * 4 + ch:p * 4 + ch + 1], g_a[part, ch, p * P:(p + 1) * P],
                                       ones[part, 0:1], start=True, stop=True)
            mm.then_inc(g_tot, 1)
            columns(Lin(U_QB + 1), xh, xl)
            pe.wait_ge(g_kd, 2)
            pe.wait_ge(g_ex, 4)
            for p in range(2):
                for h in (2 * p, 2 * p + 1):
                    for c in range(8):
                        part = slice(64 * (c % 2), 64 * (c % 2) + 64)
                        mm = pe.matmul(ps[64 * (h % 2):64 * (h % 2) + 64, 4 + 2 * p + c % 2, c // 2 * P:(c // 2 + 1) * P],
                                       g_d[part, c // 2, 64 * h:64 * h + 64], g_v[part, c // 2, P * h:P * (h + 1)],
                                       start=True, stop=True)
                mm.then_inc(g_u, 1)
            columns(Lin(U_KB), xh, xl)
            pe.wait_ge(g_state, 16)
            for h in range(TT):
                part = slice(64 * (h % 2), 64 * (h % 2) + 64)
                for c in range(8):
                    mm = pe.matmul(ps[:, 4 + h, 64 * c:64 * (c + 1)], g_st[part, h // 2, c, :],
                                   g_q[part, h // 2, 64 * c:64 * (c + 1)], start=True, stop=True)
                mm.then_inc(g_o, 1)

            def gla_stats(h):
                pe.wait_ge(g_sq, 2 * h + 2)
                pe.matmul(ps[:, 4 + h], mean_p, t2[:, h % 2], start=True, stop=True).then_inc(g_st_mm, 1)

            columns(Lin(U_KB + 1), xh, xl)
            gla_stats(0)
            gla_stats(1)
            rows(Lin(U_VB), xh, xl)
            gla_stats(2)
            gla_stats(3)
            rows(Lin(U_VB + 1), xh, xl)

            pe.wait_ge(q_sq, 2)
            pe.wait_ge(g_ln, 2 * TT)
            for n in range(8):
                if n == 4:
                    emptied(pe, Lin(U_VB))
                    emptied(pe, Lin(U_VB + 1))
                pe.matmul(ps[:, (n + 4) % 8], half_mean, q_n4[:, n // 4, n % 4], start=True, stop=True
                          ).then_inc(q_mm, 1)
            ITEMS = 8 * TT
            for l in range(ITEMS + LAG + 1):
                if l < ITEMS:
                    h, i = l // TT, l % TT
                    part = slice(64 * (h % 2), 64 * (h % 2) + 64)
                    if l % (2 * TT) == 0:
                        pe.wait_ge(q_n, 5 + h // 2)
                    if l >= 2:
                        pe.wait_ge(s_scored, l - 1)
                    pe.matmul(ps[:, 4 + l % 2, 0:P * (i + 1)], s_q[part, h // 2, i * P:(i + 1) * P],
                              s_k[part, h // 2, 0:P * (i + 1)], start=True, stop=True).then_inc(s_qk, 1)
                if LAG <= l < ITEMS + LAG:
                    n = l - LAG
                    pe.wait_ge(s_mix, n + 1)
                    if n >= 2:
                        pe.wait_ge(s_ptr, n - 1)
                    for k in range(n % TT + 1):
                        tr = flip(ps[:, 6 + n % 2, k * P:(k + 1) * P], s_e[:, n % (LAG + 1), k * P:(k + 1) * P])
                    tr.then_inc(s_tr, 1)
                if l > LAG:
                    n = l - LAG - 1
                    h, i = n // TT, n % TT
                    pe.wait_ge(s_ptr, n + 1)
                    if h >= 4 and h % 2 == 0 and i == 0:
                        pe.wait_ge(s_ll, h // 2 - 1)
                    for k in range(i + 1):
                        mm = pe.matmul(ps[64 * (h % 2):64 * (h % 2) + 64, (h // 2) % 2, i * P:(i + 1) * P],
                                       s_v[:, k, 64 * h:64 * h + 64], s_pt[:, n % 2, k * P:(k + 1) * P],
                                       start=k == 0, stop=k == i)
                    mm.then_inc(s_pv, 1)
            pe.wait_ge(s_ll, TT)

            over(pe, U_GA, 4, lambda u, k: columns(u, xh, xl))
            over(pe, U_GB, 4, lambda u, k: columns(u, xh, xl))
            pe.wait_ge(g_ll, TT)

            def branch(u, k):
                s = begin(u)
                for j, (hi, lo) in enumerate(((gh, gl), (sh, sl))):
                    for kc in range(4):
                        mm = triple(ps[:, 2 * s + j], wh[:, s, 4 * j + kc, 0:P], wl[:, s, 4 * j + kc, 0:P],
                                    hi[:, kc], lo[:, kc], kc == 0, kc == 3)
                    mm.then_inc(chunk_done, 1)

            over(pe, U_BR, KC, branch)
            first = split_ready(MIXED)
            over(pe, U_OUT, 4, lambda u, k: columns(u, xh, xl, ready=first if k.base == 0 else None))
            square_stats()

            columns(Lin(U_RT), xh, xl, ready=split_ready(8), count=1)
            pe.wait_ge(rt_cp, 1)
            for t in range(TT):
                tr = pe.transpose(ps[:, 2 * (U_RT % 2) + 1, t * 36:(t + 1) * 36], rt_t[:, t * P:(t + 1) * P],
                                  ident[0:36, 0:36])
            tr.then_inc(chunk_done, 1)
            for part in range(EXPERTS // PART_EXPERTS):
                u0, e0 = U_EX + part * (PART_EXPERTS + 4), part * PART_EXPERTS
                if part == 0:
                    columns(Lin(u0), xh, xl)
                    columns(Lin(u0 + 1), xh, xl)
                    pe.wait_ge(r_step, 30)
                    for t in range(TT):
                        tr = pe.transpose(ps[0:EXPERTS, 4, t * P:(t + 1) * P],
                                          m_cw[:, t].rearrange("p g e -> p (g e)"), ident)
                    tr.then_inc(cw_tr, 1)
                    over(pe, u0 + 2, PART_EXPERTS - 2, lambda u, k: columns(u, xh, xl), peel=0)
                else:
                    over(pe, u0, PART_EXPERTS, lambda u, k: columns(u, xh, xl))
                over(pe, u0 + PART_EXPERTS, 4, lambda u, k: columns(
                    u, ah, al, ready=(lambda kc: pe.wait_ge(m_hl, e0 + kc + 1)) if k.base == 0 else None))
            emptied(pe, Lin(UNITS - 2))
            emptied(pe, Lin(UNITS - 1))
            for c in range(KC):
                if c >= 4:
                    pe.wait_ge(o_cp, c - 3)
                for t in range(TT):
                    tr = flip(ps[:, 4 + c % 4, t * P:(t + 1) * P], X[:, c, t * P:(t + 1) * P])
                tr.then_inc(o_tr, 1)


_INS = ["x", "mem", "diff_w_qkv", "diff_lambda", "diff_subln", "diff_w_o", "dil_w_qkv", "dil_w_o", "xatt_w_q",
        "xatt_w_kv", "xatt_w_o", "ffn_w_in", "ffn_conv_w", "ffn_conv_b", "ffn_w_out", "ln_g", "ln_b", "g_mix_2",
        "w_in_2", "w_alpha2_2", "b_alpha_2", "g_gla_2", "w_br_gla_2", "g_q_2", "g_k_2", "rel_bias_2", "w_br_att_2",
        "w_out_2", "g_ffn_2", "w_rg_2", "b_rg_2", "w_re_2", "b_re_2", "w_gate_2", "w_up_2", "w_down_2"]


def kernel(**inputs):
    import concourse.bacc as bacc
    from concourse.bass_utils import run_bass_kernel_spmd

    nc = bacc.Bacc("TRN2", target_bir_lowering=False, num_devices=1)
    host = {name: np.ascontiguousarray(inputs[name]) for name in _INS}
    host.update(tables())
    arrays, aps = {}, {}
    for name, value in host.items():
        arrays[f"in_{name}"] = value
        aps[name] = nc.dram_tensor(f"in_{name}", value.shape, mybir.dt.from_np(value.dtype), kind="ExternalInput").ap()
    out = nc.dram_tensor("out", (1, T, D), F32, kind="ExternalOutput").ap()
    program(nc, aps, out)
    result = run_bass_kernel_spmd(nc, [arrays], core_ids=[0])
    return result.results[0]["out"]
```
